# Optimizing a Trainium2 kernel written in Bass

```python
import math
import jax, jax.numpy as jnp
from jax import lax
import numpy as np

D_MODEL = 1024
BATCH = 1
SEQ = 1024
DEPTH = 1

MEM_LEN = 256
EPS = 1e-6
ATTN_BLOCK = 128
MLA_HEADS = 8
MLA_NOPE = 64
MLA_ROPE = 32
MLA_V = 64
MLA_Q_RANK = 384
MLA_KV_RANK = 256
ROPE_THETA = 10000.0
DIL_HEADS = 8
DIL_HEAD_DIM = 64
DIL_CONFIGS = ((128, 1), (512, 4), (2048, 16))
MLA_WIDTH = MLA_HEADS * MLA_V
DIL_WIDTH = DIL_HEADS * DIL_HEAD_DIM
MIX_WIDTH = MLA_WIDTH + DIL_WIDTH
IN_COLS = MLA_Q_RANK + MLA_KV_RANK + MLA_ROPE + 3 * DIL_WIDTH
MEM_HEADS = 4
MEM_HEAD_DIM = D_MODEL // MEM_HEADS
PEER_HEADS = 8
PEER_KEYS = 128
PEER_N = PEER_KEYS * PEER_KEYS
PEER_QDIM = 256
PEER_TOPK = 16
PEER_CHUNK = 128

kernel_name = 'hybrid_mla_dilated_peer_block'

def rms_norm(x, g):
    xf = x.astype(jnp.float32)
    y = xf * lax.rsqrt(jnp.mean(xf * xf, axis=-1, keepdims=True) + EPS)
    return (y * g.astype(jnp.float32)).astype(x.dtype)

def alibi_slopes(n):
    return jnp.exp2(-8.0 * jnp.arange(1, n + 1, dtype=jnp.float32) / n)

def rope_tables(seq, dim):
    inv = 1.0 / (ROPE_THETA ** (jnp.arange(0, dim, 2, dtype=jnp.float32) / dim))
    ang = jnp.arange(seq, dtype=jnp.float32)[:, None] * inv[None, :]
    return jnp.cos(ang), jnp.sin(ang)

def apply_rope(x, cos, sin):
    x1, x2 = jnp.split(x.astype(jnp.float32), 2, axis=-1)
    return jnp.concatenate([x1 * cos - x2 * sin, x2 * cos + x1 * sin], axis=-1).astype(x.dtype)

def mla_attention(c_q, c_kv, k_rope, q_norm, kv_norm, w_uq, w_ukv):
    B, S, _ = c_q.shape
    H, dqk = MLA_HEADS, MLA_NOPE + MLA_ROPE
    q = (rms_norm(c_q, q_norm) @ w_uq).reshape(B, S, H, dqk)
    kv = (rms_norm(c_kv, kv_norm) @ w_ukv).reshape(B, S, H, MLA_NOPE + MLA_V)
    k_nope, v = kv[..., :MLA_NOPE], kv[..., MLA_NOPE:]
    cos, sin = rope_tables(S, MLA_ROPE)
    q_rope = apply_rope(q[..., MLA_NOPE:], cos[:, None], sin[:, None])
    k_rope = apply_rope(k_rope, cos, sin)
    q = jnp.concatenate([q[..., :MLA_NOPE], q_rope], axis=-1)
    k = jnp.concatenate([k_nope, jnp.broadcast_to(k_rope[:, :, None, :], (B, S, H, MLA_ROPE))], axis=-1)
    scale = dqk ** -0.5
    nb = S // ATTN_BLOCK
    q_blocks = q.reshape(B, nb, ATTN_BLOCK, H, dqk).transpose(1, 0, 2, 3, 4)
    key_pos = jnp.arange(S)

    def attend(args):
        qb, n = args
        s = jnp.einsum('bqhd,bkhd->bhqk', qb, k).astype(jnp.float32) * scale
        q_pos = n * ATTN_BLOCK + jnp.arange(ATTN_BLOCK)
        s = jnp.where(key_pos[None, :] <= q_pos[:, None], s, -jnp.inf)
        p = jax.nn.softmax(s, axis=-1).astype(v.dtype)
        return jnp.einsum('bhqk,bkhd->bqhd', p, v)

    o = lax.map(attend, (q_blocks, jnp.arange(nb)))
    return o.transpose(1, 0, 2, 3, 4).reshape(B, S, H * MLA_V)

def dilated_branch(q, k, v, window, dilation, slopes):
    B, S, H, Dh = q.shape
    W = window // dilation
    L = S // dilation
    nb = -(-L // W)
    Lp = nb * W

    def to_sub(t):
        t = t.reshape(B, L, dilation, H, Dh).transpose(0, 2, 3, 1, 4)
        return jnp.pad(t, ((0, 0), (0, 0), (0, 0), (0, Lp - L), (0, 0)))

    def band(t):
        tp = jnp.pad(t, ((0, 0), (0, 0), (0, 0), (W, 0), (0, 0)))
        prev = tp[..., :Lp, :].reshape(B, dilation, H, nb, W, Dh)
        cur = t.reshape(B, dilation, H, nb, W, Dh)
        return jnp.concatenate([prev, cur], axis=4)

    qs, ks, vs = to_sub(q), to_sub(k), to_sub(v)
    qb = qs.reshape(B, dilation, H, nb, W, Dh)
    kb, vb = band(ks), band(vs)
    s = jnp.einsum('brhnqd,brhnkd->brhnqk', qb, kb).astype(jnp.float32) * (Dh ** -0.5)
    qi = jnp.arange(W)[:, None]
    kj = jnp.arange(2 * W)[None, :]
    steps = W + qi - kj
    blk = jnp.arange(nb)[:, None, None]
    valid = (steps >= 0) & (steps <= W) & ((blk > 0) | (kj >= W))
    bias = -slopes[:, None, None, None] * (steps * dilation).astype(jnp.float32)
    s = jnp.where(valid, s + bias, -jnp.inf)
    lse = jax.nn.logsumexp(s, axis=-1)
    p = jnp.exp(s - lse[..., None]).astype(v.dtype)
    o = jnp.einsum('brhnqk,brhnkd->brhnqd', p, vb)
    o = o.reshape(B, dilation, H, Lp, Dh)[:, :, :, :L].transpose(0, 3, 1, 2, 4).reshape(B, S, H, Dh)
    lse = lse.reshape(B, dilation, H, Lp)[:, :, :, :L].transpose(0, 3, 1, 2).reshape(B, S, H)
    return o, lse

def dilated_attention(q, k, v):
    B, S, H, Dh = q.shape
    slopes = alibi_slopes(H)
    results = [dilated_branch(q, k, v, w, d, slopes) for (w, d) in DIL_CONFIGS]
    outs = jnp.stack([r[0] for r in results], axis=0)
    lses = jnp.stack([r[1] for r in results], axis=0)
    wts = jax.nn.softmax(lses, axis=0).astype(outs.dtype)
    o = jnp.einsum('gbsh,gbshd->bshd', wts, outs)
    return o.reshape(B, S, H * Dh)

def memory_attention(hn, memn, w_q, w_kv, w_o):
    B, S, _ = hn.shape
    M = memn.shape[1]
    q = (hn @ w_q).reshape(B, S, MEM_HEADS, MEM_HEAD_DIM)
    kv = (memn @ w_kv).reshape(B, M, 2, MEM_HEADS, MEM_HEAD_DIM)
    k, v = kv[:, :, 0], kv[:, :, 1]
    s = jnp.einsum('bshd,bmhd->bhsm', q, k).astype(jnp.float32) * (MEM_HEAD_DIM ** -0.5)
    p = jax.nn.softmax(s, axis=-1).astype(v.dtype)
    o = jnp.einsum('bhsm,bmhd->bshd', p, v).reshape(B, S, MEM_HEADS * MEM_HEAD_DIM)
    return o @ w_o

def peer_ffn(xn, w_q, sub_keys, u_tab, v_tab):
    B, S, D = xn.shape
    C, Hh, K = PEER_CHUNK, PEER_HEADS, PEER_TOPK
    half = PEER_QDIM // 2
    xt = xn.reshape((B * S) // C, C, D)

    def chunk(xc):
        q = (xc @ w_q).reshape(C, Hh, 2, half).astype(jnp.float32)
        s = jnp.einsum('chpd,hpnd->chpn', q, sub_keys.astype(jnp.float32))
        top_s, top_i = lax.top_k(s, K)
        cand = top_s[:, :, 0, :, None] + top_s[:, :, 1, None, :]
        best_s, best_j = lax.top_k(cand.reshape(C, Hh, K * K), K)
        ia = jnp.take_along_axis(top_i[:, :, 0], best_j // K, axis=-1)
        ib = jnp.take_along_axis(top_i[:, :, 1], best_j % K, axis=-1)
        expert = ia * PEER_KEYS + ib
        g = jax.nn.softmax(best_s, axis=-1)
        u = u_tab[expert]
        a = jax.nn.gelu(jnp.einsum('cd,chkd->chk', xc, u).astype(jnp.float32), approximate=False)
        coeff = (g * a).astype(xc.dtype)
        return jnp.einsum('chk,chkd->cd', coeff, v_tab[expert])

    return lax.map(chunk, xt).reshape(B, S, D)

def setup_inputs(seed: int = 0) -> dict:
    key = jax.random.key(seed)
    ks = jax.random.split(key, 22)
    f32 = jnp.float32

    def nrm(k, shape, scale):
        return jax.random.normal(k, shape, f32) * scale

    def gain(k, shape):
        return 1.0 + 0.02 * jax.random.normal(k, shape, f32)

    L = DEPTH
    return {
        'x': nrm(ks[0], (BATCH, SEQ, D_MODEL), 1.0),
        'mem': nrm(ks[1], (BATCH, MEM_LEN, D_MODEL), 1.0),
        'norm_mix': gain(ks[2], (L, D_MODEL)),
        'w_in': nrm(ks[3], (L, D_MODEL, IN_COLS), D_MODEL ** -0.5),
        'mla_q_norm': gain(ks[4], (L, MLA_Q_RANK)),
        'mla_kv_norm': gain(ks[5], (L, MLA_KV_RANK)),
        'mla_w_uq': nrm(ks[6], (L, MLA_Q_RANK, MLA_HEADS * (MLA_NOPE + MLA_ROPE)), MLA_Q_RANK ** -0.5),
        'mla_w_ukv': nrm(ks[7], (L, MLA_KV_RANK, MLA_HEADS * (MLA_NOPE + MLA_V)), MLA_KV_RANK ** -0.5),
        'grp_norm_mla': gain(ks[8], (L, MLA_WIDTH)),
        'grp_norm_dil': gain(ks[9], (L, DIL_WIDTH)),
        'w_out': nrm(ks[10], (L, MIX_WIDTH, D_MODEL), MIX_WIDTH ** -0.5),
        'norm_mem_q': gain(ks[11], (L, D_MODEL)),
        'norm_mem_kv': gain(ks[12], (L, D_MODEL)),
        'w_mem_q': nrm(ks[13], (L, D_MODEL, MEM_HEADS * MEM_HEAD_DIM), D_MODEL ** -0.5),
        'w_mem_kv': nrm(ks[14], (L, D_MODEL, 2 * MEM_HEADS * MEM_HEAD_DIM), D_MODEL ** -0.5),
        'w_mem_o': nrm(ks[15], (L, MEM_HEADS * MEM_HEAD_DIM, D_MODEL), D_MODEL ** -0.5),
        'norm_ffn': gain(ks[16], (L, D_MODEL)),
        'peer_w_q': nrm(ks[17], (L, D_MODEL, PEER_HEADS * PEER_QDIM), D_MODEL ** -0.5),
        'peer_sub_keys': nrm(ks[18], (L, PEER_HEADS, 2, PEER_KEYS, PEER_QDIM // 2), (PEER_QDIM // 2) ** -0.5),
        'peer_u': nrm(ks[19], (L, PEER_N, D_MODEL), D_MODEL ** -0.5),
        'peer_v': nrm(ks[20], (L, PEER_N, D_MODEL), PEER_HEADS ** -0.5),
        'norm_final': gain(ks[21], (D_MODEL,)),
    }

def reference(x, mem, norm_mix, w_in, mla_q_norm, mla_kv_norm, mla_w_uq, mla_w_ukv,
              grp_norm_mla, grp_norm_dil, w_out, norm_mem_q, norm_mem_kv, w_mem_q, w_mem_kv,
              w_mem_o, norm_ffn, peer_w_q, peer_sub_keys, peer_u, peer_v, norm_final):
    B, S, _ = x.shape
    o1 = MLA_Q_RANK
    o2 = o1 + MLA_KV_RANK
    o3 = o2 + MLA_ROPE
    o4 = o3 + DIL_WIDTH
    o5 = o4 + DIL_WIDTH
    h = x
    for l in range(DEPTH):
        proj = rms_norm(h, norm_mix[l]) @ w_in[l]
        c_q, c_kv, k_rope, dq, dk, dv = jnp.split(proj, [o1, o2, o3, o4, o5], axis=-1)
        o_mla = mla_attention(c_q, c_kv, k_rope, mla_q_norm[l], mla_kv_norm[l], mla_w_uq[l], mla_w_ukv[l])
        dshape = (B, S, DIL_HEADS, DIL_HEAD_DIM)
        o_dil = dilated_attention(dq.reshape(dshape), dk.reshape(dshape), dv.reshape(dshape))
        mixed = jnp.concatenate([rms_norm(o_mla, grp_norm_mla[l]), rms_norm(o_dil, grp_norm_dil[l])], axis=-1)
        h = h + mixed @ w_out[l]
        h = h + memory_attention(rms_norm(h, norm_mem_q[l]), rms_norm(mem, norm_mem_kv[l]),
                                 w_mem_q[l], w_mem_kv[l], w_mem_o[l])
        h = h + peer_ffn(rms_norm(h, norm_ffn[l]), peer_w_q[l], peer_sub_keys[l], peer_u[l], peer_v[l])
    return rms_norm(h, norm_final)


_drawn_inputs = setup_inputs


def setup_inputs(seed=0):
    import zlib

    import numpy as np

    out = dict(_drawn_inputs(seed))
    spreads = {}
    factors = {'mla_q_norm': 3.484,
     'grp_norm_mla': 3.49,
     'grp_norm_dil': 3.242,
     'norm_mem_q': 8.0,
     'norm_mem_kv': 8.0,
     'norm_ffn': 23.768,
     'norm_final': 7.553}
    for name, (base, spread) in spreads.items():
        noise = np.random.default_rng([zlib.crc32(name.encode()), seed]).standard_normal(out[name].shape)
        drawn = base * np.exp(spread * noise) if base else spread * noise
        out[name] = __import__('jax').numpy.asarray(drawn.astype(out[name].dtype))
    for name, factor in factors.items():
        out[name] = (out[name] * factor).astype(out[name].dtype)
    return out
```

```python
from contextlib import ExitStack

import numpy as np

import concourse.bass as bass
from concourse import mybir

F32 = mybir.dt.float32
U32 = mybir.dt.uint32
ALU = mybir.AluOpType
ACT = mybir.ActivationFunctionType
AX_X = mybir.AxisListType.X

P = 128
BANK = 512
D = 1024
DT = D // P
SEQ = 1024
CHUNKS = SEQ // P
EPS = 1e-6
MEM_LEN = 256
MEM_HEADS = 4
MEM_SCALE = (D // MEM_HEADS) ** -0.5
HEADS = 8
NOPE = 64
ROPE = 32
HALF_ROPE = ROPE // 2
QK = NOPE + ROPE
HEAD = 64
Q_RANK = 384
KV_RANK = 256
WIDTH = HEADS * HEAD
IN_COLS = Q_RANK + KV_RANK + ROPE + 3 * WIDTH
PEER_HEADS = 8
PEER_KEYS = 128
PEER_N = PEER_KEYS * PEER_KEYS
PEER_TABLES = 2 * PEER_HEADS
TOPK = 16
PICKS = PEER_HEADS * TOPK
RING = 8
DIL_CONFIGS = ((128, 1), (512, 4), (2048, 16))
BIAS_COLS = SEQ + 2 * P
NOWHERE = -1e30


def allocators(nc, ctx):
    def sb(name, shape, dt=F32):
        return ctx.enter_context(nc.sbuf_tensor(name, shape, dt))

    def ps(name, shape):
        return ctx.enter_context(nc.psum_tensor(name, shape, F32))

    def sem(name):
        return ctx.enter_context(nc.semaphore(name))

    return sb, ps, sem


def shape_constants():
    inv = 1.0 / (np.float32(10000.0) ** (np.arange(0, ROPE, 2, dtype=np.float32) / np.float32(ROPE)))
    angle = np.arange(SEQ, dtype=np.float32)[:, None] * inv.astype(np.float32)[None, :]
    cos, sin = np.cos(angle), np.sin(angle)

    def by_chunk(a):
        return np.ascontiguousarray(a.reshape(CHUNKS, P, ROPE).transpose(1, 0, 2), dtype=np.float32)

    distance = (np.arange(P)[:, None] + (SEQ - P) - np.arange(BIAS_COLS)[None, :]).astype(np.float64)
    count = np.zeros_like(distance)
    for window, dilation in DIL_CONFIGS:
        count += (distance >= 0) & (distance <= window) & (distance % dilation == 0)
    bias = np.full((1 + HEADS, P, BIAS_COLS), NOWHERE, dtype=np.float32)
    bias[0][distance >= 0] = 0.0
    seen = count > 0
    for h in range(HEADS):
        slope = 2.0 ** (-8.0 * (h + 1) / HEADS)
        bias[1 + h][seen] = (np.log(count[seen]) - slope * distance[seen]) * HEAD ** 0.5
    return {
        "identity": np.eye(P, dtype=np.float32),
        "cos2": by_chunk(np.concatenate([cos, cos], axis=1)),
        "sin2": by_chunk(np.concatenate([-sin, sin], axis=1)),
        "score_bias": bias,
        "slots": np.tile(np.arange(TOPK, dtype=np.float32), (P, 1)),
    }


def fold_weights(nc, io):
    with ExitStack() as ctx:
        sb, ps, sem = allocators(nc, ctx)
        ident = sb("f_ident", [P, P])
        mem_rows = sb("f_mem_rows", [P, 2, D])
        mem_scaled = sb("f_mem_scaled", [P, 2, D])
        mem_sumsq = sb("f_mem_sumsq", [P, 2])
        mem_rms = sb("f_mem_rms", [P, 2])
        mem_rstd = sb("f_mem_rstd", [P, 2])
        eps = sb("f_eps", [P, 1])
        gain_kv = sb("f_gain_kv", [P, DT])
        gain_q = sb("f_gain_q", [P, DT])
        gain_ffn = sb("f_gain_ffn", [P, DT])
        mem_t = sb("f_mem_t", [P, DT, MEM_LEN])
        w_big = sb("f_w_big", [P, DT, 2 * D])
        w_o = sb("f_w_o", [P, DT, D])
        w_q = sb("f_w_q", [P, DT, D])
        k_t = sb("f_k_t", [P, DT, MEM_LEN])
        v_t = sb("f_v_t", [P, DT, MEM_LEN])
        turned = sb("f_turned", [P, 4, D])
        keys = mem_rows[:, :, :].rearrange("p t (i n) -> p (t i) n", n=PEER_KEYS)
        keys_t = mem_scaled[:, :, :].rearrange("p t (i n) -> p (t i) n", n=PEER_KEYS)
        stage_v = sb("f_stage_v", [P, 2, D])
        stage_s = sb("f_stage_s", [P, 2, D])
        pair = [ps(f"f_pair{i}", [P, D]) for i in range(4)]

        mem_loaded = sem("f_mem_loaded")
        small_loaded = sem("f_small_loaded")
        kv_loaded = sem("f_kv_loaded")
        o_loaded = sem("f_o_loaded")
        q_loaded = sem("f_q_loaded")
        keys_loaded = sem("f_keys_loaded")
        peer_loaded = sem("f_peer_loaded")
        eps_set = sem("f_eps_set")
        mem_squared = sem("f_mem_squared")
        mem_rooted = sem("f_mem_rooted")
        mem_inverted = sem("f_mem_inverted")
        mem_normed = sem("f_mem_normed")
        pair_filled = sem("f_pair_filled")
        act_emptied = sem("f_act_emptied")
        dve_emptied = sem("f_dve_emptied")
        stored_v = [sem(f"f_stored_v{i}") for i in range(2)]
        stored_s = [sem(f"f_stored_s{i}") for i in range(2)]

        tasks = [("mem_t", 0), ("mem_t", 1), ("k_t", 0), ("k_t", 1), ("v_t", 0), ("v_t", 1)]
        tasks += [("mem_values", kt) for kt in range(DT)]
        tasks += [("turn_q", 0), ("turn_q", 1)]
        for h in range(MEM_HEADS):
            if h + 1 < MEM_HEADS:
                tasks += [("turn_q", 2 * h + 2), ("turn_q", 2 * h + 3)]
            tasks += [("mem_scores", 2 * h), ("mem_scores", 2 * h + 1)]
        tasks += [("turn_keys", 0), ("turn_keys", 1), ("turn_peer", 0)]
        for i in range(PEER_TABLES):
            if i + 1 < PEER_TABLES:
                tasks += [("turn_peer", i + 1)]
            tasks += [("peer_scores", i)]
        by_dve = {"mem_t", "mem_scores", "peer_scores", "turn_keys"}
        emptied_at = {}
        counts = {True: 0, False: 0}
        for task in tasks:
            counts[task[0] in by_dve] += 1
            emptied_at[task] = (dve_emptied if task[0] in by_dve else act_emptied, counts[task[0] in by_dve])
        number = {task: n for n, task in enumerate(tasks)}

        def wait_emptied(eng, kind, i):
            eng.wait_ge(*emptied_at[(kind, i)])

        block = ctx.enter_context(nc.Block())

        @block.sync
        def _(sp):
            sp.dma_start(mem_rows[:, :, :], io["mem"].rearrange("b (t p) d -> p (b t) d", p=P)).then_inc(mem_loaded, 16)
            sp.dma_start(ident[:, :], io["identity"]).then_inc(small_loaded, 16)
            sp.dma_start(gain_kv[:, :], io["norm_mem_kv"]).then_inc(small_loaded, 16)
            sp.dma_start(w_big[:, :, 0:D], io["w_mem_kv"].rearrange("(t p) n -> p t n", p=P)[:, :, 0:D]).then_inc(kv_loaded, 16)
            sp.dma_start(w_big[:, :, D:2 * D], io["w_mem_kv"].rearrange("(t p) n -> p t n", p=P)[:, :, D:2 * D]).then_inc(kv_loaded, 16)
            sp.dma_start(w_o[:, :, :], io["w_mem_o"].rearrange("(t p) n -> p t n", p=P)).then_inc(o_loaded, 16)
            sp.dma_start(w_q[:, :, :], io["w_mem_q"].rearrange("(t p) n -> p t n", p=P)).then_inc(q_loaded, 16)
            sp.dma_start(gain_q[:, :], io["norm_mem_q"]).then_inc(small_loaded, 16)
            sp.dma_start(gain_ffn[:, :], io["norm_ffn"]).then_inc(small_loaded, 16)
            sp.wait_ge(pair_filled, number[("mem_t", 1)] + 1)
            sp.dma_start(keys, io["peer_sub_keys"].rearrange("i n d -> n i d")).then_inc(keys_loaded, 16)
            sp.wait_ge(pair_filled, number[("v_t", 1)] + 1)
            sp.dma_start(w_big[:, :, :], io["peer_w_q"].rearrange("(t p) n -> p t n", p=P)).then_inc(peer_loaded, 16)
            for kt in range(DT):
                wait_emptied(sp, "mem_values", kt)
                sp.dma_start(io["mem_values"][:, kt, :], stage_v[:, kt % 2, :]).then_inc(stored_v[kt % 2], 16)
            for n in range(DT):
                wait_emptied(sp, "mem_scores", n)
                h, half = divmod(n, 2)
                sp.dma_start(io["mem_scores"][:, 4 * half:4 * half + 4, MEM_LEN * h:MEM_LEN * (h + 1)],
                             stage_s[:, n % 2, :].rearrange("p (t m) -> p t m", t=4)).then_inc(stored_s[n % 2], 16)
            for i in range(PEER_TABLES):
                wait_emptied(sp, "peer_scores", i)
                sp.dma_start(io["peer_scores"][:, :, P * i:P * (i + 1)],
                             stage_s[:, i % 2, :].rearrange("p (t m) -> p t m", t=DT)).then_inc(stored_s[i % 2], 16)
            for i in range(2):
                sp.wait_ge(stored_v[i], 16 * DT // 2)
                sp.wait_ge(stored_s[i], 16 * (DT + PEER_TABLES) // 2)

        @block.scalar
        def _(act):
            act.wait_ge(mem_loaded, 16)
            for t in range(2):
                act.activation(mem_scaled[:, t, :], mem_rows[:, t, :], ACT.Square,
                               accum_out=mem_sumsq[:, t:t + 1]).then_inc(mem_squared, 1)
            act.wait_ge(mem_squared, 2)
            act.wait_ge(eps_set, 1)
            act.activation(mem_rms[:, :], mem_sumsq[:, :], ACT.Sqrt, scale=1.0 / D, bias=eps[:, :]).then_inc(mem_rooted, 1)
            for n, (kind, i) in enumerate(tasks):
                if kind in by_dve:
                    continue
                act.wait_ge(pair_filled, n + 1)
                full = pair[n % 4]
                if kind == "k_t":
                    act.activation(k_t[:, 4 * i:4 * i + 4, :].rearrange("p t m -> p (t m)"), full[:, :], ACT.Copy,
                                   scale=MEM_SCALE).then_inc(act_emptied, 1)
                elif kind == "v_t":
                    act.activation(v_t[:, 4 * i:4 * i + 4, :].rearrange("p t m -> p (t m)"), full[:, :],
                                   ACT.Copy).then_inc(act_emptied, 1)
                elif kind == "mem_values":
                    if i >= 2:
                        act.wait_ge(stored_v[i % 2], 16 * (i // 2))
                    act.activation(stage_v[:, i % 2, :], full[:, :], ACT.Copy).then_inc(act_emptied, 1)
                elif kind == "turn_q":
                    if i >= 4:
                        act.wait_ge(pair_filled, number[("mem_scores", 2 * (i // 2 - 2) + 1)] + 1)
                    act.activation(turned[:, i % 4, :], full[:, :], ACT.Copy).then_inc(act_emptied, 1)
                elif kind == "turn_peer":
                    before = ("mem_scores", 2 * MEM_HEADS - 1) if i < 4 else ("peer_scores", i - 4)
                    act.wait_ge(pair_filled, number[before] + 1)
                    act.activation(turned[:, i % 4, :], full[:, :], ACT.Copy).then_inc(act_emptied, 1)

        @block.vector
        def _(dve):
            dve.memset(eps[:, :], EPS).then_inc(eps_set, 1)
            dve.wait_ge(mem_rooted, 1)
            dve.reciprocal(mem_rstd[:, :], mem_rms[:, :]).then_inc(mem_inverted, 1)
            dve.wait_ge(mem_inverted, 1)
            for t in range(2):
                dve.tensor_scalar(mem_scaled[:, t, :], mem_rows[:, t, :], mem_rstd[:, t:t + 1], None,
                                  ALU.mult).then_inc(mem_normed, 1)
            dve.wait_ge(small_loaded, 64)
            stored = 0
            for n, (kind, i) in enumerate(tasks):
                if kind not in by_dve:
                    continue
                dve.wait_ge(pair_filled, n + 1)
                full = pair[n % 4]
                if kind == "mem_t":
                    dve.tensor_tensor(mem_t[:, :, P * i:P * (i + 1)], full[:, :].rearrange("p (t m) -> p t m", t=DT),
                                      gain_kv[:, :].unsqueeze(2).to_broadcast([P, DT, P]), ALU.mult).then_inc(dve_emptied, 1)
                elif kind == "mem_scores":
                    if i >= 2:
                        dve.wait_ge(stored_s[i % 2], 16 * (i // 2))
                    half = i % 2
                    dve.tensor_tensor(stage_s[:, i % 2, :].rearrange("p (t m) -> p t m", t=4),
                                      full[:, :].rearrange("p (t m) -> p t m", t=4),
                                      gain_q[:, 4 * half:4 * half + 4].unsqueeze(2).to_broadcast([P, 4, MEM_LEN]),
                                      ALU.mult).then_inc(dve_emptied, 1)
                elif kind == "turn_keys":
                    dve.tensor_copy(keys_t[:, 8 * i:8 * i + 8, :].rearrange("p i n -> p (i n)"),
                                    full[:, :]).then_inc(dve_emptied, 1)
                elif kind == "peer_scores":
                    dve.wait_ge(stored_s[i % 2], 16 * ((DT + i) // 2))
                    dve.tensor_tensor(stage_s[:, i % 2, :].rearrange("p (t m) -> p t m", t=DT),
                                      full[:, :].rearrange("p (t m) -> p t m", t=DT),
                                      gain_ffn[:, :].unsqueeze(2).to_broadcast([P, DT, P]),
                                      ALU.mult).then_inc(dve_emptied, 1)

        @block.tensor
        def _(pe):
            pe.wait_ge(small_loaded, 64)
            for n, (kind, i) in enumerate(tasks):
                to = pair[n % 4]
                if n >= 4:
                    pe.wait_ge(*emptied_at[tasks[n - 4]])
                if kind == "mem_t":
                    pe.wait_ge(mem_normed, 2)
                    for t in range(DT):
                        last = pe.transpose(to[:, P * t:P * (t + 1)], mem_scaled[:, i, P * t:P * (t + 1)], ident[:, :])
                elif kind in ("k_t", "v_t"):
                    pe.wait_ge(kv_loaded, 32)
                    wait_emptied(pe, "mem_t", 0)
                    wait_emptied(pe, "mem_t", 1)
                    at = (D if kind == "v_t" else 0) + 4 * P * i
                    for j in range(4):
                        for t in range(DT):
                            last = pe.matmul(to[:, MEM_LEN * j:MEM_LEN * (j + 1)], w_big[:, t, at + P * j:at + P * (j + 1)],
                                             mem_t[:, t, :], start=(t == 0), stop=(t == DT - 1))
                elif kind == "mem_values":
                    pe.wait_ge(o_loaded, 16)
                    h, m = divmod(i, 2)
                    wait_emptied(pe, "v_t", 0)
                    wait_emptied(pe, "v_t", 1)
                    for c in range(2):
                        for j in range(2):
                            last = pe.matmul(to[:, BANK * c:BANK * (c + 1)], v_t[:, 2 * h + j, P * m:P * (m + 1)],
                                             w_o[:, 2 * h + j, BANK * c:BANK * (c + 1)], start=(j == 0), stop=(j == 1))
                elif kind == "turn_q":
                    pe.wait_ge(q_loaded, 16)
                    for t in range(DT):
                        last = pe.transpose(to[:, P * t:P * (t + 1)], w_q[:, t, P * i:P * (i + 1)], ident[:, :])
                elif kind == "mem_scores":
                    h, half = divmod(i, 2)
                    wait_emptied(pe, "k_t", 1)
                    for j in range(2):
                        wait_emptied(pe, "turn_q", 2 * h + j)
                    for t in range(4):
                        for j in range(2):
                            at = P * (4 * half + t)
                            last = pe.matmul(to[:, MEM_LEN * t:MEM_LEN * (t + 1)], turned[:, (2 * h + j) % 4, at:at + P],
                                             k_t[:, 2 * h + j, :], start=(j == 0), stop=(j == 1))
                elif kind == "turn_keys":
                    pe.wait_ge(keys_loaded, 16)
                    for j in range(8):
                        last = pe.transpose(to[:, P * j:P * (j + 1)], keys[:, 8 * i + j, :], ident[:, :])
                elif kind == "turn_peer":
                    pe.wait_ge(peer_loaded, 16)
                    for t in range(DT):
                        last = pe.transpose(to[:, P * t:P * (t + 1)], w_big[:, t, P * i:P * (i + 1)], ident[:, :])
                elif kind == "peer_scores":
                    wait_emptied(pe, "turn_keys", 1)
                    wait_emptied(pe, "turn_peer", i)
                    for t in range(DT):
                        last = pe.matmul(to[:, P * t:P * (t + 1)], turned[:, i % 4, P * t:P * (t + 1)],
                                         keys_t[:, i, :], start=True, stop=True)
                last.then_inc(pair_filled, 1)


def project_tokens(nc, io, keep):
    with ExitStack() as ctx:
        sb, ps, sem = allocators(nc, ctx)
        Q_TILES, KV_TILES = Q_RANK // P, KV_RANK // P
        C_TILES = Q_TILES + KV_TILES
        C_COLS = Q_RANK + KV_RANK
        QH = HEADS * QK // 2

        ident = sb("p_ident", [P, P])
        w_in = sb("p_w_in", [P, DT, IN_COLS])
        w_uq = sb("p_w_uq", [P, Q_TILES, HEADS * QK])
        w_ukv = sb("p_w_ukv", [P, KV_TILES, HEADS * (NOPE + HEAD)])
        gain_x = sb("p_gain_x", [P, DT])
        gain_c = sb("p_gain_c", [P, C_TILES])
        cos2 = sb("p_cos2", [P, CHUNKS, ROPE])
        sin2 = sb("p_sin2", [P, CHUNKS, ROPE])
        eps = sb("p_eps", [P, 1])
        x_rows = sb("p_x_rows", [P, D])
        x_scaled = sb("p_x_scaled", [P, D])
        x_t = sb("p_x_t", [P, D])
        x_stat = sb("p_x_stat", [P, 3])
        c_scaled = sb("p_c_scaled", [P, C_COLS])
        c_t = sb("p_c_t", [P, C_COLS])
        c_stat = sb("p_c_stat", [P, 6])
        dqk = sb("p_dqk", [P, 2 * WIDTH])
        q_rows = sb("p_q_rows", [P, HEADS, QK])
        k_rows = sb("p_k_rows", [P, HEADS, QK])
        q_rope_a = sb("p_q_rope_a", [P, HEADS, ROPE])
        q_rope_b = sb("p_q_rope_b", [P, HEADS, ROPE])
        k_rope_a = sb("p_k_rope_a", [P, ROPE])
        k_rope_b = sb("p_k_rope_b", [P, ROPE])
        q_out = sb("p_q_out", [QK, HEADS, P])
        dq_out = sb("p_dq_out", [P, HEADS // 2, P])
        turn_x = ps("p_turn_x", [P, D])
        pair_b = ps("p_pair_b", [P, D])
        pair_c = ps("p_pair_c", [P, D])
        pair_d = ps("p_pair_d", [P, D])

        weight_loaded = [sem(f"p_weight_loaded{i}") for i in range(DT + 2)]
        small_loaded = sem("p_small_loaded")
        weight_gained = sem("p_weight_gained")
        eps_set = sem("p_eps_set")
        x_loaded = sem("p_x_loaded")
        x_squared, x_rooted, x_inverted = sem("p_x_squared"), sem("p_x_rooted"), sem("p_x_inverted")
        x_normed, x_turned, x_t_ready = sem("p_x_normed"), sem("p_x_turned"), sem("p_x_t_ready")
        c_projected, d_projected, v_projected = sem("p_c_projected"), sem("p_d_projected"), sem("p_v_projected")
        c_squared, c_rooted, c_inverted = sem("p_c_squared"), sem("p_c_rooted"), sem("p_c_inverted")
        c_normed, c_turned, c_t_ready = sem("p_c_normed"), sem("p_c_turned"), sem("p_c_t_ready")
        dqk_ready, d_turned, dq_t_ready, dk_t_ready = (sem("p_dqk_ready"), sem("p_d_turned"), sem("p_dq_t_ready"),
                                                       sem("p_dk_t_ready"))
        q_projected, kv_projected = sem("p_q_projected"), sem("p_kv_projected")
        q_rows_ready, k_nope_ready = sem("p_q_rows_ready"), sem("p_k_nope_ready")
        q_rope_parts, q_rope_ready = sem("p_q_rope_parts"), sem("p_q_rope_ready")
        k_rope_parts, k_rope_ready = sem("p_k_rope_parts"), sem("p_k_rope_ready")
        q_turned, q_t_ready, k_turned, k_t_ready = (sem("p_q_turned"), sem("p_q_t_ready"), sem("p_k_turned"),
                                                    sem("p_k_t_ready"))
        v_ready, dv_ready = sem("p_v_ready"), sem("p_dv_ready")
        q_stored, dq_stored = sem("p_q_stored"), sem("p_dq_stored")
        block = ctx.enter_context(nc.Block())

        @block.sync
        def _(sp):
            sp.dma_start(x_rows[:, :], io["x"][0:P, :]).then_inc(x_loaded, 16)
            sp.dma_start(ident[:, :], io["identity"]).then_inc(small_loaded, 16)
            sp.dma_start(gain_x[:, :], io["norm_mix"]).then_inc(small_loaded, 16)
            sp.dma_start(gain_c[:, 0:Q_TILES], io["mla_q_norm"]).then_inc(small_loaded, 16)
            sp.dma_start(gain_c[:, Q_TILES:C_TILES], io["mla_kv_norm"]).then_inc(small_loaded, 16)
            sp.dma_start(cos2[:, :, :], io["cos2"]).then_inc(small_loaded, 16)
            sp.dma_start(sin2[:, :, :], io["sin2"]).then_inc(small_loaded, 16)
            for t in range(DT):
                sp.dma_start(w_in[:, t, :], io["w_in"][P * t:P * (t + 1), :]).then_inc(weight_loaded[t], 16)
            sp.dma_start(w_uq[:, :, :], io["mla_w_uq"].rearrange("(t p) n -> p t n", p=P)).then_inc(weight_loaded[DT], 16)
            sp.dma_start(w_ukv[:, :, :], io["mla_w_ukv"].rearrange("(t p) n -> p t n", p=P)).then_inc(weight_loaded[DT + 1], 16)

            def store_queries(t):
                sp.wait_ge(dq_t_ready, t + 1)
                sp.dma_start(io["dil_q_t"][bass.ds(t, 1)].rearrange("a p h q -> (a p) h q"), dq_out[:, :, :]).then_inc(dq_stored, 16)
                sp.wait_ge(q_t_ready, t + 1)
                sp.dma_start(io["mla_q_t"][bass.ds(t, 1)].rearrange("a p h q -> (a p) h q"), q_out[:, :, :]).then_inc(q_stored, 16)

            with sp.Fori(0, CHUNKS - 1) as t:
                sp.wait_ge(x_normed, t + 1)
                sp.dma_start(x_rows[:, :], io["x"][bass.ds((t + 1) * P, P), :]).then_inc(x_loaded, 16)
                store_queries(t)
            store_queries(CHUNKS - 1)
            sp.wait_ge(dq_stored, 16 * CHUNKS)
            sp.wait_ge(q_stored, 16 * CHUNKS)

        @block.scalar
        def _(act):
            def square_x(t):
                act.wait_ge(x_loaded, 16 * (t + 1))
                act.activation(x_scaled[:, :], x_rows[:, :], ACT.Square, accum_out=x_stat[:, 0:1]).then_inc(x_squared, 1)
                act.wait_ge(x_squared, t + 1)
                act.activation(x_stat[:, 1:2], x_stat[:, 0:1], ACT.Sqrt, scale=1.0 / D, bias=eps[:, :]).then_inc(x_rooted, 1)

            def keep_x_t(t):
                act.wait_ge(x_turned, t + 1)
                act.activation(x_t[:, :], turn_x[:, :], ACT.Copy).then_inc(x_t_ready, 1)

            def chunk(t, more):
                act.wait_ge(c_projected, t + 1)
                act.activation(c_scaled[:, 0:Q_RANK], pair_b[:, 0:Q_RANK], ACT.Square,
                               accum_out=c_stat[:, 0:1]).then_inc(c_squared, 1)
                act.activation(c_scaled[:, Q_RANK:C_COLS], pair_b[:, BANK:BANK + KV_RANK], ACT.Square,
                               accum_out=c_stat[:, 1:2]).then_inc(c_squared, 1)
                act.wait_ge(c_squared, 2 * t + 2)
                act.activation(c_stat[:, 2:3], c_stat[:, 0:1], ACT.Sqrt, scale=1.0 / Q_RANK, bias=eps[:, :]).then_inc(c_rooted, 1)
                act.activation(c_stat[:, 3:4], c_stat[:, 1:2], ACT.Sqrt, scale=1.0 / KV_RANK, bias=eps[:, :]).then_inc(c_rooted, 1)
                act.wait_ge(d_projected, t + 1)
                act.activation(dqk[:, :], pair_c[:, :], ACT.Copy).then_inc(dqk_ready, 1)
                if more:
                    square_x(t + 1)
                    keep_x_t(t + 1)
                act.wait_ge(d_turned, t + 1)
                act.activation(dq_out[:, :, :].rearrange("p h q -> p (h q)"), pair_d[:, 0:BANK], ACT.Copy).then_inc(dq_t_ready, 1)
                act.wait_ge(q_projected, t + 1)
                act.activation(q_rows[:, :, :].rearrange("p (b h) c -> p b (h c)", b=2),
                               pair_c[:, :].rearrange("p (b w) -> p b w", b=2)[:, :, 0:QH], ACT.Copy).then_inc(q_rows_ready, 1)
                act.wait_ge(kv_projected, t + 1)
                act.activation(k_rows[:, :, 0:NOPE], pair_b[:, :].rearrange("p (h c) -> p h c", h=HEADS)[:, :, 0:NOPE],
                               ACT.Copy).then_inc(k_nope_ready, 1)
                act.wait_ge(q_turned, t + 1)
                act.activation(q_out[:, :, :].rearrange("p h q -> p (h q)"), pair_d[0:QK, :], ACT.Copy).then_inc(q_t_ready, 1)
                act.wait_ge(dq_stored, 16 * (t + 1))
                act.wait_ge(q_stored, 16 * (t + 1))

            act.wait_ge(eps_set, 1)
            square_x(0)
            keep_x_t(0)
            with act.Fori(0, CHUNKS - 1) as t:
                chunk(t, True)
            chunk(CHUNKS - 1, False)

        @block.vector
        def _(dve):
            dve.memset(eps[:, :], EPS).then_inc(eps_set, 1)

            def norm_x(t):
                dve.wait_ge(x_rooted, t + 1)
                dve.reciprocal(x_stat[:, 2:3], x_stat[:, 1:2]).then_inc(x_inverted, 1)
                dve.wait_ge(x_inverted, t + 1)
                dve.tensor_scalar(x_scaled[:, :], x_rows[:, :], x_stat[:, 2:3], None, ALU.mult).then_inc(x_normed, 1)

            def chunk(t, more):
                cos = cos2[:, bass.ds(t, 1), :]
                sin = sin2[:, bass.ds(t, 1), :]
                dve.wait_ge(c_rooted, 2 * t + 2)
                dve.reciprocal(c_stat[:, 4:6], c_stat[:, 2:4]).then_inc(c_inverted, 1)
                dve.wait_ge(c_inverted, t + 1)
                dve.tensor_scalar(c_scaled[:, 0:Q_RANK], pair_b[:, 0:Q_RANK], c_stat[:, 4:5], None, ALU.mult).then_inc(c_normed, 1)
                dve.tensor_scalar(c_scaled[:, Q_RANK:C_COLS], pair_b[:, BANK:BANK + KV_RANK], c_stat[:, 5:6], None,
                                  ALU.mult).then_inc(c_normed, 1)
                at = BANK + KV_RANK
                dve.tensor_tensor(k_rope_a[:, :].unsqueeze(1), pair_b[:, at:at + ROPE].unsqueeze(1), cos, ALU.mult).then_inc(k_rope_parts, 1)
                dve.tensor_tensor(k_rope_b[:, 0:HALF_ROPE].unsqueeze(1), pair_b[:, at + HALF_ROPE:at + ROPE].unsqueeze(1),
                                  sin[:, :, 0:HALF_ROPE], ALU.mult).then_inc(k_rope_parts, 1)
                dve.tensor_tensor(k_rope_b[:, HALF_ROPE:ROPE].unsqueeze(1), pair_b[:, at:at + HALF_ROPE].unsqueeze(1),
                                  sin[:, :, HALF_ROPE:ROPE], ALU.mult).then_inc(k_rope_parts, 1)
                dve.wait_ge(k_rope_parts, 3 * t + 3)
                dve.tensor_tensor(k_rows[:, :, NOPE:QK], k_rope_a[:, :].unsqueeze(1).to_broadcast([P, HEADS, ROPE]),
                                  k_rope_b[:, :].unsqueeze(1).to_broadcast([P, HEADS, ROPE]), ALU.add).then_inc(k_rope_ready, 1)
                dve.wait_ge(v_projected, t + 1)
                dve.tensor_copy(keep["values"][:, bass.ds(t, 1), WIDTH:2 * WIDTH], pair_d[:, 0:BANK].unsqueeze(1)).then_inc(dv_ready, 1)
                if more:
                    norm_x(t + 1)
                dve.wait_ge(c_turned, t + 1)
                dve.tensor_copy(c_t[:, :], pair_b[:, 0:C_COLS]).then_inc(c_t_ready, 1)
                dve.wait_ge(d_turned, t + 1)
                dve.tensor_copy(keep["dil_k_t"][:, :, bass.ds(t * P, P)],
                                pair_d[:, BANK:2 * BANK].rearrange("p (h q) -> p h q", q=P)).then_inc(dk_t_ready, 1)
                dve.wait_ge(q_rows_ready, t + 1)
                over_heads = lambda a, n: a.to_broadcast([P, HEADS, n])
                dve.tensor_tensor(q_rope_a[:, :, :], q_rows[:, :, NOPE:QK], over_heads(cos, ROPE), ALU.mult).then_inc(q_rope_parts, 1)
                dve.tensor_tensor(q_rope_b[:, :, 0:HALF_ROPE], q_rows[:, :, NOPE + HALF_ROPE:QK],
                                  over_heads(sin[:, :, 0:HALF_ROPE], HALF_ROPE), ALU.mult).then_inc(q_rope_parts, 1)
                dve.tensor_tensor(q_rope_b[:, :, HALF_ROPE:ROPE], q_rows[:, :, NOPE:NOPE + HALF_ROPE],
                                  over_heads(sin[:, :, HALF_ROPE:ROPE], HALF_ROPE), ALU.mult).then_inc(q_rope_parts, 1)
                dve.wait_ge(q_rope_parts, 3 * t + 3)
                dve.tensor_tensor(q_rows[:, :, NOPE:QK], q_rope_a[:, :, :], q_rope_b[:, :, :], ALU.add).then_inc(q_rope_ready, 1)
                dve.wait_ge(k_nope_ready, t + 1)
                dve.tensor_copy(keep["values"][:, bass.ds(t, 1), 0:WIDTH].rearrange("p a (h c) -> p (a h) c", h=HEADS),
                                pair_b[:, :].rearrange("p (h c) -> p h c", h=HEADS)[:, :, NOPE:NOPE + HEAD]).then_inc(v_ready, 1)
                dve.wait_ge(k_turned, t + 1)
                dve.tensor_copy(keep["mla_k_t"][0:QK, :, bass.ds(t * P, P)],
                                pair_c[0:QK, :].rearrange("p (h q) -> p h q", q=P)).then_inc(k_t_ready, 1)

            dve.wait_ge(small_loaded, 96)
            norm_x(0)
            for t in range(DT):
                dve.wait_ge(weight_loaded[t], 16)
                dve.tensor_scalar(w_in[:, t, :], w_in[:, t, :], gain_x[:, t:t + 1], None, ALU.mult).then_inc(weight_gained, 1)
            dve.wait_ge(weight_loaded[DT], 16)
            for t in range(Q_TILES):
                dve.tensor_scalar(w_uq[:, t, :], w_uq[:, t, :], gain_c[:, t:t + 1], None, ALU.mult).then_inc(weight_gained, 1)
            dve.wait_ge(weight_loaded[DT + 1], 16)
            for t in range(KV_TILES):
                dve.tensor_scalar(w_ukv[:, t, :], w_ukv[:, t, :], gain_c[:, Q_TILES + t:Q_TILES + t + 1], None,
                                  ALU.mult).then_inc(weight_gained, 1)
            with dve.Fori(0, CHUNKS - 1) as t:
                chunk(t, True)
            chunk(CHUNKS - 1, False)

        @block.tensor
        def _(pe):
            def turn_x_rows(t):
                pe.wait_ge(x_normed, t + 1)
                for k in range(DT):
                    last = pe.transpose(turn_x[:, P * k:P * (k + 1)], x_scaled[:, P * k:P * (k + 1)], ident[:, :])
                last.then_inc(x_turned, 1)

            def project(to, at, width):
                for k in range(DT):
                    last = pe.matmul(to, x_t[:, P * k:P * (k + 1)], w_in[:, k, at:at + width], start=(k == 0), stop=(k == DT - 1))
                return last

            def chunk(t, more):
                pe.wait_ge(x_t_ready, t + 1)
                project(pair_b[:, 0:Q_RANK], 0, Q_RANK)
                project(pair_b[:, BANK:BANK + KV_RANK + ROPE], Q_RANK, KV_RANK + ROPE).then_inc(c_projected, 1)
                at = C_COLS + ROPE
                project(pair_c[:, 0:BANK], at, WIDTH)
                project(pair_c[:, BANK:2 * BANK], at + WIDTH, WIDTH).then_inc(d_projected, 1)
                project(pair_d[:, 0:BANK], at + 2 * WIDTH, WIDTH).then_inc(v_projected, 1)
                if more:
                    turn_x_rows(t + 1)
                pe.wait_ge(dqk_ready, t + 1)
                pe.wait_ge(dv_ready, t + 1)
                for k in range(DT):
                    last = pe.transpose(pair_d[:, P * k:P * (k + 1)], dqk[:, P * k:P * (k + 1)], ident[:, :])
                last.then_inc(d_turned, 1)
                pe.wait_ge(c_normed, 2 * t + 2)
                pe.wait_ge(k_rope_parts, 3 * t + 3)
                for k in range(C_TILES):
                    last = pe.transpose(pair_b[:, P * k:P * (k + 1)], c_scaled[:, P * k:P * (k + 1)], ident[:, :])
                last.then_inc(c_turned, 1)
                pe.wait_ge(c_t_ready, t + 1)
                for b in range(2):
                    for k in range(Q_TILES):
                        last = pe.matmul(pair_c[:, BANK * b:BANK * b + QH], c_t[:, P * k:P * (k + 1)],
                                         w_uq[:, k, QH * b:QH * (b + 1)], start=(k == 0), stop=(k == Q_TILES - 1))
                last.then_inc(q_projected, 1)
                for b in range(2):
                    for k in range(KV_TILES):
                        at = P * (Q_TILES + k)
                        last = pe.matmul(pair_b[:, BANK * b:BANK * (b + 1)], c_t[:, at:at + P],
                                         w_ukv[:, k, BANK * b:BANK * (b + 1)], start=(k == 0), stop=(k == KV_TILES - 1))
                last.then_inc(kv_projected, 1)
                pe.wait_ge(dq_t_ready, t + 1)
                pe.wait_ge(dk_t_ready, t + 1)
                pe.wait_ge(q_rope_ready, t + 1)
                for h in range(HEADS):
                    last = pe.transpose(pair_d[0:QK, P * h:P * (h + 1)], q_rows[:, h, :], ident[:, :])
                last.then_inc(q_turned, 1)
                pe.wait_ge(k_nope_ready, t + 1)
                pe.wait_ge(k_rope_ready, t + 1)
                for h in range(HEADS):
                    last = pe.transpose(pair_c[0:QK, P * h:P * (h + 1)], k_rows[:, h, :], ident[:, :])
                last.then_inc(k_turned, 1)
                pe.wait_ge(v_ready, t + 1)
                pe.wait_ge(q_t_ready, t + 1)
                pe.wait_ge(k_t_ready, t + 1)

            turn_x_rows(0)
            pe.wait_ge(weight_gained, DT + C_TILES)
            with pe.Fori(0, CHUNKS - 1) as t:
                chunk(t, True)
            chunk(CHUNKS - 1, False)


def attend(nc, io, keep):
    with ExitStack() as ctx:
        sb, ps, sem = allocators(nc, ctx)
        UNITS = 2 * HEADS
        SLOTS = 4
        RUNS = [(0, 2, 2), (2, 4, 4), (4, 6, 6), (6, 7, 7), (7, 8, 8)]
        blocks_of = {t: nb for lo, hi, nb in RUNS for t in range(lo, hi)}
        FIRST_DVE = 4

        ident = sb("a_ident", [P, P])
        w_out = sb("a_w_out", [P, DT, D])
        gain_mix = sb("a_gain_mix", [P, DT])
        eps = sb("a_eps", [P, 1])
        q_mla = sb("a_q_mla", [P, HEADS, P])
        q_dil = sb("a_q_dil", [P, HEADS // 2, P])
        causal = sb("a_causal", [P, SEQ])
        bias = sb("a_bias", [P, SLOTS, SEQ])
        probs = sb("a_probs", [P, 2, SEQ])
        probs_t = sb("a_probs_t", [P, 2, SEQ])
        neg_max = sb("a_neg_max", [P, UNITS])
        sums = sb("a_sums", [P, UNITS])
        inv_sums = sb("a_inv_sums", [P, UNITS])
        mixed = sb("a_mixed", [P, D])
        mixed_normed = sb("a_mixed_normed", [P, D])
        mixed_t = sb("a_mixed_t", [P, D])
        mix_stat = sb("a_mix_stat", [P, 6])
        residual = sb("a_residual", [P, D])
        scores = [ps(f"a_scores{i}", [P, SEQ]) for i in range(2)]
        turned = ps("a_turned", [P, SEQ])
        heads_out = ps("a_heads_out", [P, D])

        w_loaded = sem("a_w_loaded")
        small_loaded = sem("a_small_loaded")
        w_gained = sem("a_w_gained")
        eps_set = sem("a_eps_set")
        q_loaded = sem("a_q_loaded")
        causal_loaded = sem("a_causal_loaded")
        bias_loaded = [sem(f"a_bias_loaded{i}") for i in range(SLOTS)]
        x_loaded = sem("a_x_loaded")
        scored, shifted, exped = sem("a_scored"), sem("a_shifted"), sem("a_exped")
        p_turned, act_p_t, dve_p_t, weighed = sem("a_p_turned"), sem("a_act_p_t"), sem("a_dve_p_t"), sem("a_weighed")
        inverted, mixed_ready = sem("a_inverted"), sem("a_mixed_ready")
        squared, rooted, mix_inverted, normed = sem("a_squared"), sem("a_rooted"), sem("a_mix_inverted"), sem("a_normed")
        mix_turned, act_mix_t, dve_mix_t = sem("a_mix_turned"), sem("a_act_mix_t"), sem("a_dve_mix_t")
        projected, h1_ready, h1_stored = sem("a_projected"), sem("a_h1_ready"), sem("a_h1_stored")
        passed = {eng.engine: sem(f"a_passed_{i}") for i, eng in enumerate((nc.vector, nc.sync))}
        block = ctx.enter_context(nc.Block())

        def for_chunks(eng, body):
            for lo, hi, nb in RUNS:
                if hi - lo == 1:
                    body(lo, nb, hi)
                else:
                    with eng.Fori(lo, hi) as t:
                        body(t, nb, hi)

        def then_plain(eng):
            eng.sem_inc(passed[eng.engine], 1)

        @block.sync
        def _(sp):
            def load_queries(t):
                sp.dma_start(q_mla[0:QK, :, :], io["mla_q_t"][bass.ds(t, 1)].rearrange("a p h q -> (a p) h q")).then_inc(q_loaded, 16)
                sp.dma_start(q_dil[:, :, :], io["dil_q_t"][bass.ds(t, 1)].rearrange("a p h q -> (a p) h q")).then_inc(q_loaded, 16)

            def window(table, t, nb):
                return io["score_bias"][table, :, bass.ds(SEQ - P - P * t, P * nb)]

            def load_causal(t, nb):
                sp.dma_start(causal[:, 0:P * nb], window(0, t, nb)).then_inc(causal_loaded, 16)

            def load_bias(h, t, nb):
                sp.dma_start(bias[:, h % SLOTS, 0:P * nb], window(1 + h, t, nb)).then_inc(bias_loaded[h % SLOTS], 16)

            def chunk(t, nb, end):
                more = end < CHUNKS
                nb_next = blocks_of[end] if more else nb
                if more:
                    sp.wait_ge(shifted, UNITS * t + HEADS)
                    then_plain(sp)
                    load_causal(t + 1, nb_next)
                for h in range(SLOTS, HEADS):
                    sp.wait_ge(shifted, UNITS * t + HEADS + h - SLOTS + 1)
                    then_plain(sp)
                    load_bias(h, t, nb)
                if more:
                    for h in range(SLOTS):
                        sp.wait_ge(shifted, UNITS * t + HEADS + h + SLOTS + 1)
                        then_plain(sp)
                        load_bias(h, t + 1, nb_next)
                    sp.wait_ge(scored, UNITS * (t + 1))
                    then_plain(sp)
                    load_queries(t + 1)
                sp.wait_ge(h1_ready, t + 1)
                then_plain(sp)
                sp.dma_start(io["h1"][bass.ds(t, 1)].rearrange("a p d -> (a p) d"), residual[:, :]).then_inc(h1_stored, 16)
                sp.wait_ge(h1_stored, 16 * (t + 1))
                then_plain(sp)
                if more:
                    sp.dma_start(residual[:, :], io["x"][bass.ds((t + 1) * P, P), :]).then_inc(x_loaded, 16)

            load_queries(0)
            load_causal(0, blocks_of[0])
            sp.dma_start(ident[:, :], io["identity"]).then_inc(small_loaded, 16)
            sp.dma_start(gain_mix[:, :], io["grp_norm"]).then_inc(small_loaded, 16)
            for h in range(SLOTS):
                load_bias(h, 0, blocks_of[0])
            sp.dma_start(w_out[:, :, :], io["w_out"].rearrange("(t p) n -> p t n", p=P)).then_inc(w_loaded, 16)
            sp.dma_start(residual[:, :], io["x"][0:P, :]).then_inc(x_loaded, 16)
            for_chunks(sp, chunk)

        @block.scalar
        def _(act):
            def softmax(t, u):
                act.wait_ge(shifted, UNITS * t + u + 1)
                nk = P * act_blocks[0]
                act.activation(probs[:, u % 2, 0:nk], probs[:, u % 2, 0:nk], ACT.Exp, scale=-1.0,
                               bias=neg_max[:, u:u + 1], accum_out=sums[:, u:u + 1]).then_inc(exped, 1)

            def chunk(t, nb, end):
                act_blocks[0] = nb
                softmax(t, 0)
                for u in range(UNITS):
                    if u + 1 < UNITS:
                        softmax(t, u + 1)
                    act.wait_ge(p_turned, UNITS * t + u + 1)
                    n = P * min(nb, FIRST_DVE)
                    act.activation(probs_t[:, u % 2, 0:n], turned[:, 0:n], ACT.Copy).then_inc(act_p_t, 1)
                for g in range(2):
                    act.wait_ge(mixed_ready, 2 * t + g + 1)
                    act.activation(mixed_normed[:, WIDTH * g:WIDTH * (g + 1)], mixed[:, WIDTH * g:WIDTH * (g + 1)],
                                   ACT.Square, accum_out=mix_stat[:, g:g + 1]).then_inc(squared, 1)
                act.wait_ge(squared, 2 * t + 2)
                act.activation(mix_stat[:, 2:4], mix_stat[:, 0:2], ACT.Sqrt, scale=1.0 / WIDTH, bias=eps[:, :]).then_inc(rooted, 1)
                act.wait_ge(mix_turned, t + 1)
                act.activation(mixed_t[:, 0:BANK], turned[:, 0:BANK], ACT.Copy).then_inc(act_mix_t, 1)

            act_blocks = [0]
            act.wait_ge(eps_set, 1)
            for_chunks(act, chunk)

        @block.vector
        def _(dve):
            def shift(t, u, nb):
                dve.wait_ge(scored, UNITS * t + u + 1)
                nk = P * nb
                if u < HEADS:
                    if u == 0:
                        dve.wait_ge(causal_loaded, 16 * (t + 1))
                    table, scale = causal[:, 0:nk], QK ** -0.5
                else:
                    h = u - HEADS
                    dve.wait_ge(bias_loaded[h % SLOTS], 16 * (2 * t + h // SLOTS + 1))
                    table, scale = bias[:, h % SLOTS, 0:nk], HEAD ** -0.5
                then_plain(dve)
                dve.tensor_tensor_reduce(probs[:, u % 2, 0:nk], scores[u % 2][:, 0:nk], table, -scale, 3e38,
                                         ALU.add, ALU.min, neg_max[:, u:u + 1]).then_inc(shifted, 1)

            def chunk(t, nb, end):
                shift(t, 0, nb)
                for u in range(UNITS):
                    if u + 1 < UNITS:
                        shift(t, u + 1, nb)
                    if nb > FIRST_DVE:
                        at, to = P * FIRST_DVE, P * nb
                        dve.wait_ge(p_turned, UNITS * t + u + 1)
                        dve.tensor_copy(probs_t[:, u % 2, at:to], turned[:, at:to]).then_inc(dve_p_t, 1)
                dve.wait_ge(weighed, t + 1)
                dve.reciprocal(inv_sums[:, :], sums[:, :]).then_inc(inverted, 1)
                dve.wait_ge(inverted, t + 1)
                for g in range(2):
                    by_head = lambda a: a[:, WIDTH * g:WIDTH * (g + 1)].rearrange("p (h c) -> p h c", h=HEADS)
                    dve.tensor_tensor(by_head(mixed), by_head(heads_out),
                                      inv_sums[:, HEADS * g:HEADS * (g + 1)].unsqueeze(2).to_broadcast([P, HEADS, HEAD]),
                                      ALU.mult).then_inc(mixed_ready, 1)
                dve.wait_ge(rooted, t + 1)
                dve.reciprocal(mix_stat[:, 4:6], mix_stat[:, 2:4]).then_inc(mix_inverted, 1)
                dve.wait_ge(mix_inverted, t + 1)
                for g in range(2):
                    dve.tensor_scalar(mixed_normed[:, WIDTH * g:WIDTH * (g + 1)], mixed[:, WIDTH * g:WIDTH * (g + 1)],
                                      mix_stat[:, 4 + g:5 + g], None, ALU.mult).then_inc(normed, 1)
                dve.wait_ge(mix_turned, t + 1)
                dve.tensor_copy(mixed_t[:, BANK:D], turned[:, BANK:D]).then_inc(dve_mix_t, 1)
                dve.wait_ge(projected, t + 1)
                dve.wait_ge(x_loaded, 16 * (t + 1))
                dve.tensor_tensor(residual[:, :], heads_out[:, :], residual[:, :], ALU.add).then_inc(h1_ready, 1)

            dve.memset(eps[:, :], EPS).then_inc(eps_set, 1)
            dve.wait_ge(small_loaded, 32)
            dve.wait_ge(w_loaded, 16)
            for k in range(DT):
                dve.tensor_scalar(w_out[:, k, :], w_out[:, k, :], gain_mix[:, k:k + 1], None, ALU.mult).then_inc(w_gained, 1)
            for_chunks(dve, chunk)

        @block.tensor
        def _(pe):
            def score(t, u, nb):
                if u == 0:
                    pe.wait_ge(q_loaded, 32 * (t + 1))
                if u >= 2:
                    pe.wait_ge(shifted, UNITS * t + u - 1)
                for at in range(0, P * nb, BANK):
                    n = min(BANK, P * nb - at)
                    if u < HEADS:
                        last = pe.matmul(scores[u % 2][:, at:at + n], q_mla[0:QK, u, :], keep["mla_k_t"][0:QK, u, at:at + n],
                                         start=True, stop=True)
                    else:
                        h = u - HEADS
                        rows = slice(HEAD * (h % 2), HEAD * (h % 2) + HEAD)
                        last = pe.matmul(scores[u % 2][:, at:at + n], q_dil[rows, h // 2, :],
                                         keep["dil_k_t"][rows, h // 2, at:at + n], start=True, stop=True)
                last.then_inc(scored, 1)

            def chunk(t, nb, end):
                score(t, 0, nb)
                score(t, 1, nb)
                for u in range(UNITS):
                    pe.wait_ge(exped, UNITS * t + u + 1)
                    for k in range(nb):
                        last = pe.transpose(turned[:, P * k:P * (k + 1)], probs[:, u % 2, P * k:P * (k + 1)], ident[:, :])
                    last.then_inc(p_turned, 1)
                    if u + 2 < UNITS:
                        score(t, u + 2, nb)
                    pe.wait_ge(act_p_t, UNITS * t + u + 1)
                    if nb > FIRST_DVE:
                        pe.wait_ge(dve_p_t, UNITS * (t - FIRST_DVE) + u + 1)
                    for k in range(nb):
                        last = pe.matmul(heads_out[:, HEAD * u:HEAD * (u + 1)], probs_t[:, u % 2, P * k:P * (k + 1)],
                                         keep["values"][:, k, HEAD * u:HEAD * (u + 1)], start=(k == 0), stop=(k == nb - 1))
                last.then_inc(weighed, 1)
                pe.wait_ge(normed, 2 * t + 2)
                for k in range(DT):
                    last = pe.transpose(turned[:, P * k:P * (k + 1)], mixed_normed[:, P * k:P * (k + 1)], ident[:, :])
                last.then_inc(mix_turned, 1)
                pe.wait_ge(act_mix_t, t + 1)
                pe.wait_ge(dve_mix_t, t + 1)
                for c in range(2):
                    for k in range(DT):
                        last = pe.matmul(heads_out[:, BANK * c:BANK * (c + 1)], mixed_t[:, P * k:P * (k + 1)],
                                         w_out[:, k, BANK * c:BANK * (c + 1)], start=(k == 0), stop=(k == DT - 1))
                last.then_inc(projected, 1)
                pe.wait_ge(h1_ready, t + 1)

            pe.wait_ge(small_loaded, 32)
            pe.wait_ge(w_gained, DT)
            for_chunks(pe, chunk)


def attend_memory_and_experts(nc, io):
    ORDER = [("u", k) for k in range(TOPK)]
    for h in range(1, PEER_HEADS):
        for i in range(TOPK):
            ORDER += [("u", TOPK * h + i), ("v", TOPK * (h - 1) + i)]
    ORDER += [("v", k) for k in range(PICKS - TOPK, PICKS)]
    GATHERS = len(ORDER)
    PIECES = GATHERS // RING
    U_END = {h: max(p for p, (kind, k) in enumerate(ORDER) if kind == "u" and k // TOPK == h) for h in range(PEER_HEADS)}
    DIAGONALS = 4
    PIECE_AT = {"end_sum": 0, "end_root": 1, "end_out": 2,
                "square": 3, "norm": 4, "turn": 5, "mem_a": 6, "mem_b": 7, "mem_max": 8, "mem_exp": 9,
                "mem_norm": 10, "mem_turn": 11, "out_a": 12, "out_b": 13, "h2": 14, "square2": 15, "norm2": 16,
                "turn2": 17, "peer_0": 18, "peer_1": 19, "peer_2": 20, "peer_3": 21,
                "keep_0": 19, "keep_1": 20, "keep_2": 21, "keep_3": 22,
                "top_0": 20, "top_1": 21, "top_2": 22, "top_3": 23,
                "pairs": 24, "best_0": 24, "best_1": 25, "best_2": 26, "best_3": 27, "gate_exp": 28,
                "pick_a": 28, "pick_b": 29, "live": 30}
    pieces_at = {n: [name for name, at in PIECE_AT.items() if at == n] for n in range(PIECES)}
    FRONT = [name for name in PIECE_AT if not name.startswith("end")]

    with ExitStack() as ctx:
        sb, ps, sem = allocators(nc, ctx)
        ident = sb("e_ident", [P, P])
        mem_scores = sb("e_mem_scores", [P, DT, D])
        mem_values = sb("e_mem_values", [P, DT, D])
        peer_scores = sb("e_peer_scores", [P, DT, 2 * D])
        gain_ffn = sb("e_gain_ffn", [P, D])
        gain_final = sb("e_gain_final", [P, D])
        slots = sb("e_slots", [P, TOPK])
        eps = sb("e_eps", [P, 1])
        ring = sb("e_ring", [P, RING, D])
        diagonal = sb("e_diagonal", [P, DIAGONALS, P])
        h_next = sb("e_h_next", [P, D])
        rows = sb("e_rows", [P, D])
        rows_t = sb("e_rows_t", [P, D])
        work = sb("e_work", [P, 2 * D])
        stat = sb("e_stat", [P, 3])
        stat2 = sb("e_stat2", [P, 3])
        mem_stat = sb("e_mem_stat", [P, 4, MEM_HEADS])
        top = sb("e_top", [P, PEER_TABLES, TOPK])
        top_at = sb("e_top_at", [P, PEER_TABLES, TOPK], U32)
        top_at_f = top
        best = sb("e_best", [P, PEER_HEADS, TOPK])
        best_at = sb("e_best_at", [P, PICKS], U32)
        place = sb("e_place", [P, 2, PICKS], U32)
        place_f = sb("e_place_f", [P, 2, PICKS])
        key_at = place_f
        gate_next = sb("e_gate_next", [P, PEER_HEADS, TOPK])
        gate_sum = sb("e_gate_sum", [P, 2, PEER_HEADS])
        x_ffn = sb("e_x_ffn", [P, D])
        h_live = sb("e_h_live", [P, D])
        expert_u = sb("e_expert_u", [P, PICKS], U32)
        expert_v = sb("e_expert_v", [P, PICKS], U32)
        gate = sb("e_gate", [P, PEER_HEADS, TOPK])
        dots = sb("e_dots", [P, PICKS])
        active = dots
        coeff = sb("e_coeff", [P, PICKS])
        end_stat = sb("e_end_stat", [P, 3])
        acc = ps("e_acc", [P, D])
        turned = ps("e_turned", [P, D])
        product = [ps(f"e_product{i}", [P, D]) for i in range(2)]

        small_loaded = sem("e_small_loaded")
        tables_loaded = [sem(f"e_tables_loaded{i}") for i in range(3)]
        eps_set = sem("e_eps_set")
        h1_loaded = sem("e_h1_loaded")
        squared, rooted, inverted, normed = sem("e_squared"), sem("e_rooted"), sem("e_inverted"), sem("e_normed")
        rows_turned, rows_t_ready = sem("e_rows_turned"), sem("e_rows_t_ready")
        mem_scored, mem_maxed, mem_negated = sem("e_mem_scored"), sem("e_mem_maxed"), sem("e_mem_negated")
        mem_exped, mem_inverted, mem_normed = sem("e_mem_exped"), sem("e_mem_inverted"), sem("e_mem_normed")
        mem_out, h2_ready = sem("e_mem_out"), sem("e_h2_ready")
        squared2, rooted2, inverted2, normed2 = sem("e_squared2"), sem("e_rooted2"), sem("e_inverted2"), sem("e_normed2")
        peer_scored, scores_kept = sem("e_peer_scored"), sem("e_scores_kept")
        step = sem("e_step")
        gate_shifted, gate_exped = sem("e_gate_shifted"), sem("e_gate_exped")
        expert_u_ready, expert_v_ready = sem("e_expert_u_ready"), sem("e_expert_v_ready")
        gathered = [sem(f"e_gathered{i}") for i in range(RING)]
        u_used, v_used = sem("e_u_used"), sem("e_v_used")
        activated, coeff_ready, diagonal_ready = sem("e_activated"), sem("e_coeff_ready"), sem("e_diagonal_ready")
        h3_ready, h2_kept = sem("e_h3_ready"), sem("e_h2_kept")
        end_squared, end_rooted, end_inverted = sem("e_end_squared"), sem("e_end_rooted"), sem("e_end_inverted")
        out_ready, out_stored = sem("e_out_ready"), sem("e_out_stored")
        passed = {eng.engine: sem(f"e_passed_{i}") for i, eng in enumerate((nc.vector, nc.gpsimd))}
        block = ctx.enter_context(nc.Block())

        def need(eng, semaphore, value):
            if not (isinstance(value, int) and value <= 0):
                eng.wait_ge(semaphore, value)

        def then_plain(eng):
            eng.sem_inc(passed[eng.engine], 1)

        def for_chunks(eng, front, body, end):
            front(0, FRONT)
            body(0, True)
            with eng.Fori(1, CHUNKS - 1) as t:
                body(t, True)
            body(CHUNKS - 1, False)
            end(CHUNKS - 1, ["end_sum", "end_root", "end_out"])

        def pieces(t, more, position, front, end):
            if position % RING != RING - 1:
                return
            names = pieces_at[position // RING]
            if not (isinstance(t, int) and t == 0):
                end(t - 1, [n for n in names if n.startswith("end")])
            if more:
                front(t + 1, [n for n in names if not n.startswith("end")])

        @block.sync
        def _(sp):
            def load_h1(t):
                sp.dma_start(h_next[:, :], io["h1"][bass.ds(t, 1)].rearrange("a p d -> (a p) d")).then_inc(h1_loaded, 16)

            def store_out(t):
                sp.wait_ge(out_ready, t + 1)
                sp.dma_start(io["out"][bass.ds(t, 1)].rearrange("a p d -> (a p) d"), work[:, 0:D]).then_inc(out_stored, 16)

            load_h1(0)
            sp.dma_start(ident[:, :], io["identity"]).then_inc(small_loaded, 16)
            sp.dma_start(slots[:, :], io["slots"]).then_inc(small_loaded, 16)
            sp.dma_start(gain_ffn[:, :], io["norm_ffn_row"].partition_broadcast(P)).then_inc(small_loaded, 16)
            sp.dma_start(gain_final[:, :], io["norm_final_row"].partition_broadcast(P)).then_inc(small_loaded, 16)
            for i, (table, name) in enumerate(((mem_scores, "mem_scores"), (mem_values, "mem_values"),
                                               (peer_scores, "peer_scores"))):
                sp.dma_start(table[:, :, :], io[name]).then_inc(tables_loaded[i], 16)
            sp.wait_ge(h2_kept, 1)
            load_h1(1)
            with sp.Fori(1, CHUNKS - 1) as t:
                sp.wait_ge(h2_kept, t + 1)
                load_h1(t + 1)
                store_out(t - 1)
            store_out(CHUNKS - 2)
            store_out(CHUNKS - 1)
            sp.wait_ge(out_stored, 16 * CHUNKS)

        @block.gpsimd
        def _(pool):
            def body(t, more):
                for p, (kind, k) in enumerate(ORDER):
                    before_kind, before = ORDER[(p - RING) % GATHERS]
                    chunk = t if p >= RING else t - 1
                    need(pool, u_used if before_kind == "u" else v_used, PICKS * chunk + before + 1)
                    if p == 0:
                        pool.wait_ge(expert_u_ready, t + 1)
                    if (kind, k) == ("v", 0):
                        pool.wait_ge(expert_v_ready, t + 1)
                    then_plain(pool)
                    expert, table = (expert_u, io["peer_u"]) if kind == "u" else (expert_v, io["peer_v"])
                    pool.indirect_dma_start(out=ring[:, p % RING, :], out_offset=None, in_=table,
                                            in_offset=bass.IndirectOffsetOnAxis(ap=expert[:, k:k + 1], axis=0)
                                            ).then_inc(gathered[p % RING], 16)

            for_chunks(pool, lambda f, names: None, body, lambda t, names: None)

        @block.scalar
        def _(act):
            def front(f, names):
                for name in names:
                    if name == "square":
                        act.wait_ge(h1_loaded, 16 * (f + 1))
                        act.activation(rows[:, :], h_next[:, :], ACT.Square, accum_out=stat[:, 0:1]).then_inc(squared, 1)
                        act.wait_ge(squared, f + 1)
                        act.activation(stat[:, 1:2], stat[:, 0:1], ACT.Sqrt, scale=1.0 / D, bias=eps[:, :]).then_inc(rooted, 1)
                    elif name in ("turn", "mem_turn", "turn2"):
                        n = 3 * f + 1 + ("turn", "mem_turn", "turn2").index(name)
                        act.wait_ge(rows_turned, n)
                        act.activation(rows_t[:, :], turned[:, :], ACT.Copy).then_inc(rows_t_ready, 1)
                    elif name == "mem_exp":
                        act.wait_ge(mem_negated, f + 1)
                        for h in range(MEM_HEADS):
                            at = slice(MEM_LEN * h, MEM_LEN * (h + 1))
                            act.activation(rows[:, at], product[0][:, at], ACT.Exp, bias=mem_stat[:, 1, h:h + 1],
                                           accum_out=mem_stat[:, 2, h:h + 1]).then_inc(mem_exped, 1)
                    elif name == "square2":
                        act.wait_ge(h2_ready, f + 1)
                        act.activation(rows[:, :], h_next[:, :], ACT.Square, accum_out=stat2[:, 0:1]).then_inc(squared2, 1)
                        act.wait_ge(squared2, f + 1)
                        act.activation(stat2[:, 1:2], stat2[:, 0:1], ACT.Sqrt, scale=1.0 / D, bias=eps[:, :]).then_inc(rooted2, 1)
                    elif name.startswith("keep_"):
                        g = int(name[-1])
                        act.wait_ge(peer_scored, 4 * f + g + 1)
                        if g == 0:
                            need(act, out_stored, 16 * (f - 1))
                        act.activation(work[:, BANK * g:BANK * (g + 1)],
                                       product[g // 2][:, BANK * (g % 2):BANK * (g % 2 + 1)], ACT.Copy).then_inc(scores_kept, 1)
                    elif name == "gate_exp":
                        act.wait_ge(gate_shifted, f + 1)
                        act.activation(gate_next[:, :, :], gate_next[:, :, :], ACT.Exp).then_inc(gate_exped, 1)

            def end(t, names):
                if "end_root" in names:
                    act.wait_ge(h3_ready, t + 1)
                    act.activation(work[:, D:2 * D], work[:, 0:D], ACT.Square, accum_out=end_stat[:, 0:1]).then_inc(end_squared, 1)
                    act.wait_ge(end_squared, t + 1)
                    act.activation(end_stat[:, 1:2], end_stat[:, 0:1], ACT.Sqrt, scale=1.0 / D, bias=eps[:, :]).then_inc(end_rooted, 1)

            def body(t, more):
                for p, (kind, k) in enumerate(ORDER):
                    if kind == "v":
                        if k % TOPK == 0:
                            h = k // TOPK
                            act.wait_ge(u_used, PICKS * t + TOPK * (h + 1))
                            at = slice(TOPK * h, TOPK * (h + 1))
                            act.activation(active[:, at], dots[:, at], ACT.Gelu).then_inc(activated, 1)
                            act.wait_ge(coeff_ready, PEER_HEADS * t + h + 1)
                        need(act, v_used, PICKS * t + k - DIAGONALS + 1)
                        act.activation(diagonal[:, k % DIAGONALS, :], ident[:, :], ACT.Copy,
                                       scale=coeff[:, k:k + 1]).then_inc(diagonal_ready, 1)
                    pieces(t, more, p, front, end)

            act.wait_ge(eps_set, 1)
            act.wait_ge(small_loaded, 64)
            for_chunks(act, front, body, end)

        @block.vector
        def _(dve):
            STEPS = 5 * PEER_TABLES + 5 * PEER_HEADS + 15
            made = [0]

            def stepped(instruction):
                made[0] += 1
                instruction.then_inc(step, 1)

            def after_steps(f):
                dve.wait_ge(step, STEPS * f + made[0])
                then_plain(dve)

            def top_16(f, values, tops, places):
                for i in range(len(values)):
                    stepped(dve.max(tops[i][:, 0:8], values[i]))
                after_steps(f)
                for i in range(len(values)):
                    stepped(dve.max_index(places[i][:, 0:8], tops[i][:, 0:8], values[i]))
                after_steps(f)
                for i in range(len(values)):
                    stepped(dve.match_replace(values[i], tops[i][:, 0:8], values[i], -3e38))
                after_steps(f)
                for i in range(len(values)):
                    stepped(dve.max(tops[i][:, 8:16], values[i]))
                after_steps(f)
                for i in range(len(values)):
                    stepped(dve.max_index(places[i][:, 8:16], tops[i][:, 8:16], values[i]))

            by_head = lambda a: a.rearrange("p (h k) -> p h k", h=PEER_HEADS)

            def front(f, names):
                for name in names:
                    if name == "norm":
                        dve.wait_ge(rooted, f + 1)
                        dve.reciprocal(stat[:, 2:3], stat[:, 1:2]).then_inc(inverted, 1)
                        dve.wait_ge(inverted, f + 1)
                        dve.tensor_scalar(rows[:, :], h_next[:, :], stat[:, 2:3], None, ALU.mult).then_inc(normed, 1)
                    elif name == "mem_max":
                        dve.wait_ge(mem_scored, f + 1)
                        dve.tensor_reduce(mem_stat[:, 0, :], product[0][:, :].rearrange("p (h m) -> p h m", h=MEM_HEADS),
                                          AX_X, ALU.max).then_inc(mem_maxed, 1)
                        dve.wait_ge(mem_maxed, f + 1)
                        dve.tensor_scalar(mem_stat[:, 1, :], mem_stat[:, 0, :], -1.0, None, ALU.mult).then_inc(mem_negated, 1)
                    elif name == "mem_norm":
                        dve.wait_ge(mem_exped, MEM_HEADS * (f + 1))
                        dve.reciprocal(mem_stat[:, 3, :], mem_stat[:, 2, :]).then_inc(mem_inverted, 1)
                        dve.wait_ge(mem_inverted, f + 1)
                        heads = rows[:, :].rearrange("p (h m) -> p h m", h=MEM_HEADS)
                        dve.tensor_tensor(heads, heads, mem_stat[:, 3, :].unsqueeze(2).to_broadcast([P, MEM_HEADS, MEM_LEN]),
                                          ALU.mult).then_inc(mem_normed, 1)
                    elif name == "h2":
                        dve.wait_ge(mem_out, f + 1)
                        dve.tensor_tensor(h_next[:, :], product[1][:, :], h_next[:, :], ALU.add).then_inc(h2_ready, 1)
                    elif name == "norm2":
                        dve.wait_ge(rooted2, f + 1)
                        dve.reciprocal(stat2[:, 2:3], stat2[:, 1:2]).then_inc(inverted2, 1)
                        dve.wait_ge(inverted2, f + 1)
                        dve.tensor_scalar(rows[:, :], h_next[:, :], stat2[:, 2:3], None, ALU.mult).then_inc(normed2, 1)
                    elif name.startswith("top_"):
                        g = int(name[-1])
                        if g == 0:
                            made[0] = 0
                        dve.wait_ge(scores_kept, 4 * f + g + 1)
                        then_plain(dve)
                        four = range(4 * g, 4 * g + 4)
                        top_16(f, [work[:, PEER_KEYS * i:PEER_KEYS * (i + 1)] for i in four], [top[:, i, :] for i in four],
                               [top_at[:, i, :] for i in four])
                    elif name == "pairs":
                        after_steps(f)
                        halves = top[:, :, :].rearrange("p (h two) k -> p h two k", two=2)
                        stepped(dve.tensor_tensor(
                            work[:, :].rearrange("p (h i j) -> p h i j", h=PEER_HEADS, i=TOPK),
                            halves[:, :, 0, :].unsqueeze(3).to_broadcast([P, PEER_HEADS, TOPK, TOPK]),
                            halves[:, :, 1, :].unsqueeze(2).to_broadcast([P, PEER_HEADS, TOPK, TOPK]), ALU.add))
                        after_steps(f)
                        stepped(dve.tensor_copy(top_at_f[:, :, :], top_at[:, :, :]))
                    elif name.startswith("best_"):
                        g = int(name[-1])
                        after_steps(f)
                        two = range(2 * g, 2 * g + 2)
                        pairs = TOPK * TOPK
                        top_16(f, [work[:, pairs * h:pairs * (h + 1)] for h in two], [best[:, h, :] for h in two],
                               [best_at[:, TOPK * h:TOPK * (h + 1)] for h in two])
                        if g == 3:
                            after_steps(f)
                            dve.tensor_tensor(gate_next[:, :, :], best[:, :, :],
                                              best[:, :, 0:1].to_broadcast([P, PEER_HEADS, TOPK]), ALU.subtract).then_inc(gate_shifted, 1)
                            stepped(dve.tensor_scalar(place[:, 0, :], best_at[:, :], 4, None, ALU.logical_shift_right))
                            stepped(dve.tensor_scalar(place[:, 1, :], best_at[:, :], TOPK - 1, None, ALU.bitwise_and))
                            after_steps(f)
                            stepped(dve.tensor_copy(place_f[:, :, :], place[:, :, :]))
                    elif name in ("pick_a", "pick_b"):
                        half = int(name == "pick_b")
                        after_steps(f)
                        one_hot = work[:, :].rearrange("p (k s) -> p k s", s=TOPK)
                        stepped(dve.tensor_tensor(one_hot, place_f[:, half, :].unsqueeze(2).to_broadcast([P, PICKS, TOPK]),
                                                  slots[:, :].unsqueeze(1).to_broadcast([P, PICKS, TOPK]), ALU.is_equal))
                        after_steps(f)
                        keys = top_at_f[:, :, :].rearrange("p (h two) s -> p h two s", two=2)[:, :, half, :]
                        four_d = work[:, :].rearrange("p (h k s) -> p h k s", h=PEER_HEADS, k=TOPK)
                        stepped(dve.tensor_tensor(four_d, four_d, keys.unsqueeze(2).to_broadcast([P, PEER_HEADS, TOPK, TOPK]),
                                                  ALU.mult))
                        after_steps(f)
                        stepped(dve.tensor_reduce(key_at[:, half, :], one_hot, AX_X, ALU.add))
                    elif name == "live":
                        after_steps(f)
                        dve.scalar_tensor_tensor(expert_u[:, :], key_at[:, 0, :], float(PEER_KEYS), key_at[:, 1, :],
                                                 ALU.mult, ALU.add).then_inc(expert_u_ready, 1)
                        dve.scalar_tensor_tensor(x_ffn[:, :], h_next[:, :], stat2[:, 2:3], gain_ffn[:, :], ALU.mult,
                                                 ALU.mult).then_inc(step, 1)
                        made[0] += 1
                        dve.wait_ge(gate_exped, f + 1)
                        stepped(dve.tensor_reduce(gate_sum[:, 0, :], gate_next[:, :, :], AX_X, ALU.add))
                        after_steps(f)
                        stepped(dve.reciprocal(gate_sum[:, 1, :], gate_sum[:, 0, :]))
                        after_steps(f)
                        stepped(dve.tensor_tensor(gate[:, :, :], gate_next[:, :, :],
                                                  gate_sum[:, 1, :].unsqueeze(2).to_broadcast([P, PEER_HEADS, TOPK]), ALU.mult))
                        after_steps(f)
                        assert made[0] == STEPS, (made[0], STEPS)

            def end(t, names):
                if "end_sum" in names:
                    dve.wait_ge(v_used, PICKS * (t + 1))
                    need(dve, out_stored, 16 * t)
                    dve.tensor_tensor(work[:, 0:D], acc[:, :], h_live[:, :], ALU.add).then_inc(h3_ready, 1)
                    dve.wait_ge(h3_ready, t + 1)
                if "end_out" in names:
                    dve.wait_ge(end_rooted, t + 1)
                    dve.reciprocal(end_stat[:, 2:3], end_stat[:, 1:2]).then_inc(end_inverted, 1)
                    dve.wait_ge(end_inverted, t + 1)
                    dve.scalar_tensor_tensor(work[:, 0:D], work[:, 0:D], end_stat[:, 2:3], gain_final[:, :], ALU.mult,
                                             ALU.mult).then_inc(out_ready, 1)

            def body(t, more):
                for p, (kind, k) in enumerate(ORDER):
                    for h, at in U_END.items():
                        if p == at + 4:
                            dve.wait_ge(activated, PEER_HEADS * t + h + 1)
                            dve.tensor_tensor(coeff[:, TOPK * h:TOPK * (h + 1)], active[:, TOPK * h:TOPK * (h + 1)],
                                              gate[:, h, :], ALU.mult).then_inc(coeff_ready, 1)
                    if kind == "u":
                        dve.wait_ge(gathered[p % RING], 16 * (PIECES * t + p // RING + 1))
                        row = ring[:, p % RING, :]
                        dve.tensor_tensor_reduce(row, row, x_ffn[:, :], 1.0, 0.0, ALU.mult, ALU.add,
                                                 dots[:, k:k + 1]).then_inc(u_used, 1)
                    pieces(t, more, p, front, end)
                    if p == RING - 1:
                        need(dve, v_used, PICKS * t)
                        dve.tensor_copy(expert_v[:, :], expert_u[:, :]).then_inc(expert_v_ready, 1)
                        dve.tensor_copy(h_live[:, :], h_next[:, :]).then_inc(h2_kept, 1)

            dve.memset(eps[:, :], EPS).then_inc(eps_set, 1)
            dve.wait_ge(eps_set, 1)
            dve.wait_ge(small_loaded, 64)
            for_chunks(dve, front, body, end)

        @block.tensor
        def _(pe):
            def multiply(f, to, table, at):
                for k in range(DT):
                    last = pe.matmul(to, rows_t[:, P * k:P * (k + 1)], table[:, k, at:at + BANK], start=(k == 0), stop=(k == DT - 1))
                return last

            def front(f, names):
                for name in names:
                    if name in ("turn", "mem_turn", "turn2"):
                        n = ("turn", "mem_turn", "turn2").index(name)
                        pe.wait_ge((normed, mem_normed, normed2)[n], f + 1)
                        need(pe, rows_t_ready, 3 * f + n)
                        for k in range(DT):
                            last = pe.transpose(turned[:, P * k:P * (k + 1)], rows[:, P * k:P * (k + 1)], ident[:, :])
                        last.then_inc(rows_turned, 1)
                    elif name == "mem_a":
                        pe.wait_ge(rows_t_ready, 3 * f + 1)
                        pe.wait_ge(tables_loaded[0], 16)
                        need(pe, scores_kept, 4 * f)
                        multiply(f, product[0][:, 0:BANK], mem_scores, 0)
                    elif name == "mem_b":
                        multiply(f, product[0][:, BANK:D], mem_scores, BANK).then_inc(mem_scored, 1)
                    elif name == "out_a":
                        pe.wait_ge(rows_t_ready, 3 * f + 2)
                        pe.wait_ge(tables_loaded[1], 16)
                        multiply(f, product[1][:, 0:BANK], mem_values, 0)
                    elif name == "out_b":
                        multiply(f, product[1][:, BANK:D], mem_values, BANK).then_inc(mem_out, 1)
                    elif name.startswith("peer_"):
                        g = int(name[-1])
                        if g == 0:
                            pe.wait_ge(rows_t_ready, 3 * f + 3)
                            pe.wait_ge(tables_loaded[2], 16)
                        multiply(f, product[g // 2][:, BANK * (g % 2):BANK * (g % 2 + 1)], peer_scores,
                                 BANK * g).then_inc(peer_scored, 1)

            def body(t, more):
                for p, (kind, k) in enumerate(ORDER):
                    if kind == "v":
                        if k == 0:
                            need(pe, h3_ready, t)
                        pe.wait_ge(diagonal_ready, PICKS * t + k + 1)
                        pe.wait_ge(gathered[p % RING], 16 * (PIECES * t + p // RING + 1))
                        for c in range(2):
                            last = pe.matmul(acc[:, BANK * c:BANK * (c + 1)], diagonal[:, k % DIAGONALS, :],
                                             ring[:, p % RING, BANK * c:BANK * (c + 1)], start=(k == 0), stop=(k == PICKS - 1))
                        last.then_inc(v_used, 1)
                    pieces(t, more, p, front, lambda t, names: None)

            pe.wait_ge(small_loaded, 64)
            for_chunks(pe, front, body, lambda t, names: None)


def hybrid_layer(nc, io):
    fold_weights(nc, io)
    with ExitStack() as ctx:
        sb, _, _ = allocators(nc, ctx)
        keep = {
            "mla_k_t": sb("mla_k_t", [P, HEADS, SEQ]),
            "dil_k_t": sb("dil_k_t", [P, HEADS // 2, SEQ]),
            "values": sb("values", [P, CHUNKS, 2 * WIDTH]),
        }
        project_tokens(nc, io, keep)
        attend(nc, io, keep)
    attend_memory_and_experts(nc, io)


def kernel(x, mem, norm_mix, w_in, mla_q_norm, mla_kv_norm, mla_w_uq, mla_w_ukv, grp_norm_mla, grp_norm_dil, w_out,
           norm_mem_q, norm_mem_kv, w_mem_q, w_mem_kv, w_mem_o, norm_ffn, peer_w_q, peer_sub_keys, peer_u, peer_v,
           norm_final):
    import concourse.bacc as bacc
    from concourse.bass_utils import run_bass_kernel_spmd

    def columns(*gains):
        return np.ascontiguousarray(np.concatenate([np.asarray(g)[0].reshape(-1, P).T for g in gains], axis=1))

    arrays = {
        "x": np.asarray(x)[0],
        "mem": np.asarray(mem),
        "norm_mix": columns(norm_mix),
        "w_in": np.asarray(w_in)[0],
        "mla_q_norm": columns(mla_q_norm),
        "mla_kv_norm": columns(mla_kv_norm),
        "mla_w_uq": np.asarray(mla_w_uq)[0],
        "mla_w_ukv": np.asarray(mla_w_ukv)[0],
        "grp_norm": columns(grp_norm_mla, grp_norm_dil),
        "w_out": np.asarray(w_out)[0],
        "norm_mem_q": columns(norm_mem_q),
        "norm_mem_kv": columns(norm_mem_kv),
        "w_mem_q": np.asarray(w_mem_q)[0],
        "w_mem_kv": np.asarray(w_mem_kv)[0],
        "w_mem_o": np.asarray(w_mem_o)[0],
        "norm_ffn": columns(norm_ffn),
        "norm_ffn_row": np.asarray(norm_ffn)[0],
        "peer_w_q": np.asarray(peer_w_q)[0],
        "peer_sub_keys": np.asarray(peer_sub_keys)[0].reshape(PEER_TABLES, PEER_KEYS, P),
        "peer_u": np.asarray(peer_u)[0],
        "peer_v": np.asarray(peer_v)[0],
        "norm_final_row": np.asarray(norm_final),
    }
    arrays.update(shape_constants())
    arrays = {name: np.ascontiguousarray(a) for name, a in arrays.items()}

    nc = bacc.Bacc("TRN2", target_bir_lowering=False, num_devices=1)
    io = {name: nc.dram_tensor(name, a.shape, mybir.dt.from_np(a.dtype), kind="ExternalInput").ap()
          for name, a in arrays.items()}
    scratch = {
        "mem_scores": (P, DT, D),
        "mem_values": (P, DT, D),
        "peer_scores": (P, DT, 2 * D),
        "mla_q_t": (CHUNKS, QK, HEADS, P),
        "dil_q_t": (CHUNKS, P, HEADS // 2, P),
        "h1": (CHUNKS, P, D),
    }
    for name, shape in scratch.items():
        io[name] = nc.dram_tensor(name, shape, F32, kind="Internal").ap()
    io["out"] = nc.dram_tensor("out", (CHUNKS, P, D), F32, kind="ExternalOutput").ap()
    hybrid_layer(nc, io)
    result = run_bass_kernel_spmd(nc, [arrays], core_ids=[0])
    return result.results[0]["out"].reshape(1, SEQ, D)
```

```python
from contextlib import ExitStack

import numpy as np

import concourse.bass as bass
from concourse import mybir

F32 = mybir.dt.float32
U32 = mybir.dt.uint32
ALU = mybir.AluOpType
ACT = mybir.ActivationFunctionType
AX_X = mybir.AxisListType.X

P = 128
BANK = 512
D = 1024
DT = D // P
SEQ = 1024
CHUNKS = SEQ // P
EPS = 1e-6
MEM_LEN = 256
MEM_HEADS = 4
MEM_SCALE = (D // MEM_HEADS) ** -0.5
HEADS = 8
NOPE = 64
ROPE = 32
HALF_ROPE = ROPE // 2
QK = NOPE + ROPE
HEAD = 64
Q_RANK = 384
KV_RANK = 256
WIDTH = HEADS * HEAD
IN_COLS = Q_RANK + KV_RANK + ROPE + 3 * WIDTH
PEER_HEADS = 8
PEER_KEYS = 128
PEER_N = PEER_KEYS * PEER_KEYS
PEER_TABLES = 2 * PEER_HEADS
TOPK = 16
PICKS = PEER_HEADS * TOPK
RING = 8
DIL_CONFIGS = ((128, 1), (512, 4), (2048, 16))
BIAS_COLS = SEQ + 2 * P
NOWHERE = -1e30


def allocators(nc, ctx):
    def sb(name, shape, dt=F32):
        return ctx.enter_context(nc.sbuf_tensor(name, shape, dt))

    def ps(name, shape):
        return ctx.enter_context(nc.psum_tensor(name, shape, F32))

    def sem(name):
        return ctx.enter_context(nc.semaphore(name))

    return sb, ps, sem


def shape_constants():
    inv = 1.0 / (np.float32(10000.0) ** (np.arange(0, ROPE, 2, dtype=np.float32) / np.float32(ROPE)))
    angle = np.arange(SEQ, dtype=np.float32)[:, None] * inv.astype(np.float32)[None, :]
    cos, sin = np.cos(angle), np.sin(angle)

    def by_chunk(a):
        return np.ascontiguousarray(a.reshape(CHUNKS, P, ROPE).transpose(1, 0, 2), dtype=np.float32)

    distance = (np.arange(P)[:, None] + (SEQ - P) - np.arange(BIAS_COLS)[None, :]).astype(np.float64)
    count = np.zeros_like(distance)
    for window, dilation in DIL_CONFIGS:
        count += (distance >= 0) & (distance <= window) & (distance % dilation == 0)
    bias = np.full((1 + HEADS, P, BIAS_COLS), NOWHERE, dtype=np.float32)
    bias[0][distance >= 0] = 0.0
    seen = count > 0
    for h in range(HEADS):
        slope = 2.0 ** (-8.0 * (h + 1) / HEADS)
        bias[1 + h][seen] = (np.log(count[seen]) - slope * distance[seen]) * HEAD ** 0.5
    return {
        "identity": np.eye(P, dtype=np.float32),
        "cos2": by_chunk(np.concatenate([cos, cos], axis=1)),
        "sin2": by_chunk(np.concatenate([-sin, sin], axis=1)),
        "score_bias": bias,
        "slots": np.tile(np.arange(TOPK, dtype=np.float32), (P, 1)),
    }


def fold_weights(nc, io):
    with ExitStack() as ctx:
        sb, ps, sem = allocators(nc, ctx)
        ident = sb("f_ident", [P, P])
        mem_rows = sb("f_mem_rows", [P, 2, D])
        mem_scaled = sb("f_mem_scaled", [P, 2, D])
        mem_sumsq = sb("f_mem_sumsq", [P, 2])
        mem_rms = sb("f_mem_rms", [P, 2])
        mem_rstd = sb("f_mem_rstd", [P, 2])
        eps = sb("f_eps", [P, 1])
        gain_kv = sb("f_gain_kv", [P, DT])
        gain_q = sb("f_gain_q", [P, DT])
        gain_ffn = sb("f_gain_ffn", [P, DT])
        mem_t = sb("f_mem_t", [P, DT, MEM_LEN])
        w_big = sb("f_w_big", [P, DT, 2 * D])
        w_o = sb("f_w_o", [P, DT, D])
        w_q = sb("f_w_q", [P, DT, D])
        k_t = sb("f_k_t", [P, DT, MEM_LEN])
        v_t = sb("f_v_t", [P, DT, MEM_LEN])
        turned = sb("f_turned", [P, 4, D])
        keys = mem_rows[:, :, :].rearrange("p t (i n) -> p (t i) n", n=PEER_KEYS)
        keys_t = mem_scaled[:, :, :].rearrange("p t (i n) -> p (t i) n", n=PEER_KEYS)
        stage_v = sb("f_stage_v", [P, 2, D])
        stage_s = sb("f_stage_s", [P, 2, D])
        pair = [ps(f"f_pair{i}", [P, D]) for i in range(4)]

        mem_loaded = sem("f_mem_loaded")
        small_loaded = sem("f_small_loaded")
        kv_loaded = [sem(f"f_kv_loaded{i}") for i in range(4)]
        o_loaded = sem("f_o_loaded")
        q_loaded = sem("f_q_loaded")
        keys_loaded = sem("f_keys_loaded")
        peer_loaded = sem("f_peer_loaded")
        eps_set = sem("f_eps_set")
        mem_squared = sem("f_mem_squared")
        mem_rooted = sem("f_mem_rooted")
        mem_inverted = sem("f_mem_inverted")
        mem_normed = sem("f_mem_normed")
        pair_filled = sem("f_pair_filled")
        act_emptied = sem("f_act_emptied")
        dve_emptied = sem("f_dve_emptied")
        stored_v = [sem(f"f_stored_v{i}") for i in range(2)]
        stored_s = [sem(f"f_stored_s{i}") for i in range(2)]

        tasks = [("mem_t", 0), ("mem_t", 1), ("k_t", 0), ("k_t", 1), ("v_t", 0), ("v_t", 1)]
        tasks += [("mem_values", kt) for kt in range(DT)]
        tasks += [("turn_q", 0), ("turn_q", 1)]
        for h in range(MEM_HEADS):
            if h + 1 < MEM_HEADS:
                tasks += [("turn_q", 2 * h + 2), ("turn_q", 2 * h + 3)]
            tasks += [("mem_scores", 2 * h), ("mem_scores", 2 * h + 1)]
        tasks += [("turn_keys", 0), ("turn_keys", 1), ("turn_peer", 0)]
        for i in range(PEER_TABLES):
            if i + 1 < PEER_TABLES:
                tasks += [("turn_peer", i + 1)]
            tasks += [("peer_scores", i)]
        by_dve = {"mem_t", "mem_scores", "peer_scores", "turn_keys"}
        emptied_at = {}
        counts = {True: 0, False: 0}
        for task in tasks:
            counts[task[0] in by_dve] += 1
            emptied_at[task] = (dve_emptied if task[0] in by_dve else act_emptied, counts[task[0] in by_dve])
        number = {task: n for n, task in enumerate(tasks)}

        def wait_emptied(eng, kind, i):
            eng.wait_ge(*emptied_at[(kind, i)])

        block = ctx.enter_context(nc.Block())

        @block.sync
        def _(sp):
            sp.dma_start(mem_rows[:, :, :], io["mem"].rearrange("b (t p) d -> p (b t) d", p=P)).then_inc(mem_loaded, 16)
            sp.dma_start(ident[:, :], io["identity"]).then_inc(small_loaded, 16)
            sp.dma_start(gain_kv[:, :], io["norm_mem_kv"]).then_inc(small_loaded, 16)
            sp.dma_start(gain_q[:, :], io["norm_mem_q"]).then_inc(small_loaded, 16)
            sp.dma_start(gain_ffn[:, :], io["norm_ffn"]).then_inc(small_loaded, 16)
            kv_weights = io["w_mem_kv"].rearrange("(t p) n -> p t n", p=P)
            for i in range(4):
                at = slice(BANK * i, BANK * (i + 1))
                sp.dma_start(w_big[:, :, at], kv_weights[:, :, at]).then_inc(kv_loaded[i], 16)
            sp.dma_start(w_o[:, :, :], io["w_mem_o"].rearrange("(t p) n -> p t n", p=P)).then_inc(o_loaded, 16)
            sp.dma_start(w_q[:, :, :], io["w_mem_q"].rearrange("(t p) n -> p t n", p=P)).then_inc(q_loaded, 16)
            sp.wait_ge(pair_filled, number[("mem_t", 1)] + 1)
            sp.dma_start(keys, io["peer_sub_keys"].rearrange("i n d -> n i d")).then_inc(keys_loaded, 16)
            sp.wait_ge(pair_filled, number[("v_t", 1)] + 1)
            sp.dma_start(w_big[:, :, :], io["peer_w_q"].rearrange("(t p) n -> p t n", p=P)).then_inc(peer_loaded, 16)
            for kt in range(DT):
                wait_emptied(sp, "mem_values", kt)
                sp.dma_start(io["mem_values"][:, kt, :], stage_v[:, kt % 2, :]).then_inc(stored_v[kt % 2], 16)
            for n in range(DT):
                wait_emptied(sp, "mem_scores", n)
                h, half = divmod(n, 2)
                sp.dma_start(io["mem_scores"][:, 4 * half:4 * half + 4, MEM_LEN * h:MEM_LEN * (h + 1)],
                             stage_s[:, n % 2, :].rearrange("p (t m) -> p t m", t=4)).then_inc(stored_s[n % 2], 16)
            for i in range(PEER_TABLES):
                wait_emptied(sp, "peer_scores", i)
                sp.dma_start(io["peer_scores"][:, :, P * i:P * (i + 1)],
                             stage_s[:, i % 2, :].rearrange("p (t m) -> p t m", t=DT)).then_inc(stored_s[i % 2], 16)
            for i in range(2):
                sp.wait_ge(stored_v[i], 16 * DT // 2)
                sp.wait_ge(stored_s[i], 16 * (DT + PEER_TABLES) // 2)

        @block.scalar
        def _(act):
            act.wait_ge(mem_loaded, 16)
            for t in range(2):
                act.activation(mem_scaled[:, t, :], mem_rows[:, t, :], ACT.Square,
                               accum_out=mem_sumsq[:, t:t + 1]).then_inc(mem_squared, 1)
            act.wait_ge(mem_squared, 2)
            act.wait_ge(eps_set, 1)
            act.activation(mem_rms[:, :], mem_sumsq[:, :], ACT.Sqrt, scale=1.0 / D, bias=eps[:, :]).then_inc(mem_rooted, 1)
            for n, (kind, i) in enumerate(tasks):
                if kind in by_dve:
                    continue
                act.wait_ge(pair_filled, n + 1)
                full = pair[n % 4]
                if kind == "k_t":
                    act.activation(k_t[:, 4 * i:4 * i + 4, :].rearrange("p t m -> p (t m)"), full[:, :], ACT.Copy,
                                   scale=MEM_SCALE).then_inc(act_emptied, 1)
                elif kind == "v_t":
                    act.activation(v_t[:, 4 * i:4 * i + 4, :].rearrange("p t m -> p (t m)"), full[:, :],
                                   ACT.Copy).then_inc(act_emptied, 1)
                elif kind == "mem_values":
                    if i >= 2:
                        act.wait_ge(stored_v[i % 2], 16 * (i // 2))
                    act.activation(stage_v[:, i % 2, :], full[:, :], ACT.Copy).then_inc(act_emptied, 1)
                elif kind == "turn_q":
                    if i >= 4:
                        act.wait_ge(pair_filled, number[("mem_scores", 2 * (i // 2 - 2) + 1)] + 1)
                    act.activation(turned[:, i % 4, :], full[:, :], ACT.Copy).then_inc(act_emptied, 1)
                elif kind == "turn_peer":
                    before = ("mem_scores", 2 * MEM_HEADS - 1) if i < 4 else ("peer_scores", i - 4)
                    act.wait_ge(pair_filled, number[before] + 1)
                    act.activation(turned[:, i % 4, :], full[:, :], ACT.Copy).then_inc(act_emptied, 1)

        @block.vector
        def _(dve):
            dve.memset(eps[:, :], EPS).then_inc(eps_set, 1)
            dve.wait_ge(mem_rooted, 1)
            dve.reciprocal(mem_rstd[:, :], mem_rms[:, :]).then_inc(mem_inverted, 1)
            dve.wait_ge(mem_inverted, 1)
            for t in range(2):
                dve.tensor_scalar(mem_scaled[:, t, :], mem_rows[:, t, :], mem_rstd[:, t:t + 1], None,
                                  ALU.mult).then_inc(mem_normed, 1)
            dve.wait_ge(small_loaded, 64)
            stored = 0
            for n, (kind, i) in enumerate(tasks):
                if kind not in by_dve:
                    continue
                dve.wait_ge(pair_filled, n + 1)
                full = pair[n % 4]
                if kind == "mem_t":
                    dve.tensor_tensor(mem_t[:, :, P * i:P * (i + 1)], full[:, :].rearrange("p (t m) -> p t m", t=DT),
                                      gain_kv[:, :].unsqueeze(2).to_broadcast([P, DT, P]), ALU.mult).then_inc(dve_emptied, 1)
                elif kind == "mem_scores":
                    if i >= 2:
                        dve.wait_ge(stored_s[i % 2], 16 * (i // 2))
                    half = i % 2
                    dve.tensor_tensor(stage_s[:, i % 2, :].rearrange("p (t m) -> p t m", t=4),
                                      full[:, :].rearrange("p (t m) -> p t m", t=4),
                                      gain_q[:, 4 * half:4 * half + 4].unsqueeze(2).to_broadcast([P, 4, MEM_LEN]),
                                      ALU.mult).then_inc(dve_emptied, 1)
                elif kind == "turn_keys":
                    dve.tensor_copy(keys_t[:, 8 * i:8 * i + 8, :].rearrange("p i n -> p (i n)"),
                                    full[:, :]).then_inc(dve_emptied, 1)
                elif kind == "peer_scores":
                    dve.wait_ge(stored_s[i % 2], 16 * ((DT + i) // 2))
                    dve.tensor_tensor(stage_s[:, i % 2, :].rearrange("p (t m) -> p t m", t=DT),
                                      full[:, :].rearrange("p (t m) -> p t m", t=DT),
                                      gain_ffn[:, :].unsqueeze(2).to_broadcast([P, DT, P]),
                                      ALU.mult).then_inc(dve_emptied, 1)

        @block.tensor
        def _(pe):
            pe.wait_ge(small_loaded, 64)
            for n, (kind, i) in enumerate(tasks):
                to = pair[n % 4]
                if n >= 4:
                    pe.wait_ge(*emptied_at[tasks[n - 4]])
                if kind == "mem_t":
                    pe.wait_ge(mem_normed, 2)
                    for t in range(DT):
                        last = pe.transpose(to[:, P * t:P * (t + 1)], mem_scaled[:, i, P * t:P * (t + 1)], ident[:, :])
                elif kind in ("k_t", "v_t"):
                    pe.wait_ge(kv_loaded[2 * (kind == "v_t") + i], 16)
                    wait_emptied(pe, "mem_t", 0)
                    wait_emptied(pe, "mem_t", 1)
                    at = (D if kind == "v_t" else 0) + 4 * P * i
                    for j in range(4):
                        for t in range(DT):
                            last = pe.matmul(to[:, MEM_LEN * j:MEM_LEN * (j + 1)], w_big[:, t, at + P * j:at + P * (j + 1)],
                                             mem_t[:, t, :], start=(t == 0), stop=(t == DT - 1))
                elif kind == "mem_values":
                    pe.wait_ge(o_loaded, 16)
                    h, m = divmod(i, 2)
                    wait_emptied(pe, "v_t", 0)
                    wait_emptied(pe, "v_t", 1)
                    for c in range(2):
                        for j in range(2):
                            last = pe.matmul(to[:, BANK * c:BANK * (c + 1)], v_t[:, 2 * h + j, P * m:P * (m + 1)],
                                             w_o[:, 2 * h + j, BANK * c:BANK * (c + 1)], start=(j == 0), stop=(j == 1))
                elif kind == "turn_q":
                    pe.wait_ge(q_loaded, 16)
                    for t in range(DT):
                        last = pe.transpose(to[:, P * t:P * (t + 1)], w_q[:, t, P * i:P * (i + 1)], ident[:, :])
                elif kind == "mem_scores":
                    h, half = divmod(i, 2)
                    wait_emptied(pe, "k_t", 1)
                    for j in range(2):
                        wait_emptied(pe, "turn_q", 2 * h + j)
                    for t in range(4):
                        for j in range(2):
                            at = P * (4 * half + t)
                            last = pe.matmul(to[:, MEM_LEN * t:MEM_LEN * (t + 1)], turned[:, (2 * h + j) % 4, at:at + P],
                                             k_t[:, 2 * h + j, :], start=(j == 0), stop=(j == 1))
                elif kind == "turn_keys":
                    pe.wait_ge(keys_loaded, 16)
                    for j in range(8):
                        last = pe.transpose(to[:, P * j:P * (j + 1)], keys[:, 8 * i + j, :], ident[:, :])
                elif kind == "turn_peer":
                    pe.wait_ge(peer_loaded, 16)
                    for t in range(DT):
                        last = pe.transpose(to[:, P * t:P * (t + 1)], w_big[:, t, P * i:P * (i + 1)], ident[:, :])
                elif kind == "peer_scores":
                    wait_emptied(pe, "turn_keys", 1)
                    wait_emptied(pe, "turn_peer", i)
                    for t in range(DT):
                        last = pe.matmul(to[:, P * t:P * (t + 1)], turned[:, i % 4, P * t:P * (t + 1)],
                                         keys_t[:, i, :], start=True, stop=True)
                last.then_inc(pair_filled, 1)


def project_tokens(nc, io, keep):
    with ExitStack() as ctx:
        sb, ps, sem = allocators(nc, ctx)
        Q_TILES, KV_TILES = Q_RANK // P, KV_RANK // P
        C_TILES = Q_TILES + KV_TILES
        C_COLS = Q_RANK + KV_RANK
        QH = HEADS * QK // 2

        ident = sb("p_ident", [P, P])
        w_in = sb("p_w_in", [P, DT, IN_COLS])
        w_uq = sb("p_w_uq", [P, Q_TILES, HEADS * QK])
        w_ukv = sb("p_w_ukv", [P, KV_TILES, HEADS * (NOPE + HEAD)])
        gain_x = sb("p_gain_x", [P, DT])
        gain_c = sb("p_gain_c", [P, C_TILES])
        cos2 = sb("p_cos2", [P, CHUNKS, ROPE])
        sin2 = sb("p_sin2", [P, CHUNKS, ROPE])
        eps = sb("p_eps", [P, 1])
        x_rows = sb("p_x_rows", [P, D])
        x_scaled = sb("p_x_scaled", [P, D])
        x_t = sb("p_x_t", [P, D])
        x_stat = sb("p_x_stat", [P, 3])
        c_scaled = sb("p_c_scaled", [P, C_COLS])
        c_t = sb("p_c_t", [P, C_COLS])
        c_stat = sb("p_c_stat", [P, 6])
        dqk = sb("p_dqk", [P, 2 * WIDTH])
        q_rows = sb("p_q_rows", [P, HEADS, QK])
        k_rows = sb("p_k_rows", [P, HEADS, QK])
        q_rope_a = sb("p_q_rope_a", [P, HEADS, ROPE])
        q_rope_b = sb("p_q_rope_b", [P, HEADS, ROPE])
        k_rope_a = sb("p_k_rope_a", [P, ROPE])
        k_rope_b = sb("p_k_rope_b", [P, ROPE])
        q_out = sb("p_q_out", [QK, HEADS, P])
        dq_out = sb("p_dq_out", [P, HEADS // 2, P])
        turn_x = ps("p_turn_x", [P, D])
        pair_b = ps("p_pair_b", [P, D])
        pair_c = ps("p_pair_c", [P, D])
        pair_d = ps("p_pair_d", [P, D])

        weight_loaded = [sem(f"p_weight_loaded{i}") for i in range(DT + 2)]
        small_loaded = sem("p_small_loaded")
        weight_gained = sem("p_weight_gained")
        eps_set = sem("p_eps_set")
        x_loaded = sem("p_x_loaded")
        x_squared, x_rooted, x_inverted = sem("p_x_squared"), sem("p_x_rooted"), sem("p_x_inverted")
        x_normed, x_turned, x_t_ready = sem("p_x_normed"), sem("p_x_turned"), sem("p_x_t_ready")
        c_projected, d_projected, v_projected = sem("p_c_projected"), sem("p_d_projected"), sem("p_v_projected")
        c_squared, c_rooted, c_inverted = sem("p_c_squared"), sem("p_c_rooted"), sem("p_c_inverted")
        c_normed, c_turned, c_t_ready = sem("p_c_normed"), sem("p_c_turned"), sem("p_c_t_ready")
        dqk_ready, d_turned, dq_t_ready, dk_t_ready = (sem("p_dqk_ready"), sem("p_d_turned"), sem("p_dq_t_ready"),
                                                       sem("p_dk_t_ready"))
        q_projected, kv_projected = sem("p_q_projected"), sem("p_kv_projected")
        q_rows_ready, k_nope_ready = sem("p_q_rows_ready"), sem("p_k_nope_ready")
        q_rope_parts, q_rope_ready = sem("p_q_rope_parts"), sem("p_q_rope_ready")
        k_rope_parts, k_rope_ready = sem("p_k_rope_parts"), sem("p_k_rope_ready")
        q_turned, q_t_ready, k_turned, k_t_ready = (sem("p_q_turned"), sem("p_q_t_ready"), sem("p_k_turned"),
                                                    sem("p_k_t_ready"))
        v_ready, dv_ready = sem("p_v_ready"), sem("p_dv_ready")
        q_stored, dq_stored = sem("p_q_stored"), sem("p_dq_stored")
        block = ctx.enter_context(nc.Block())

        @block.sync
        def _(sp):
            sp.dma_start(x_rows[:, :], io["x"][0:P, :]).then_inc(x_loaded, 16)
            sp.dma_start(ident[:, :], io["identity"]).then_inc(small_loaded, 16)
            sp.dma_start(gain_x[:, :], io["norm_mix"]).then_inc(small_loaded, 16)
            sp.dma_start(gain_c[:, 0:Q_TILES], io["mla_q_norm"]).then_inc(small_loaded, 16)
            sp.dma_start(gain_c[:, Q_TILES:C_TILES], io["mla_kv_norm"]).then_inc(small_loaded, 16)
            sp.dma_start(cos2[:, :, :], io["cos2"]).then_inc(small_loaded, 16)
            sp.dma_start(sin2[:, :, :], io["sin2"]).then_inc(small_loaded, 16)
            for t in range(DT):
                sp.dma_start(w_in[:, t, :], io["w_in"][P * t:P * (t + 1), :]).then_inc(weight_loaded[t], 16)
            sp.dma_start(w_uq[:, :, :], io["mla_w_uq"].rearrange("(t p) n -> p t n", p=P)).then_inc(weight_loaded[DT], 16)
            sp.dma_start(w_ukv[:, :, :], io["mla_w_ukv"].rearrange("(t p) n -> p t n", p=P)).then_inc(weight_loaded[DT + 1], 16)

            def store_queries(t):
                sp.wait_ge(dq_t_ready, t + 1)
                sp.dma_start(io["dil_q_t"][bass.ds(t, 1)].rearrange("a p h q -> (a p) h q"), dq_out[:, :, :]).then_inc(dq_stored, 16)
                sp.wait_ge(q_t_ready, t + 1)
                sp.dma_start(io["mla_q_t"][bass.ds(t, 1)].rearrange("a p h q -> (a p) h q"), q_out[:, :, :]).then_inc(q_stored, 16)

            with sp.Fori(0, CHUNKS - 1) as t:
                sp.wait_ge(x_normed, t + 1)
                sp.dma_start(x_rows[:, :], io["x"][bass.ds((t + 1) * P, P), :]).then_inc(x_loaded, 16)
                store_queries(t)
            store_queries(CHUNKS - 1)
            sp.wait_ge(dq_stored, 16 * CHUNKS)
            sp.wait_ge(q_stored, 16 * CHUNKS)

        @block.scalar
        def _(act):
            def square_x(t):
                act.wait_ge(x_loaded, 16 * (t + 1))
                act.activation(x_scaled[:, :], x_rows[:, :], ACT.Square, accum_out=x_stat[:, 0:1]).then_inc(x_squared, 1)
                act.wait_ge(x_squared, t + 1)
                act.activation(x_stat[:, 1:2], x_stat[:, 0:1], ACT.Sqrt, scale=1.0 / D, bias=eps[:, :]).then_inc(x_rooted, 1)

            def keep_x_t(t):
                act.wait_ge(x_turned, t + 1)
                act.activation(x_t[:, :], turn_x[:, :], ACT.Copy).then_inc(x_t_ready, 1)

            def chunk(t, more):
                act.wait_ge(c_projected, t + 1)
                act.activation(c_scaled[:, 0:Q_RANK], pair_b[:, 0:Q_RANK], ACT.Square,
                               accum_out=c_stat[:, 0:1]).then_inc(c_squared, 1)
                act.activation(c_scaled[:, Q_RANK:C_COLS], pair_b[:, BANK:BANK + KV_RANK], ACT.Square,
                               accum_out=c_stat[:, 1:2]).then_inc(c_squared, 1)
                act.wait_ge(c_squared, 2 * t + 2)
                act.activation(c_stat[:, 2:3], c_stat[:, 0:1], ACT.Sqrt, scale=1.0 / Q_RANK, bias=eps[:, :]).then_inc(c_rooted, 1)
                act.activation(c_stat[:, 3:4], c_stat[:, 1:2], ACT.Sqrt, scale=1.0 / KV_RANK, bias=eps[:, :]).then_inc(c_rooted, 1)
                act.wait_ge(d_projected, t + 1)
                act.activation(dqk[:, :], pair_c[:, :], ACT.Copy).then_inc(dqk_ready, 1)
                if more:
                    square_x(t + 1)
                    keep_x_t(t + 1)
                act.wait_ge(d_turned, t + 1)
                act.activation(dq_out[:, :, :].rearrange("p h q -> p (h q)"), pair_d[:, 0:BANK], ACT.Copy).then_inc(dq_t_ready, 1)
                act.wait_ge(q_projected, t + 1)
                act.activation(q_rows[:, :, :].rearrange("p (b h) c -> p b (h c)", b=2),
                               pair_c[:, :].rearrange("p (b w) -> p b w", b=2)[:, :, 0:QH], ACT.Copy).then_inc(q_rows_ready, 1)
                act.wait_ge(kv_projected, t + 1)
                act.activation(k_rows[:, :, 0:NOPE], pair_b[:, :].rearrange("p (h c) -> p h c", h=HEADS)[:, :, 0:NOPE],
                               ACT.Copy).then_inc(k_nope_ready, 1)
                act.wait_ge(q_turned, t + 1)
                act.activation(q_out[:, :, :].rearrange("p h q -> p (h q)"), pair_d[0:QK, :], ACT.Copy).then_inc(q_t_ready, 1)
                act.wait_ge(dq_stored, 16 * (t + 1))
                act.wait_ge(q_stored, 16 * (t + 1))

            act.wait_ge(eps_set, 1)
            square_x(0)
            keep_x_t(0)
            with act.Fori(0, CHUNKS - 1) as t:
                chunk(t, True)
            chunk(CHUNKS - 1, False)

        @block.vector
        def _(dve):
            dve.memset(eps[:, :], EPS).then_inc(eps_set, 1)

            def norm_x(t):
                dve.wait_ge(x_rooted, t + 1)
                dve.reciprocal(x_stat[:, 2:3], x_stat[:, 1:2]).then_inc(x_inverted, 1)
                dve.wait_ge(x_inverted, t + 1)
                dve.tensor_scalar(x_scaled[:, :], x_rows[:, :], x_stat[:, 2:3], None, ALU.mult).then_inc(x_normed, 1)

            def chunk(t, more):
                cos = cos2[:, bass.ds(t, 1), :]
                sin = sin2[:, bass.ds(t, 1), :]
                dve.wait_ge(c_rooted, 2 * t + 2)
                dve.reciprocal(c_stat[:, 4:6], c_stat[:, 2:4]).then_inc(c_inverted, 1)
                dve.wait_ge(c_inverted, t + 1)
                dve.tensor_scalar(c_scaled[:, 0:Q_RANK], pair_b[:, 0:Q_RANK], c_stat[:, 4:5], None, ALU.mult).then_inc(c_normed, 1)
                dve.tensor_scalar(c_scaled[:, Q_RANK:C_COLS], pair_b[:, BANK:BANK + KV_RANK], c_stat[:, 5:6], None,
                                  ALU.mult).then_inc(c_normed, 1)
                at = BANK + KV_RANK
                dve.tensor_tensor(k_rope_a[:, :].unsqueeze(1), pair_b[:, at:at + ROPE].unsqueeze(1), cos, ALU.mult).then_inc(k_rope_parts, 1)
                dve.tensor_tensor(k_rope_b[:, 0:HALF_ROPE].unsqueeze(1), pair_b[:, at + HALF_ROPE:at + ROPE].unsqueeze(1),
                                  sin[:, :, 0:HALF_ROPE], ALU.mult).then_inc(k_rope_parts, 1)
                dve.tensor_tensor(k_rope_b[:, HALF_ROPE:ROPE].unsqueeze(1), pair_b[:, at:at + HALF_ROPE].unsqueeze(1),
                                  sin[:, :, HALF_ROPE:ROPE], ALU.mult).then_inc(k_rope_parts, 1)
                dve.wait_ge(k_rope_parts, 3 * t + 3)
                dve.tensor_tensor(k_rows[:, :, NOPE:QK], k_rope_a[:, :].unsqueeze(1).to_broadcast([P, HEADS, ROPE]),
                                  k_rope_b[:, :].unsqueeze(1).to_broadcast([P, HEADS, ROPE]), ALU.add).then_inc(k_rope_ready, 1)
                dve.wait_ge(v_projected, t + 1)
                dve.tensor_copy(keep["values"][:, bass.ds(t, 1), WIDTH:2 * WIDTH], pair_d[:, 0:BANK].unsqueeze(1)).then_inc(dv_ready, 1)
                if more:
                    norm_x(t + 1)
                dve.wait_ge(c_turned, t + 1)
                dve.tensor_copy(c_t[:, :], pair_b[:, 0:C_COLS]).then_inc(c_t_ready, 1)
                dve.wait_ge(d_turned, t + 1)
                dve.tensor_copy(keep["dil_k_t"][:, :, bass.ds(t * P, P)],
                                pair_d[:, BANK:2 * BANK].rearrange("p (h q) -> p h q", q=P)).then_inc(dk_t_ready, 1)
                dve.wait_ge(q_rows_ready, t + 1)
                over_heads = lambda a, n: a.to_broadcast([P, HEADS, n])
                dve.tensor_tensor(q_rope_a[:, :, :], q_rows[:, :, NOPE:QK], over_heads(cos, ROPE), ALU.mult).then_inc(q_rope_parts, 1)
                dve.tensor_tensor(q_rope_b[:, :, 0:HALF_ROPE], q_rows[:, :, NOPE + HALF_ROPE:QK],
                                  over_heads(sin[:, :, 0:HALF_ROPE], HALF_ROPE), ALU.mult).then_inc(q_rope_parts, 1)
                dve.tensor_tensor(q_rope_b[:, :, HALF_ROPE:ROPE], q_rows[:, :, NOPE:NOPE + HALF_ROPE],
                                  over_heads(sin[:, :, HALF_ROPE:ROPE], HALF_ROPE), ALU.mult).then_inc(q_rope_parts, 1)
                dve.wait_ge(q_rope_parts, 3 * t + 3)
                dve.tensor_tensor(q_rows[:, :, NOPE:QK], q_rope_a[:, :, :], q_rope_b[:, :, :], ALU.add).then_inc(q_rope_ready, 1)
                dve.wait_ge(k_nope_ready, t + 1)
                dve.tensor_copy(keep["values"][:, bass.ds(t, 1), 0:WIDTH].rearrange("p a (h c) -> p (a h) c", h=HEADS),
                                pair_b[:, :].rearrange("p (h c) -> p h c", h=HEADS)[:, :, NOPE:NOPE + HEAD]).then_inc(v_ready, 1)
                dve.wait_ge(k_turned, t + 1)
                dve.tensor_copy(keep["mla_k_t"][0:QK, :, bass.ds(t * P, P)],
                                pair_c[0:QK, :].rearrange("p (h q) -> p h q", q=P)).then_inc(k_t_ready, 1)

            dve.wait_ge(small_loaded, 96)
            norm_x(0)
            for t in range(DT):
                dve.wait_ge(weight_loaded[t], 16)
                dve.tensor_scalar(w_in[:, t, :], w_in[:, t, :], gain_x[:, t:t + 1], None, ALU.mult).then_inc(weight_gained, 1)
            dve.wait_ge(weight_loaded[DT], 16)
            for t in range(Q_TILES):
                dve.tensor_scalar(w_uq[:, t, :], w_uq[:, t, :], gain_c[:, t:t + 1], None, ALU.mult).then_inc(weight_gained, 1)
            dve.wait_ge(weight_loaded[DT + 1], 16)
            for t in range(KV_TILES):
                dve.tensor_scalar(w_ukv[:, t, :], w_ukv[:, t, :], gain_c[:, Q_TILES + t:Q_TILES + t + 1], None,
                                  ALU.mult).then_inc(weight_gained, 1)
            with dve.Fori(0, CHUNKS - 1) as t:
                chunk(t, True)
            chunk(CHUNKS - 1, False)

        @block.tensor
        def _(pe):
            def turn_x_rows(t):
                pe.wait_ge(x_normed, t + 1)
                for k in range(DT):
                    last = pe.transpose(turn_x[:, P * k:P * (k + 1)], x_scaled[:, P * k:P * (k + 1)], ident[:, :])
                last.then_inc(x_turned, 1)

            def project(to, at, width):
                for k in range(DT):
                    last = pe.matmul(to, x_t[:, P * k:P * (k + 1)], w_in[:, k, at:at + width], start=(k == 0), stop=(k == DT - 1))
                return last

            def chunk(t, more):
                pe.wait_ge(x_t_ready, t + 1)
                project(pair_b[:, 0:Q_RANK], 0, Q_RANK)
                project(pair_b[:, BANK:BANK + KV_RANK + ROPE], Q_RANK, KV_RANK + ROPE).then_inc(c_projected, 1)
                at = C_COLS + ROPE
                project(pair_c[:, 0:BANK], at, WIDTH)
                project(pair_c[:, BANK:2 * BANK], at + WIDTH, WIDTH).then_inc(d_projected, 1)
                project(pair_d[:, 0:BANK], at + 2 * WIDTH, WIDTH).then_inc(v_projected, 1)
                if more:
                    turn_x_rows(t + 1)
                pe.wait_ge(dqk_ready, t + 1)
                pe.wait_ge(dv_ready, t + 1)
                for k in range(DT):
                    last = pe.transpose(pair_d[:, P * k:P * (k + 1)], dqk[:, P * k:P * (k + 1)], ident[:, :])
                last.then_inc(d_turned, 1)
                pe.wait_ge(c_normed, 2 * t + 2)
                pe.wait_ge(k_rope_parts, 3 * t + 3)
                for k in range(C_TILES):
                    last = pe.transpose(pair_b[:, P * k:P * (k + 1)], c_scaled[:, P * k:P * (k + 1)], ident[:, :])
                last.then_inc(c_turned, 1)
                pe.wait_ge(c_t_ready, t + 1)
                for b in range(2):
                    for k in range(Q_TILES):
                        last = pe.matmul(pair_c[:, BANK * b:BANK * b + QH], c_t[:, P * k:P * (k + 1)],
                                         w_uq[:, k, QH * b:QH * (b + 1)], start=(k == 0), stop=(k == Q_TILES - 1))
                last.then_inc(q_projected, 1)
                for b in range(2):
                    for k in range(KV_TILES):
                        at = P * (Q_TILES + k)
                        last = pe.matmul(pair_b[:, BANK * b:BANK * (b + 1)], c_t[:, at:at + P],
                                         w_ukv[:, k, BANK * b:BANK * (b + 1)], start=(k == 0), stop=(k == KV_TILES - 1))
                last.then_inc(kv_projected, 1)
                pe.wait_ge(dq_t_ready, t + 1)
                pe.wait_ge(dk_t_ready, t + 1)
                pe.wait_ge(q_rope_ready, t + 1)
                for h in range(HEADS):
                    last = pe.transpose(pair_d[0:QK, P * h:P * (h + 1)], q_rows[:, h, :], ident[:, :])
                last.then_inc(q_turned, 1)
                pe.wait_ge(k_nope_ready, t + 1)
                pe.wait_ge(k_rope_ready, t + 1)
                for h in range(HEADS):
                    last = pe.transpose(pair_c[0:QK, P * h:P * (h + 1)], k_rows[:, h, :], ident[:, :])
                last.then_inc(k_turned, 1)
                pe.wait_ge(v_ready, t + 1)
                pe.wait_ge(q_t_ready, t + 1)
                pe.wait_ge(k_t_ready, t + 1)

            turn_x_rows(0)
            pe.wait_ge(weight_gained, DT + C_TILES)
            with pe.Fori(0, CHUNKS - 1) as t:
                chunk(t, True)
            chunk(CHUNKS - 1, False)


def attend(nc, io, keep):
    with ExitStack() as ctx:
        sb, ps, sem = allocators(nc, ctx)
        UNITS = 2 * HEADS
        SLOTS = 4
        FIRST_DVE = 4
        FINISH_AT, ROOT_AT, NORM_AT, TURN_AT, PROJECT_AT = 0, 1, 2, 3, 5
        ALL_UNITS = [(t, u, t + 1) for t in range(CHUNKS) for u in range(UNITS)]

        ident = sb("a_ident", [P, P])
        w_out = sb("a_w_out", [P, DT, D])
        gain_mix = sb("a_gain_mix", [P, DT])
        eps = sb("a_eps", [P, 1])
        q_mla = sb("a_q_mla", [P, HEADS, P])
        q_dil = sb("a_q_dil", [P, HEADS // 2, P])
        causal = sb("a_causal", [P, SEQ])
        bias = sb("a_bias", [P, SLOTS, SEQ])
        probs = sb("a_probs", [P, 2, SEQ])
        probs_t = sb("a_probs_t", [P, 2, SEQ])
        neg_max = sb("a_neg_max", [P, UNITS])
        sums = sb("a_sums", [P, UNITS])
        inv_sums = sb("a_inv_sums", [P, UNITS])
        mixed = sb("a_mixed", [P, D])
        mixed_normed = sb("a_mixed_normed", [P, D])
        mixed_t = sb("a_mixed_t", [P, D])
        mix_stat = sb("a_mix_stat", [P, 6])
        residual = sb("a_residual", [P, D])
        scores = [ps(f"a_scores{i}", [P, SEQ]) for i in range(2)]
        turned = ps("a_turned", [P, SEQ])
        heads_out = ps("a_heads_out", [P, D])

        w_loaded = sem("a_w_loaded")
        small_loaded = sem("a_small_loaded")
        w_gained = sem("a_w_gained")
        eps_set = sem("a_eps_set")
        q_mla_loaded, q_dil_loaded = sem("a_q_mla_loaded"), sem("a_q_dil_loaded")
        causal_loaded = sem("a_causal_loaded")
        bias_loaded = [sem(f"a_bias_loaded{i}") for i in range(SLOTS)]
        x_loaded = sem("a_x_loaded")
        scored, shifted, exped = sem("a_scored"), sem("a_shifted"), sem("a_exped")
        p_turned, act_p_t, dve_p_t, weighed = sem("a_p_turned"), sem("a_act_p_t"), sem("a_dve_p_t"), sem("a_weighed")
        inverted, mixed_ready = sem("a_inverted"), sem("a_mixed_ready")
        squared, rooted, mix_inverted, normed = sem("a_squared"), sem("a_rooted"), sem("a_mix_inverted"), sem("a_normed")
        mix_turned, act_mix_t, dve_mix_t = sem("a_mix_turned"), sem("a_act_mix_t"), sem("a_dve_mix_t")
        projected, h1_ready, h1_stored = sem("a_projected"), sem("a_h1_ready"), sem("a_h1_stored")
        block = ctx.enter_context(nc.Block())

        @block.sync
        def _(sp):
            def load_mla_q(t):
                sp.dma_start(q_mla[0:QK, :, :], io["mla_q_t"][t]).then_inc(q_mla_loaded, 16)

            def load_dil_q(t):
                sp.dma_start(q_dil[:, :, :], io["dil_q_t"][t]).then_inc(q_dil_loaded, 16)

            def window(table, t):
                at = SEQ - P - P * t
                return io["score_bias"][table, :, at:at + P * (t + 1)]

            def load_causal(t):
                sp.dma_start(causal[:, 0:P * (t + 1)], window(0, t)).then_inc(causal_loaded, 16)

            def load_bias(h, t):
                sp.dma_start(bias[:, h % SLOTS, 0:P * (t + 1)], window(1 + h, t)).then_inc(bias_loaded[h % SLOTS], 16)

            def load_residual(t):
                sp.dma_start(residual[:, :], io["x"][P * t:P * (t + 1), :]).then_inc(x_loaded, 16)

            def store_h1(t):
                sp.wait_ge(h1_ready, t + 1)
                sp.dma_start(io["h1"][t], residual[:, :]).then_inc(h1_stored, 16)
                sp.wait_ge(h1_stored, 16 * (t + 1))

            load_mla_q(0)
            load_causal(0)
            sp.dma_start(ident[:, :], io["identity"]).then_inc(small_loaded, 16)
            sp.dma_start(gain_mix[:, :], io["grp_norm"]).then_inc(small_loaded, 16)
            load_dil_q(0)
            for h in range(SLOTS):
                load_bias(h, 0)
            sp.dma_start(w_out[:, :, :], io["w_out"].rearrange("(t p) n -> p t n", p=P)).then_inc(w_loaded, 16)
            load_residual(0)
            for t in range(CHUNKS):
                more = t + 1 < CHUNKS
                if more:
                    sp.wait_ge(scored, UNITS * t + HEADS)
                    load_mla_q(t + 1)
                    sp.wait_ge(shifted, UNITS * t + HEADS)
                    load_causal(t + 1)
                for h in range(SLOTS, HEADS):
                    sp.wait_ge(shifted, UNITS * t + HEADS + h - SLOTS + 1)
                    load_bias(h, t)
                    if t > 0 and h == SLOTS:
                        store_h1(t - 1)
                        load_residual(t)
                if more:
                    for h in range(SLOTS):
                        sp.wait_ge(shifted, UNITS * t + HEADS + h + SLOTS + 1)
                        load_bias(h, t + 1)
                    sp.wait_ge(scored, UNITS * (t + 1))
                    load_dil_q(t + 1)
            store_h1(CHUNKS - 1)

        @block.scalar
        def _(act):
            def softmax(n):
                t, u, nb = ALL_UNITS[n]
                act.wait_ge(shifted, n + 1)
                nk = P * nb
                act.activation(probs[:, u % 2, 0:nk], probs[:, u % 2, 0:nk], ACT.Exp, scale=-1.0,
                               bias=neg_max[:, u:u + 1], accum_out=sums[:, u:u + 1]).then_inc(exped, 1)

            def square_mixed(t, g):
                act.wait_ge(mixed_ready, 2 * t + g + 1)
                act.activation(mixed_normed[:, WIDTH * g:WIDTH * (g + 1)], mixed[:, WIDTH * g:WIDTH * (g + 1)],
                               ACT.Square, accum_out=mix_stat[:, g:g + 1]).then_inc(squared, 1)

            def root_mixed(t):
                square_mixed(t, 1)
                act.wait_ge(squared, 2 * t + 2)
                act.activation(mix_stat[:, 2:4], mix_stat[:, 0:2], ACT.Sqrt, scale=1.0 / WIDTH, bias=eps[:, :]).then_inc(rooted, 1)

            def keep_mixed_t(t):
                act.wait_ge(mix_turned, t + 1)
                act.activation(mixed_t[:, 0:BANK], turned[:, 0:BANK], ACT.Copy).then_inc(act_mix_t, 1)

            act.wait_ge(eps_set, 1)
            softmax(0)
            for n, (t, u, nb) in enumerate(ALL_UNITS):
                if n + 1 < len(ALL_UNITS):
                    softmax(n + 1)
                act.wait_ge(p_turned, n + 1)
                to = P * min(nb, FIRST_DVE)
                act.activation(probs_t[:, u % 2, 0:to], turned[:, 0:to], ACT.Copy).then_inc(act_p_t, 1)
                if u == HEADS + 1:
                    square_mixed(t, 0)
                if t > 0 and u == ROOT_AT:
                    root_mixed(t - 1)
                if t > 0 and u == TURN_AT:
                    keep_mixed_t(t - 1)
            root_mixed(CHUNKS - 1)
            keep_mixed_t(CHUNKS - 1)

        @block.vector
        def _(dve):
            def shift(n):
                t, u, nb = ALL_UNITS[n]
                dve.wait_ge(scored, n + 1)
                nk = P * nb
                if u < HEADS:
                    if u == 0:
                        dve.wait_ge(causal_loaded, 16 * (t + 1))
                    table, scale = causal[:, 0:nk], QK ** -0.5
                else:
                    h = u - HEADS
                    dve.wait_ge(bias_loaded[h % SLOTS], 16 * (2 * t + h // SLOTS + 1))
                    table, scale = bias[:, h % SLOTS, 0:nk], HEAD ** -0.5
                dve.tensor_tensor_reduce(probs[:, u % 2, 0:nk], scores[u % 2][:, 0:nk], table, -scale, 3e38,
                                         ALU.add, ALU.min, neg_max[:, u:u + 1]).then_inc(shifted, 1)

            def finish_group(t, g):
                heads = slice(HEADS * g, HEADS * (g + 1))
                cols = slice(WIDTH * g, WIDTH * (g + 1))
                by_head = lambda a: a[:, cols].rearrange("p (h c) -> p h c", h=HEADS)
                dve.wait_ge(weighed, 2 * t + g + 1)
                dve.reciprocal(inv_sums[:, heads], sums[:, heads]).then_inc(inverted, 1)
                dve.wait_ge(inverted, 2 * t + g + 1)
                dve.tensor_tensor(by_head(mixed), by_head(heads_out),
                                  inv_sums[:, heads].unsqueeze(2).to_broadcast([P, HEADS, HEAD]), ALU.mult).then_inc(mixed_ready, 1)

            def norm_mixed(t):
                dve.wait_ge(rooted, t + 1)
                dve.reciprocal(mix_stat[:, 4:6], mix_stat[:, 2:4]).then_inc(mix_inverted, 1)
                dve.wait_ge(mix_inverted, t + 1)
                for g in range(2):
                    dve.tensor_scalar(mixed_normed[:, WIDTH * g:WIDTH * (g + 1)], mixed[:, WIDTH * g:WIDTH * (g + 1)],
                                      mix_stat[:, 4 + g:5 + g], None, ALU.mult).then_inc(normed, 1)

            def keep_mixed_t(t):
                dve.wait_ge(mix_turned, t + 1)
                dve.tensor_copy(mixed_t[:, BANK:D], turned[:, BANK:D]).then_inc(dve_mix_t, 1)

            def add_residual(t):
                dve.wait_ge(projected, t + 1)
                dve.wait_ge(x_loaded, 16 * (t + 1))
                dve.tensor_tensor(residual[:, :], turned[:, :], residual[:, :], ALU.add).then_inc(h1_ready, 1)

            dve.memset(eps[:, :], EPS).then_inc(eps_set, 1)
            shift(0)
            for n, (t, u, nb) in enumerate(ALL_UNITS):
                if n + 1 < len(ALL_UNITS):
                    shift(n + 1)
                if nb > FIRST_DVE:
                    at, to = P * FIRST_DVE, P * nb
                    dve.wait_ge(p_turned, n + 1)
                    dve.tensor_copy(probs_t[:, u % 2, at:to], turned[:, at:to]).then_inc(dve_p_t, 1)
                if u == HEADS:
                    finish_group(t, 0)
                if t > 0:
                    if u == FINISH_AT:
                        finish_group(t - 1, 1)
                    if u == NORM_AT:
                        norm_mixed(t - 1)
                    if u == TURN_AT:
                        keep_mixed_t(t - 1)
                    if u == PROJECT_AT:
                        add_residual(t - 1)
            finish_group(CHUNKS - 1, 1)
            norm_mixed(CHUNKS - 1)
            keep_mixed_t(CHUNKS - 1)
            add_residual(CHUNKS - 1)

        @block.gpsimd
        def _(pool):
            pool.wait_ge(small_loaded, 32)
            pool.wait_ge(w_loaded, 16)
            for k in range(DT):
                pool.tensor_scalar(w_out[:, k, :], w_out[:, k, :], gain_mix[:, k:k + 1], 1.0, ALU.mult,
                                   ALU.mult).then_inc(w_gained, 1)

        @block.tensor
        def _(pe):
            def score(n):
                t, u, nb = ALL_UNITS[n]
                if u == 0:
                    pe.wait_ge(q_mla_loaded, 16 * (t + 1))
                if u == HEADS:
                    pe.wait_ge(q_dil_loaded, 16 * (t + 1))
                if n >= 2:
                    pe.wait_ge(shifted, n - 1)
                for at in range(0, P * nb, BANK):
                    width = min(BANK, P * nb - at)
                    to = scores[u % 2][:, at:at + width]
                    if u < HEADS:
                        last = pe.matmul(to, q_mla[0:QK, u, :], keep["mla_k_t"][0:QK, u, at:at + width], start=True, stop=True)
                    else:
                        h = u - HEADS
                        rows = slice(HEAD * (h % 2), HEAD * (h % 2) + HEAD)
                        last = pe.matmul(to, q_dil[rows, h // 2, :], keep["dil_k_t"][rows, h // 2, at:at + width],
                                         start=True, stop=True)
                last.then_inc(scored, 1)

            def weigh(n):
                t, u, nb = ALL_UNITS[n]
                pe.wait_ge(act_p_t, n + 1)
                if nb > FIRST_DVE:
                    pe.wait_ge(dve_p_t, n + 1 - UNITS * FIRST_DVE)
                if t > 0 and u in (0, HEADS):
                    pe.wait_ge(mixed_ready, 2 * (t - 1) + u // HEADS + 1)
                for k in range(nb):
                    last = pe.matmul(heads_out[:, HEAD * u:HEAD * (u + 1)], probs_t[:, u % 2, P * k:P * (k + 1)],
                                     keep["values"][:, k, HEAD * u:HEAD * (u + 1)], start=(k == 0), stop=(k == nb - 1))
                if u in (HEADS - 1, UNITS - 1):
                    last.then_inc(weighed, 1)

            def turn_mixed(t):
                pe.wait_ge(normed, 2 * t + 2)
                for k in range(DT):
                    last = pe.transpose(turned[:, P * k:P * (k + 1)], mixed_normed[:, P * k:P * (k + 1)], ident[:, :])
                last.then_inc(mix_turned, 1)

            def project(t):
                pe.wait_ge(w_gained, DT)
                for c in range(2):
                    for k in range(DT):
                        last = pe.matmul(turned[:, BANK * c:BANK * (c + 1)], mixed_t[:, P * k:P * (k + 1)],
                                         w_out[:, k, BANK * c:BANK * (c + 1)], start=(k == 0), stop=(k == DT - 1))
                last.then_inc(projected, 1)

            def wait_mixed_t(t):
                pe.wait_ge(act_mix_t, t + 1)
                pe.wait_ge(dve_mix_t, t + 1)

            pe.wait_ge(small_loaded, 32)
            score(0)
            score(1)
            for n, (t, u, nb) in enumerate(ALL_UNITS):
                if t > 0 and u == TURN_AT + 1:
                    wait_mixed_t(t - 1)
                if t > 0 and u == PROJECT_AT + 1:
                    pe.wait_ge(h1_ready, t)
                pe.wait_ge(exped, n + 1)
                for k in range(nb):
                    last = pe.transpose(turned[:, P * k:P * (k + 1)], probs[:, u % 2, P * k:P * (k + 1)], ident[:, :])
                last.then_inc(p_turned, 1)
                if t > 0 and u == TURN_AT:
                    weigh(n)
                    turn_mixed(t - 1)
                elif t > 0 and u == PROJECT_AT:
                    weigh(n)
                    project(t - 1)
                if n + 2 < len(ALL_UNITS):
                    score(n + 2)
                if not (t > 0 and u in (TURN_AT, PROJECT_AT)):
                    weigh(n)
            turn_mixed(CHUNKS - 1)
            wait_mixed_t(CHUNKS - 1)
            project(CHUNKS - 1)


def attend_memory_and_experts(nc, io):
    ORDER = [("u", k) for k in range(TOPK)]
    for h in range(1, PEER_HEADS):
        for i in range(TOPK):
            ORDER += [("u", TOPK * h + i), ("v", TOPK * (h - 1) + i)]
    ORDER += [("v", k) for k in range(PICKS - TOPK, PICKS)]
    GATHERS = len(ORDER)
    PIECES = GATHERS // RING
    U_END = {h: max(p for p, (kind, k) in enumerate(ORDER) if kind == "u" and k // TOPK == h) for h in range(PEER_HEADS)}
    DIAGONALS = 4
    PIECE_AT = {"end_sum": 0, "end_root": 1, "end_out": 2,
                "square": 3, "norm": 4, "turn": 5, "mem_a": 6, "mem_b": 7, "mem_max": 8, "mem_exp": 9,
                "mem_norm": 10, "mem_turn": 11, "out_a": 12, "out_b": 13, "h2": 14, "square2": 15, "norm2": 16,
                "turn2": 17, "peer_0": 18, "peer_1": 19, "peer_2": 20, "peer_3": 21,
                "keep_0": 19, "keep_1": 20, "keep_2": 21, "keep_3": 22,
                "top_0": 20, "top_1": 21, "top_2": 22, "top_3": 23,
                "pairs": 24, "best_0": 24, "best_1": 25, "best_2": 26, "best_3": 27, "gate_exp": 28,
                "pick_a": 28, "pick_b": 29, "live": 30}
    pieces_at = {n: [name for name, at in PIECE_AT.items() if at == n] for n in range(PIECES)}
    FRONT = [name for name in PIECE_AT if not name.startswith("end")]

    with ExitStack() as ctx:
        sb, ps, sem = allocators(nc, ctx)
        ident = sb("e_ident", [P, P])
        mem_scores = sb("e_mem_scores", [P, DT, D])
        mem_values = sb("e_mem_values", [P, DT, D])
        peer_scores = sb("e_peer_scores", [P, DT, 2 * D])
        gain_ffn = sb("e_gain_ffn", [P, D])
        gain_final = sb("e_gain_final", [P, D])
        slots = sb("e_slots", [P, TOPK])
        eps = sb("e_eps", [P, 1])
        ring = sb("e_ring", [P, RING, D])
        diagonal = sb("e_diagonal", [P, DIAGONALS, P])
        h_next = sb("e_h_next", [P, D])
        rows = sb("e_rows", [P, D])
        rows_t = sb("e_rows_t", [P, D])
        work = sb("e_work", [P, 2 * D])
        stat = sb("e_stat", [P, 3])
        stat2 = sb("e_stat2", [P, 3])
        mem_stat = sb("e_mem_stat", [P, 4, MEM_HEADS])
        top = sb("e_top", [P, PEER_TABLES, TOPK])
        top_at = sb("e_top_at", [P, PEER_TABLES, TOPK], U32)
        top_at_f = top
        best = sb("e_best", [P, PEER_HEADS, TOPK])
        best_at = sb("e_best_at", [P, PICKS], U32)
        place = sb("e_place", [P, 2, PICKS], U32)
        place_f = sb("e_place_f", [P, 2, PICKS])
        key_at = place_f
        gate_next = sb("e_gate_next", [P, PEER_HEADS, TOPK])
        gate_sum = sb("e_gate_sum", [P, 2, PEER_HEADS])
        x_ffn = sb("e_x_ffn", [P, D])
        h_live = sb("e_h_live", [P, D])
        expert_u = sb("e_expert_u", [P, PICKS], U32)
        expert_v = sb("e_expert_v", [P, PICKS], U32)
        gate = sb("e_gate", [P, PEER_HEADS, TOPK])
        dots = sb("e_dots", [P, PICKS])
        active = dots
        coeff = sb("e_coeff", [P, PICKS])
        end_stat = sb("e_end_stat", [P, 3])
        acc = ps("e_acc", [P, D])
        turned = ps("e_turned", [P, D])
        product = [ps(f"e_product{i}", [P, D]) for i in range(2)]

        small_loaded = sem("e_small_loaded")
        tables_loaded = [sem(f"e_tables_loaded{i}") for i in range(3)]
        eps_set = sem("e_eps_set")
        h1_loaded = sem("e_h1_loaded")
        squared, rooted, inverted, normed = sem("e_squared"), sem("e_rooted"), sem("e_inverted"), sem("e_normed")
        rows_turned, rows_t_ready = sem("e_rows_turned"), sem("e_rows_t_ready")
        mem_scored, mem_maxed, mem_negated = sem("e_mem_scored"), sem("e_mem_maxed"), sem("e_mem_negated")
        mem_exped, mem_inverted, mem_normed = sem("e_mem_exped"), sem("e_mem_inverted"), sem("e_mem_normed")
        mem_out, h2_ready = sem("e_mem_out"), sem("e_h2_ready")
        squared2, rooted2, inverted2, normed2 = sem("e_squared2"), sem("e_rooted2"), sem("e_inverted2"), sem("e_normed2")
        peer_scored, scores_kept = sem("e_peer_scored"), sem("e_scores_kept")
        step = sem("e_step")
        gate_shifted, gate_exped = sem("e_gate_shifted"), sem("e_gate_exped")
        expert_u_ready, expert_v_ready = sem("e_expert_u_ready"), sem("e_expert_v_ready")
        gathered = [sem(f"e_gathered{i}") for i in range(RING)]
        u_used, v_used = sem("e_u_used"), sem("e_v_used")
        activated, coeff_ready, diagonal_ready = sem("e_activated"), sem("e_coeff_ready"), sem("e_diagonal_ready")
        h3_ready, h2_kept = sem("e_h3_ready"), sem("e_h2_kept")
        end_squared, end_rooted, end_inverted = sem("e_end_squared"), sem("e_end_rooted"), sem("e_end_inverted")
        out_ready, out_stored = sem("e_out_ready"), sem("e_out_stored")
        passed = {eng.engine: sem(f"e_passed_{i}") for i, eng in enumerate((nc.vector, nc.gpsimd))}
        block = ctx.enter_context(nc.Block())

        def need(eng, semaphore, value):
            if not (isinstance(value, int) and value <= 0):
                eng.wait_ge(semaphore, value)

        def then_plain(eng):
            eng.sem_inc(passed[eng.engine], 1)

        def for_chunks(eng, front, body, end):
            front(0, FRONT)
            body(0, True)
            with eng.Fori(1, CHUNKS - 1) as t:
                body(t, True)
            body(CHUNKS - 1, False)
            end(CHUNKS - 1, ["end_sum", "end_root", "end_out"])

        def pieces(t, more, position, front, end):
            if position % RING != RING - 1:
                return
            names = pieces_at[position // RING]
            if not (isinstance(t, int) and t == 0):
                end(t - 1, [n for n in names if n.startswith("end")])
            if more:
                front(t + 1, [n for n in names if not n.startswith("end")])

        @block.sync
        def _(sp):
            def load_h1(t):
                sp.dma_start(h_next[:, :], io["h1"][bass.ds(t, 1)].rearrange("a p d -> (a p) d")).then_inc(h1_loaded, 16)

            def store_out(t):
                sp.wait_ge(out_ready, t + 1)
                sp.dma_start(io["out"][bass.ds(t, 1)].rearrange("a p d -> (a p) d"), work[:, 0:D]).then_inc(out_stored, 16)

            load_h1(0)
            sp.dma_start(ident[:, :], io["identity"]).then_inc(small_loaded, 16)
            sp.dma_start(slots[:, :], io["slots"]).then_inc(small_loaded, 16)
            sp.dma_start(gain_ffn[:, :], io["norm_ffn_row"].partition_broadcast(P)).then_inc(small_loaded, 16)
            sp.dma_start(gain_final[:, :], io["norm_final_row"].partition_broadcast(P)).then_inc(small_loaded, 16)
            for i, (table, name) in enumerate(((mem_scores, "mem_scores"), (mem_values, "mem_values"),
                                               (peer_scores, "peer_scores"))):
                sp.dma_start(table[:, :, :], io[name]).then_inc(tables_loaded[i], 16)
            sp.wait_ge(h2_kept, 1)
            load_h1(1)
            with sp.Fori(1, CHUNKS - 1) as t:
                sp.wait_ge(h2_kept, t + 1)
                load_h1(t + 1)
                store_out(t - 1)
            store_out(CHUNKS - 2)
            store_out(CHUNKS - 1)
            sp.wait_ge(out_stored, 16 * CHUNKS)

        @block.gpsimd
        def _(pool):
            def body(t, more):
                for p, (kind, k) in enumerate(ORDER):
                    before_kind, before = ORDER[(p - RING) % GATHERS]
                    chunk = t if p >= RING else t - 1
                    need(pool, u_used if before_kind == "u" else v_used, PICKS * chunk + before + 1)
                    if p == 0:
                        pool.wait_ge(expert_u_ready, t + 1)
                    if (kind, k) == ("v", 0):
                        pool.wait_ge(expert_v_ready, t + 1)
                    then_plain(pool)
                    expert, table = (expert_u, io["peer_u"]) if kind == "u" else (expert_v, io["peer_v"])
                    pool.indirect_dma_start(out=ring[:, p % RING, :], out_offset=None, in_=table,
                                            in_offset=bass.IndirectOffsetOnAxis(ap=expert[:, k:k + 1], axis=0)
                                            ).then_inc(gathered[p % RING], 16)

            for_chunks(pool, lambda f, names: None, body, lambda t, names: None)

        @block.scalar
        def _(act):
            def front(f, names):
                for name in names:
                    if name == "square":
                        act.wait_ge(h1_loaded, 16 * (f + 1))
                        act.activation(rows[:, :], h_next[:, :], ACT.Square, accum_out=stat[:, 0:1]).then_inc(squared, 1)
                        act.wait_ge(squared, f + 1)
                        act.activation(stat[:, 1:2], stat[:, 0:1], ACT.Sqrt, scale=1.0 / D, bias=eps[:, :]).then_inc(rooted, 1)
                    elif name in ("turn", "mem_turn", "turn2"):
                        n = 3 * f + 1 + ("turn", "mem_turn", "turn2").index(name)
                        act.wait_ge(rows_turned, n)
                        act.activation(rows_t[:, :], turned[:, :], ACT.Copy).then_inc(rows_t_ready, 1)
                    elif name == "mem_exp":
                        act.wait_ge(mem_negated, f + 1)
                        for h in range(MEM_HEADS):
                            at = slice(MEM_LEN * h, MEM_LEN * (h + 1))
                            act.activation(rows[:, at], product[0][:, at], ACT.Exp, bias=mem_stat[:, 1, h:h + 1],
                                           accum_out=mem_stat[:, 2, h:h + 1]).then_inc(mem_exped, 1)
                    elif name == "square2":
                        act.wait_ge(h2_ready, f + 1)
                        act.activation(rows[:, :], h_next[:, :], ACT.Square, accum_out=stat2[:, 0:1]).then_inc(squared2, 1)
                        act.wait_ge(squared2, f + 1)
                        act.activation(stat2[:, 1:2], stat2[:, 0:1], ACT.Sqrt, scale=1.0 / D, bias=eps[:, :]).then_inc(rooted2, 1)
                    elif name.startswith("keep_"):
                        g = int(name[-1])
                        act.wait_ge(peer_scored, 4 * f + g + 1)
                        if g == 0:
                            need(act, out_stored, 16 * (f - 1))
                        act.activation(work[:, BANK * g:BANK * (g + 1)],
                                       product[g // 2][:, BANK * (g % 2):BANK * (g % 2 + 1)], ACT.Copy).then_inc(scores_kept, 1)
                    elif name == "gate_exp":
                        act.wait_ge(gate_shifted, f + 1)
                        act.activation(gate_next[:, :, :], gate_next[:, :, :], ACT.Exp).then_inc(gate_exped, 1)

            def end(t, names):
                if "end_root" in names:
                    act.wait_ge(h3_ready, t + 1)
                    act.activation(work[:, D:2 * D], work[:, 0:D], ACT.Square, accum_out=end_stat[:, 0:1]).then_inc(end_squared, 1)
                    act.wait_ge(end_squared, t + 1)
                    act.activation(end_stat[:, 1:2], end_stat[:, 0:1], ACT.Sqrt, scale=1.0 / D, bias=eps[:, :]).then_inc(end_rooted, 1)

            def body(t, more):
                for p, (kind, k) in enumerate(ORDER):
                    if kind == "v":
                        if k % TOPK == 0:
                            h = k // TOPK
                            act.wait_ge(u_used, PICKS * t + TOPK * (h + 1))
                            at = slice(TOPK * h, TOPK * (h + 1))
                            act.activation(active[:, at], dots[:, at], ACT.Gelu).then_inc(activated, 1)
                            act.wait_ge(coeff_ready, PEER_HEADS * t + h + 1)
                        need(act, v_used, PICKS * t + k - DIAGONALS + 1)
                        act.activation(diagonal[:, k % DIAGONALS, :], ident[:, :], ACT.Copy,
                                       scale=coeff[:, k:k + 1]).then_inc(diagonal_ready, 1)
                    pieces(t, more, p, front, end)

            act.wait_ge(eps_set, 1)
            act.wait_ge(small_loaded, 64)
            for_chunks(act, front, body, end)

        @block.vector
        def _(dve):
            STEPS = 5 * PEER_TABLES + 5 * PEER_HEADS + 15
            made = [0]

            def stepped(instruction):
                made[0] += 1
                instruction.then_inc(step, 1)

            def after_steps(f):
                dve.wait_ge(step, STEPS * f + made[0])
                then_plain(dve)

            def top_16(f, values, tops, places):
                for i in range(len(values)):
                    stepped(dve.max(tops[i][:, 0:8], values[i]))
                after_steps(f)
                for i in range(len(values)):
                    stepped(dve.max_index(places[i][:, 0:8], tops[i][:, 0:8], values[i]))
                after_steps(f)
                for i in range(len(values)):
                    stepped(dve.match_replace(values[i], tops[i][:, 0:8], values[i], -3e38))
                after_steps(f)
                for i in range(len(values)):
                    stepped(dve.max(tops[i][:, 8:16], values[i]))
                after_steps(f)
                for i in range(len(values)):
                    stepped(dve.max_index(places[i][:, 8:16], tops[i][:, 8:16], values[i]))

            by_head = lambda a: a.rearrange("p (h k) -> p h k", h=PEER_HEADS)

            def front(f, names):
                for name in names:
                    if name == "norm":
                        dve.wait_ge(rooted, f + 1)
                        dve.reciprocal(stat[:, 2:3], stat[:, 1:2]).then_inc(inverted, 1)
                        dve.wait_ge(inverted, f + 1)
                        dve.tensor_scalar(rows[:, :], h_next[:, :], stat[:, 2:3], None, ALU.mult).then_inc(normed, 1)
                    elif name == "mem_max":
                        dve.wait_ge(mem_scored, f + 1)
                        dve.tensor_reduce(mem_stat[:, 0, :], product[0][:, :].rearrange("p (h m) -> p h m", h=MEM_HEADS),
                                          AX_X, ALU.max).then_inc(mem_maxed, 1)
                        dve.wait_ge(mem_maxed, f + 1)
                        dve.tensor_scalar(mem_stat[:, 1, :], mem_stat[:, 0, :], -1.0, None, ALU.mult).then_inc(mem_negated, 1)
                    elif name == "mem_norm":
                        dve.wait_ge(mem_exped, MEM_HEADS * (f + 1))
                        dve.reciprocal(mem_stat[:, 3, :], mem_stat[:, 2, :]).then_inc(mem_inverted, 1)
                        dve.wait_ge(mem_inverted, f + 1)
                        heads = rows[:, :].rearrange("p (h m) -> p h m", h=MEM_HEADS)
                        dve.tensor_tensor(heads, heads, mem_stat[:, 3, :].unsqueeze(2).to_broadcast([P, MEM_HEADS, MEM_LEN]),
                                          ALU.mult).then_inc(mem_normed, 1)
                    elif name == "h2":
                        dve.wait_ge(mem_out, f + 1)
                        dve.tensor_tensor(h_next[:, :], product[1][:, :], h_next[:, :], ALU.add).then_inc(h2_ready, 1)
                    elif name == "norm2":
                        dve.wait_ge(rooted2, f + 1)
                        dve.reciprocal(stat2[:, 2:3], stat2[:, 1:2]).then_inc(inverted2, 1)
                        dve.wait_ge(inverted2, f + 1)
                        dve.tensor_scalar(rows[:, :], h_next[:, :], stat2[:, 2:3], None, ALU.mult).then_inc(normed2, 1)
                    elif name.startswith("top_"):
                        g = int(name[-1])
                        if g == 0:
                            made[0] = 0
                        dve.wait_ge(scores_kept, 4 * f + g + 1)
                        then_plain(dve)
                        four = range(4 * g, 4 * g + 4)
                        top_16(f, [work[:, PEER_KEYS * i:PEER_KEYS * (i + 1)] for i in four], [top[:, i, :] for i in four],
                               [top_at[:, i, :] for i in four])
                    elif name == "pairs":
                        after_steps(f)
                        halves = top[:, :, :].rearrange("p (h two) k -> p h two k", two=2)
                        stepped(dve.tensor_tensor(
                            work[:, :].rearrange("p (h i j) -> p h i j", h=PEER_HEADS, i=TOPK),
                            halves[:, :, 0, :].unsqueeze(3).to_broadcast([P, PEER_HEADS, TOPK, TOPK]),
                            halves[:, :, 1, :].unsqueeze(2).to_broadcast([P, PEER_HEADS, TOPK, TOPK]), ALU.add))
                        after_steps(f)
                        stepped(dve.tensor_copy(top_at_f[:, :, :], top_at[:, :, :]))
                    elif name.startswith("best_"):
                        g = int(name[-1])
                        after_steps(f)
                        two = range(2 * g, 2 * g + 2)
                        pairs = TOPK * TOPK
                        top_16(f, [work[:, pairs * h:pairs * (h + 1)] for h in two], [best[:, h, :] for h in two],
                               [best_at[:, TOPK * h:TOPK * (h + 1)] for h in two])
                        if g == 3:
                            after_steps(f)
                            dve.tensor_tensor(gate_next[:, :, :], best[:, :, :],
                                              best[:, :, 0:1].to_broadcast([P, PEER_HEADS, TOPK]), ALU.subtract).then_inc(gate_shifted, 1)
                            stepped(dve.tensor_scalar(place[:, 0, :], best_at[:, :], 4, None, ALU.logical_shift_right))
                            stepped(dve.tensor_scalar(place[:, 1, :], best_at[:, :], TOPK - 1, None, ALU.bitwise_and))
                            after_steps(f)
                            stepped(dve.tensor_copy(place_f[:, :, :], place[:, :, :]))
                    elif name in ("pick_a", "pick_b"):
                        half = int(name == "pick_b")
                        after_steps(f)
                        one_hot = work[:, :].rearrange("p (k s) -> p k s", s=TOPK)
                        stepped(dve.tensor_tensor(one_hot, place_f[:, half, :].unsqueeze(2).to_broadcast([P, PICKS, TOPK]),
                                                  slots[:, :].unsqueeze(1).to_broadcast([P, PICKS, TOPK]), ALU.is_equal))
                        after_steps(f)
                        keys = top_at_f[:, :, :].rearrange("p (h two) s -> p h two s", two=2)[:, :, half, :]
                        four_d = work[:, :].rearrange("p (h k s) -> p h k s", h=PEER_HEADS, k=TOPK)
                        stepped(dve.tensor_tensor(four_d, four_d, keys.unsqueeze(2).to_broadcast([P, PEER_HEADS, TOPK, TOPK]),
                                                  ALU.mult))
                        after_steps(f)
                        stepped(dve.tensor_reduce(key_at[:, half, :], one_hot, AX_X, ALU.add))
                    elif name == "live":
                        after_steps(f)
                        dve.scalar_tensor_tensor(expert_u[:, :], key_at[:, 0, :], float(PEER_KEYS), key_at[:, 1, :],
                                                 ALU.mult, ALU.add).then_inc(expert_u_ready, 1)
                        dve.scalar_tensor_tensor(x_ffn[:, :], h_next[:, :], stat2[:, 2:3], gain_ffn[:, :], ALU.mult,
                                                 ALU.mult).then_inc(step, 1)
                        made[0] += 1
                        dve.wait_ge(gate_exped, f + 1)
                        stepped(dve.tensor_reduce(gate_sum[:, 0, :], gate_next[:, :, :], AX_X, ALU.add))
                        after_steps(f)
                        stepped(dve.reciprocal(gate_sum[:, 1, :], gate_sum[:, 0, :]))
                        after_steps(f)
                        stepped(dve.tensor_tensor(gate[:, :, :], gate_next[:, :, :],
                                                  gate_sum[:, 1, :].unsqueeze(2).to_broadcast([P, PEER_HEADS, TOPK]), ALU.mult))
                        after_steps(f)
                        assert made[0] == STEPS, (made[0], STEPS)

            def end(t, names):
                if "end_sum" in names:
                    dve.wait_ge(v_used, PICKS * (t + 1))
                    need(dve, out_stored, 16 * t)
                    dve.tensor_tensor(work[:, 0:D], acc[:, :], h_live[:, :], ALU.add).then_inc(h3_ready, 1)
                    dve.wait_ge(h3_ready, t + 1)
                if "end_out" in names:
                    dve.wait_ge(end_rooted, t + 1)
                    dve.reciprocal(end_stat[:, 2:3], end_stat[:, 1:2]).then_inc(end_inverted, 1)
                    dve.wait_ge(end_inverted, t + 1)
                    dve.scalar_tensor_tensor(work[:, 0:D], work[:, 0:D], end_stat[:, 2:3], gain_final[:, :], ALU.mult,
                                             ALU.mult).then_inc(out_ready, 1)

            def body(t, more):
                for p, (kind, k) in enumerate(ORDER):
                    for h, at in U_END.items():
                        if p == at + 4:
                            dve.wait_ge(activated, PEER_HEADS * t + h + 1)
                            dve.tensor_tensor(coeff[:, TOPK * h:TOPK * (h + 1)], active[:, TOPK * h:TOPK * (h + 1)],
                                              gate[:, h, :], ALU.mult).then_inc(coeff_ready, 1)
                    if kind == "u":
                        dve.wait_ge(gathered[p % RING], 16 * (PIECES * t + p // RING + 1))
                        row = ring[:, p % RING, :]
                        dve.tensor_tensor_reduce(row, row, x_ffn[:, :], 1.0, 0.0, ALU.mult, ALU.add,
                                                 dots[:, k:k + 1]).then_inc(u_used, 1)
                    pieces(t, more, p, front, end)
                    if p == RING - 1:
                        need(dve, v_used, PICKS * t)
                        dve.tensor_copy(expert_v[:, :], expert_u[:, :]).then_inc(expert_v_ready, 1)
                        dve.tensor_copy(h_live[:, :], h_next[:, :]).then_inc(h2_kept, 1)

            dve.memset(eps[:, :], EPS).then_inc(eps_set, 1)
            dve.wait_ge(eps_set, 1)
            dve.wait_ge(small_loaded, 64)
            for_chunks(dve, front, body, end)

        @block.tensor
        def _(pe):
            def multiply(f, to, table, at):
                for k in range(DT):
                    last = pe.matmul(to, rows_t[:, P * k:P * (k + 1)], table[:, k, at:at + BANK], start=(k == 0), stop=(k == DT - 1))
                return last

            def front(f, names):
                for name in names:
                    if name in ("turn", "mem_turn", "turn2"):
                        n = ("turn", "mem_turn", "turn2").index(name)
                        pe.wait_ge((normed, mem_normed, normed2)[n], f + 1)
                        need(pe, rows_t_ready, 3 * f + n)
                        for k in range(DT):
                            last = pe.transpose(turned[:, P * k:P * (k + 1)], rows[:, P * k:P * (k + 1)], ident[:, :])
                        last.then_inc(rows_turned, 1)
                    elif name == "mem_a":
                        pe.wait_ge(rows_t_ready, 3 * f + 1)
                        pe.wait_ge(tables_loaded[0], 16)
                        need(pe, scores_kept, 4 * f)
                        multiply(f, product[0][:, 0:BANK], mem_scores, 0)
                    elif name == "mem_b":
                        multiply(f, product[0][:, BANK:D], mem_scores, BANK).then_inc(mem_scored, 1)
                    elif name == "out_a":
                        pe.wait_ge(rows_t_ready, 3 * f + 2)
                        pe.wait_ge(tables_loaded[1], 16)
                        multiply(f, product[1][:, 0:BANK], mem_values, 0)
                    elif name == "out_b":
                        multiply(f, product[1][:, BANK:D], mem_values, BANK).then_inc(mem_out, 1)
                    elif name.startswith("peer_"):
                        g = int(name[-1])
                        if g == 0:
                            pe.wait_ge(rows_t_ready, 3 * f + 3)
                            pe.wait_ge(tables_loaded[2], 16)
                        multiply(f, product[g // 2][:, BANK * (g % 2):BANK * (g % 2 + 1)], peer_scores,
                                 BANK * g).then_inc(peer_scored, 1)

            def body(t, more):
                for p, (kind, k) in enumerate(ORDER):
                    if kind == "v":
                        if k == 0:
                            need(pe, h3_ready, t)
                        pe.wait_ge(diagonal_ready, PICKS * t + k + 1)
                        pe.wait_ge(gathered[p % RING], 16 * (PIECES * t + p // RING + 1))
                        for c in range(2):
                            last = pe.matmul(acc[:, BANK * c:BANK * (c + 1)], diagonal[:, k % DIAGONALS, :],
                                             ring[:, p % RING, BANK * c:BANK * (c + 1)], start=(k == 0), stop=(k == PICKS - 1))
                        last.then_inc(v_used, 1)
                    pieces(t, more, p, front, lambda t, names: None)

            pe.wait_ge(small_loaded, 64)
            for_chunks(pe, front, body, lambda t, names: None)


def hybrid_layer(nc, io):
    fold_weights(nc, io)
    with ExitStack() as ctx:
        sb, _, _ = allocators(nc, ctx)
        keep = {
            "mla_k_t": sb("mla_k_t", [P, HEADS, SEQ]),
            "dil_k_t": sb("dil_k_t", [P, HEADS // 2, SEQ]),
            "values": sb("values", [P, CHUNKS, 2 * WIDTH]),
        }
        project_tokens(nc, io, keep)
        attend(nc, io, keep)
    attend_memory_and_experts(nc, io)


def kernel(x, mem, norm_mix, w_in, mla_q_norm, mla_kv_norm, mla_w_uq, mla_w_ukv, grp_norm_mla, grp_norm_dil, w_out,
           norm_mem_q, norm_mem_kv, w_mem_q, w_mem_kv, w_mem_o, norm_ffn, peer_w_q, peer_sub_keys, peer_u, peer_v,
           norm_final):
    import concourse.bacc as bacc
    from concourse.bass_utils import run_bass_kernel_spmd

    def columns(*gains):
        return np.ascontiguousarray(np.concatenate([np.asarray(g)[0].reshape(-1, P).T for g in gains], axis=1))

    arrays = {
        "x": np.asarray(x)[0],
        "mem": np.asarray(mem),
        "norm_mix": columns(norm_mix),
        "w_in": np.asarray(w_in)[0],
        "mla_q_norm": columns(mla_q_norm),
        "mla_kv_norm": columns(mla_kv_norm),
        "mla_w_uq": np.asarray(mla_w_uq)[0],
        "mla_w_ukv": np.asarray(mla_w_ukv)[0],
        "grp_norm": columns(grp_norm_mla, grp_norm_dil),
        "w_out": np.asarray(w_out)[0],
        "norm_mem_q": columns(norm_mem_q),
        "norm_mem_kv": columns(norm_mem_kv),
        "w_mem_q": np.asarray(w_mem_q)[0],
        "w_mem_kv": np.asarray(w_mem_kv)[0],
        "w_mem_o": np.asarray(w_mem_o)[0],
        "norm_ffn": columns(norm_ffn),
        "norm_ffn_row": np.asarray(norm_ffn)[0],
        "peer_w_q": np.asarray(peer_w_q)[0],
        "peer_sub_keys": np.asarray(peer_sub_keys)[0].reshape(PEER_TABLES, PEER_KEYS, P),
        "peer_u": np.asarray(peer_u)[0],
        "peer_v": np.asarray(peer_v)[0],
        "norm_final_row": np.asarray(norm_final),
    }
    arrays.update(shape_constants())
    arrays = {name: np.ascontiguousarray(a) for name, a in arrays.items()}

    nc = bacc.Bacc("TRN2", target_bir_lowering=False, num_devices=1)
    io = {name: nc.dram_tensor(name, a.shape, mybir.dt.from_np(a.dtype), kind="ExternalInput").ap()
          for name, a in arrays.items()}
    scratch = {
        "mem_scores": (P, DT, D),
        "mem_values": (P, DT, D),
        "peer_scores": (P, DT, 2 * D),
        "mla_q_t": (CHUNKS, QK, HEADS, P),
        "dil_q_t": (CHUNKS, P, HEADS // 2, P),
        "h1": (CHUNKS, P, D),
    }
    for name, shape in scratch.items():
        io[name] = nc.dram_tensor(name, shape, F32, kind="Internal").ap()
    io["out"] = nc.dram_tensor("out", (CHUNKS, P, D), F32, kind="ExternalOutput").ap()
    hybrid_layer(nc, io)
    result = run_bass_kernel_spmd(nc, [arrays], core_ids=[0])
    return result.results[0]["out"].reshape(1, SEQ, D)
```

```python
from contextlib import ExitStack

import numpy as np

import concourse.bass as bass
from concourse import mybir

F32 = mybir.dt.float32
U32 = mybir.dt.uint32
ALU = mybir.AluOpType
ACT = mybir.ActivationFunctionType
AX_X = mybir.AxisListType.X

P = 128
BANK = 512
D = 1024
DT = D // P
SEQ = 1024
CHUNKS = SEQ // P
EPS = 1e-6
MEM_LEN = 256
MEM_HEADS = 4
MEM_SCALE = (D // MEM_HEADS) ** -0.5
HEADS = 8
NOPE = 64
ROPE = 32
HALF_ROPE = ROPE // 2
QK = NOPE + ROPE
HEAD = 64
Q_RANK = 384
KV_RANK = 256
WIDTH = HEADS * HEAD
IN_COLS = Q_RANK + KV_RANK + ROPE + 3 * WIDTH
PEER_HEADS = 8
PEER_KEYS = 128
PEER_N = PEER_KEYS * PEER_KEYS
PEER_TABLES = 2 * PEER_HEADS
TOPK = 16
PICKS = PEER_HEADS * TOPK
RING = 8
PICK_STEPS = 5 * PEER_TABLES + 5 * PEER_HEADS + 15
FRONT_STEPS = (["square", "norm", "turn"] + [f"mem_{i}_{k}" for i in "ab" for k in range(DT)] +
               ["mem_max", "mem_exp", "mem_norm", "mem_turn"] + [f"out_{i}_{k}" for i in "ab" for k in range(DT)] +
               ["h2", "square2", "norm2", "turn2"] + [f"peer_{g}_{k}" for g in range(4) for k in range(DT)] +
               [f"keep_{g}" for g in range(4)] + [f"top_{g}_{i}" for g in range(4) for i in range(5)] +
               ["pairs", "floats"] + [f"best_{g}_{i}" for g in range(4) for i in range(5)] +
               ["places", "gate_exp"] + [f"pick_{half}_{i}" for half in range(2) for i in range(3)] + ["live"])
DIL_CONFIGS = ((128, 1), (512, 4), (2048, 16))
BIAS_COLS = SEQ + 2 * P
NOWHERE = -1e30


class Picks:
    def __init__(self, x, expert, gate, h=None, h_next=None, stat2=None):
        self.x = x
        self.expert, self.gate = expert, gate
        self.h = h
        self.h_next, self.stat2 = h_next, stat2


class PickBuffers:
    pass


def allocators(nc, ctx, stage=""):
    def sb(name, shape, dt=F32):
        return ctx.enter_context(nc.sbuf_tensor(name + stage, shape, dt))

    def ps(name, shape):
        return ctx.enter_context(nc.psum_tensor(name + stage, shape, F32))

    def sem(name):
        semaphores.append(nc.alloc_semaphore(name + stage))
        return semaphores[-1]

    def clear():
        if semaphores:
            nc.clear_and_free_semaphores(semaphores)
            nc.all_engine_barrier()

    semaphores = []
    ctx.callback(clear)
    return sb, ps, sem



def shape_constants():
    inv = 1.0 / (np.float32(10000.0) ** (np.arange(0, ROPE, 2, dtype=np.float32) / np.float32(ROPE)))
    angle = np.arange(SEQ, dtype=np.float32)[:, None] * inv.astype(np.float32)[None, :]
    cos, sin = np.cos(angle), np.sin(angle)

    def by_chunk(a):
        return np.ascontiguousarray(a.reshape(CHUNKS, P, ROPE).transpose(1, 0, 2), dtype=np.float32)

    distance = (np.arange(P)[:, None] + (SEQ - P) - np.arange(BIAS_COLS)[None, :]).astype(np.float64)
    count = np.zeros_like(distance)
    for window, dilation in DIL_CONFIGS:
        count += (distance >= 0) & (distance <= window) & (distance % dilation == 0)
    bias = np.full((1 + HEADS, P, BIAS_COLS), NOWHERE, dtype=np.float32)
    bias[0][distance >= 0] = 0.0
    seen = count > 0
    for h in range(HEADS):
        slope = 2.0 ** (-8.0 * (h + 1) / HEADS)
        bias[1 + h][seen] = (np.log(count[seen]) - slope * distance[seen]) * HEAD ** 0.5
    return {
        "identity": np.eye(P, dtype=np.float32),
        "cos2": by_chunk(np.concatenate([cos, cos], axis=1)),
        "sin2": by_chunk(np.concatenate([-sin, sin], axis=1)),
        "score_bias": bias,
        "slots": np.tile(np.arange(TOPK, dtype=np.float32), (P, 1)),
    }


def fold_weights(nc, io):
    with ExitStack() as ctx:
        sb, ps, sem = allocators(nc, ctx)
        ident = sb("f_ident", [P, P])
        mem_rows = sb("f_mem_rows", [P, 2, D])
        mem_scaled = sb("f_mem_scaled", [P, 2, D])
        mem_sumsq = sb("f_mem_sumsq", [P, 2])
        mem_rms = sb("f_mem_rms", [P, 2])
        mem_rstd = sb("f_mem_rstd", [P, 2])
        eps = sb("f_eps", [P, 1])
        gain_kv = sb("f_gain_kv", [P, DT])
        gain_q = sb("f_gain_q", [P, DT])
        gain_ffn = sb("f_gain_ffn", [P, DT])
        mem_t = sb("f_mem_t", [P, DT, MEM_LEN])
        w_big = sb("f_w_big", [P, DT, 2 * D])
        w_o = sb("f_w_o", [P, DT, D])
        w_q = sb("f_w_q", [P, DT, D])
        k_t = sb("f_k_t", [P, DT, MEM_LEN])
        v_t = sb("f_v_t", [P, DT, MEM_LEN])
        turned = sb("f_turned", [P, 4, D])
        keys = mem_rows[:, :, :].rearrange("p t (i n) -> p (t i) n", n=PEER_KEYS)
        keys_t = mem_scaled[:, :, :].rearrange("p t (i n) -> p (t i) n", n=PEER_KEYS)
        stage_v = sb("f_stage_v", [P, 2, D])
        stage_s = sb("f_stage_s", [P, 2, D])
        pair = [ps(f"f_pair{i}", [P, D]) for i in range(4)]

        mem_loaded = sem("f_mem_loaded")
        small_loaded = sem("f_small_loaded")
        kv_loaded = [sem(f"f_kv_loaded{i}") for i in range(4)]
        o_loaded = sem("f_o_loaded")
        q_loaded = sem("f_q_loaded")
        keys_loaded = sem("f_keys_loaded")
        peer_loaded = sem("f_peer_loaded")
        eps_set = sem("f_eps_set")
        mem_squared = sem("f_mem_squared")
        mem_rooted = sem("f_mem_rooted")
        mem_inverted = sem("f_mem_inverted")
        mem_normed = sem("f_mem_normed")
        pair_filled = sem("f_pair_filled")
        act_emptied = sem("f_act_emptied")
        dve_emptied = sem("f_dve_emptied")
        stored_v = [sem(f"f_stored_v{i}") for i in range(2)]
        stored_s = [sem(f"f_stored_s{i}") for i in range(2)]

        tasks = [("mem_t", 0), ("mem_t", 1), ("k_t", 0), ("k_t", 1), ("v_t", 0), ("v_t", 1)]
        tasks += [("mem_values", kt) for kt in range(DT)]
        tasks += [("turn_q", 0), ("turn_q", 1)]
        for h in range(MEM_HEADS):
            if h + 1 < MEM_HEADS:
                tasks += [("turn_q", 2 * h + 2), ("turn_q", 2 * h + 3)]
            tasks += [("mem_scores", 2 * h), ("mem_scores", 2 * h + 1)]
        tasks += [("turn_keys", 0), ("turn_keys", 1), ("turn_peer", 0)]
        for i in range(PEER_TABLES):
            if i + 1 < PEER_TABLES:
                tasks += [("turn_peer", i + 1)]
            tasks += [("peer_scores", i)]
        by_dve = {"mem_t", "mem_scores", "peer_scores", "turn_keys"}
        emptied_at = {}
        counts = {True: 0, False: 0}
        for task in tasks:
            counts[task[0] in by_dve] += 1
            emptied_at[task] = (dve_emptied if task[0] in by_dve else act_emptied, counts[task[0] in by_dve])
        number = {task: n for n, task in enumerate(tasks)}

        def wait_emptied(eng, kind, i):
            eng.wait_ge(*emptied_at[(kind, i)])

        block = ctx.enter_context(nc.Block())

        @block.sync
        def _(sp):
            sp.dma_start(mem_rows[:, :, :], io["mem"].rearrange("b (t p) d -> p (b t) d", p=P)).then_inc(mem_loaded, 16)
            sp.dma_start(ident[:, :], io["identity"]).then_inc(small_loaded, 16)
            sp.dma_start(gain_kv[:, :], io["norm_mem_kv"]).then_inc(small_loaded, 16)
            sp.dma_start(gain_q[:, :], io["norm_mem_q"]).then_inc(small_loaded, 16)
            sp.dma_start(gain_ffn[:, :], io["norm_ffn"]).then_inc(small_loaded, 16)
            kv_weights = io["w_mem_kv"].rearrange("(t p) n -> p t n", p=P)
            for i in range(4):
                at = slice(BANK * i, BANK * (i + 1))
                sp.dma_start(w_big[:, :, at], kv_weights[:, :, at]).then_inc(kv_loaded[i], 16)
            sp.dma_start(w_o[:, :, :], io["w_mem_o"].rearrange("(t p) n -> p t n", p=P)).then_inc(o_loaded, 16)
            sp.dma_start(w_q[:, :, :], io["w_mem_q"].rearrange("(t p) n -> p t n", p=P)).then_inc(q_loaded, 16)
            sp.wait_ge(pair_filled, number[("mem_t", 1)] + 1)
            sp.dma_start(keys, io["peer_sub_keys"].rearrange("i n d -> n i d")).then_inc(keys_loaded, 16)
            sp.wait_ge(pair_filled, number[("v_t", 1)] + 1)
            sp.dma_start(w_big[:, :, :], io["peer_w_q"].rearrange("(t p) n -> p t n", p=P)).then_inc(peer_loaded, 16)
            for kt in range(DT):
                wait_emptied(sp, "mem_values", kt)
                sp.dma_start(io["mem_values"][:, kt, :], stage_v[:, kt % 2, :]).then_inc(stored_v[kt % 2], 16)
            for n in range(DT):
                wait_emptied(sp, "mem_scores", n)
                h, half = divmod(n, 2)
                sp.dma_start(io["mem_scores"][:, 4 * half:4 * half + 4, MEM_LEN * h:MEM_LEN * (h + 1)],
                             stage_s[:, n % 2, :].rearrange("p (t m) -> p t m", t=4)).then_inc(stored_s[n % 2], 16)
            for i in range(PEER_TABLES):
                wait_emptied(sp, "peer_scores", i)
                sp.dma_start(io["peer_scores"][:, :, P * i:P * (i + 1)],
                             stage_s[:, i % 2, :].rearrange("p (t m) -> p t m", t=DT)).then_inc(stored_s[i % 2], 16)
            for i in range(2):
                sp.wait_ge(stored_v[i], 16 * DT // 2)
                sp.wait_ge(stored_s[i], 16 * (DT + PEER_TABLES) // 2)

        @block.scalar
        def _(act):
            act.wait_ge(mem_loaded, 16)
            for t in range(2):
                act.activation(mem_scaled[:, t, :], mem_rows[:, t, :], ACT.Square,
                               accum_out=mem_sumsq[:, t:t + 1]).then_inc(mem_squared, 1)
            act.wait_ge(mem_squared, 2)
            act.wait_ge(eps_set, 1)
            act.activation(mem_rms[:, :], mem_sumsq[:, :], ACT.Sqrt, scale=1.0 / D, bias=eps[:, :]).then_inc(mem_rooted, 1)
            for n, (kind, i) in enumerate(tasks):
                if kind in by_dve:
                    continue
                act.wait_ge(pair_filled, n + 1)
                full = pair[n % 4]
                if kind == "k_t":
                    act.activation(k_t[:, 4 * i:4 * i + 4, :].rearrange("p t m -> p (t m)"), full[:, :], ACT.Copy,
                                   scale=MEM_SCALE).then_inc(act_emptied, 1)
                elif kind == "v_t":
                    act.activation(v_t[:, 4 * i:4 * i + 4, :].rearrange("p t m -> p (t m)"), full[:, :],
                                   ACT.Copy).then_inc(act_emptied, 1)
                elif kind == "mem_values":
                    if i >= 2:
                        act.wait_ge(stored_v[i % 2], 16 * (i // 2))
                    act.activation(stage_v[:, i % 2, :], full[:, :], ACT.Copy).then_inc(act_emptied, 1)
                elif kind == "turn_q":
                    if i >= 4:
                        act.wait_ge(pair_filled, number[("mem_scores", 2 * (i // 2 - 2) + 1)] + 1)
                    act.activation(turned[:, i % 4, :], full[:, :], ACT.Copy).then_inc(act_emptied, 1)
                elif kind == "turn_peer":
                    before = ("mem_scores", 2 * MEM_HEADS - 1) if i < 4 else ("peer_scores", i - 4)
                    act.wait_ge(pair_filled, number[before] + 1)
                    act.activation(turned[:, i % 4, :], full[:, :], ACT.Copy).then_inc(act_emptied, 1)

        @block.vector
        def _(dve):
            dve.memset(eps[:, :], EPS).then_inc(eps_set, 1)
            dve.wait_ge(mem_rooted, 1)
            dve.reciprocal(mem_rstd[:, :], mem_rms[:, :]).then_inc(mem_inverted, 1)
            dve.wait_ge(mem_inverted, 1)
            for t in range(2):
                dve.tensor_scalar(mem_scaled[:, t, :], mem_rows[:, t, :], mem_rstd[:, t:t + 1], None,
                                  ALU.mult).then_inc(mem_normed, 1)
            dve.wait_ge(small_loaded, 64)
            stored = 0
            for n, (kind, i) in enumerate(tasks):
                if kind not in by_dve:
                    continue
                dve.wait_ge(pair_filled, n + 1)
                full = pair[n % 4]
                if kind == "mem_t":
                    dve.tensor_tensor(mem_t[:, :, P * i:P * (i + 1)], full[:, :].rearrange("p (t m) -> p t m", t=DT),
                                      gain_kv[:, :].unsqueeze(2).to_broadcast([P, DT, P]), ALU.mult).then_inc(dve_emptied, 1)
                elif kind == "mem_scores":
                    if i >= 2:
                        dve.wait_ge(stored_s[i % 2], 16 * (i // 2))
                    half = i % 2
                    dve.tensor_tensor(stage_s[:, i % 2, :].rearrange("p (t m) -> p t m", t=4),
                                      full[:, :].rearrange("p (t m) -> p t m", t=4),
                                      gain_q[:, 4 * half:4 * half + 4].unsqueeze(2).to_broadcast([P, 4, MEM_LEN]),
                                      ALU.mult).then_inc(dve_emptied, 1)
                elif kind == "turn_keys":
                    dve.tensor_copy(keys_t[:, 8 * i:8 * i + 8, :].rearrange("p i n -> p (i n)"),
                                    full[:, :]).then_inc(dve_emptied, 1)
                elif kind == "peer_scores":
                    dve.wait_ge(stored_s[i % 2], 16 * ((DT + i) // 2))
                    dve.tensor_tensor(stage_s[:, i % 2, :].rearrange("p (t m) -> p t m", t=DT),
                                      full[:, :].rearrange("p (t m) -> p t m", t=DT),
                                      gain_ffn[:, :].unsqueeze(2).to_broadcast([P, DT, P]),
                                      ALU.mult).then_inc(dve_emptied, 1)

        @block.tensor
        def _(pe):
            pe.wait_ge(small_loaded, 64)
            for n, (kind, i) in enumerate(tasks):
                to = pair[n % 4]
                if n >= 4:
                    pe.wait_ge(*emptied_at[tasks[n - 4]])
                if kind == "mem_t":
                    pe.wait_ge(mem_normed, 2)
                    for t in range(DT):
                        last = pe.transpose(to[:, P * t:P * (t + 1)], mem_scaled[:, i, P * t:P * (t + 1)], ident[:, :])
                elif kind in ("k_t", "v_t"):
                    pe.wait_ge(kv_loaded[2 * (kind == "v_t") + i], 16)
                    wait_emptied(pe, "mem_t", 0)
                    wait_emptied(pe, "mem_t", 1)
                    at = (D if kind == "v_t" else 0) + 4 * P * i
                    for j in range(4):
                        for t in range(DT):
                            last = pe.matmul(to[:, MEM_LEN * j:MEM_LEN * (j + 1)], w_big[:, t, at + P * j:at + P * (j + 1)],
                                             mem_t[:, t, :], start=(t == 0), stop=(t == DT - 1))
                elif kind == "mem_values":
                    pe.wait_ge(o_loaded, 16)
                    h, m = divmod(i, 2)
                    wait_emptied(pe, "v_t", 0)
                    wait_emptied(pe, "v_t", 1)
                    for c in range(2):
                        for j in range(2):
                            last = pe.matmul(to[:, BANK * c:BANK * (c + 1)], v_t[:, 2 * h + j, P * m:P * (m + 1)],
                                             w_o[:, 2 * h + j, BANK * c:BANK * (c + 1)], start=(j == 0), stop=(j == 1))
                elif kind == "turn_q":
                    pe.wait_ge(q_loaded, 16)
                    for t in range(DT):
                        last = pe.transpose(to[:, P * t:P * (t + 1)], w_q[:, t, P * i:P * (i + 1)], ident[:, :])
                elif kind == "mem_scores":
                    h, half = divmod(i, 2)
                    wait_emptied(pe, "k_t", 1)
                    for j in range(2):
                        wait_emptied(pe, "turn_q", 2 * h + j)
                    for t in range(4):
                        for j in range(2):
                            at = P * (4 * half + t)
                            last = pe.matmul(to[:, MEM_LEN * t:MEM_LEN * (t + 1)], turned[:, (2 * h + j) % 4, at:at + P],
                                             k_t[:, 2 * h + j, :], start=(j == 0), stop=(j == 1))
                elif kind == "turn_keys":
                    pe.wait_ge(keys_loaded, 16)
                    for j in range(8):
                        last = pe.transpose(to[:, P * j:P * (j + 1)], keys[:, 8 * i + j, :], ident[:, :])
                elif kind == "turn_peer":
                    pe.wait_ge(peer_loaded, 16)
                    for t in range(DT):
                        last = pe.transpose(to[:, P * t:P * (t + 1)], w_big[:, t, P * i:P * (i + 1)], ident[:, :])
                elif kind == "peer_scores":
                    wait_emptied(pe, "turn_keys", 1)
                    wait_emptied(pe, "turn_peer", i)
                    for t in range(DT):
                        last = pe.matmul(to[:, P * t:P * (t + 1)], turned[:, i % 4, P * t:P * (t + 1)],
                                         keys_t[:, i, :], start=True, stop=True)
                last.then_inc(pair_filled, 1)


def project_tokens(nc, io, keep):
    with ExitStack() as ctx:
        sb, ps, sem = allocators(nc, ctx)
        Q_TILES, KV_TILES = Q_RANK // P, KV_RANK // P
        C_TILES = Q_TILES + KV_TILES
        C_COLS = Q_RANK + KV_RANK
        QH = HEADS * QK // 2

        ident = sb("p_ident", [P, P])
        w_in = sb("p_w_in", [P, DT, IN_COLS])
        w_uq = sb("p_w_uq", [P, Q_TILES, HEADS * QK])
        w_ukv = sb("p_w_ukv", [P, KV_TILES, HEADS * (NOPE + HEAD)])
        gain_x = sb("p_gain_x", [P, DT])
        gain_c = sb("p_gain_c", [P, C_TILES])
        cos2 = sb("p_cos2", [P, CHUNKS, ROPE])
        sin2 = sb("p_sin2", [P, CHUNKS, ROPE])
        eps = sb("p_eps", [P, 1])
        x_rows = sb("p_x_rows", [P, D])
        x_scaled = sb("p_x_scaled", [P, D])
        x_t = sb("p_x_t", [P, D])
        x_stat = sb("p_x_stat", [P, 3])
        c_scaled = sb("p_c_scaled", [P, C_COLS])
        c_t = sb("p_c_t", [P, C_COLS])
        c_stat = sb("p_c_stat", [P, 6])
        dqk = sb("p_dqk", [P, 2 * WIDTH])
        q_rows = sb("p_q_rows", [P, HEADS, QK])
        k_rows = sb("p_k_rows", [P, HEADS, QK])
        q_rope_a = sb("p_q_rope_a", [P, HEADS, ROPE])
        q_rope_b = sb("p_q_rope_b", [P, HEADS, ROPE])
        k_rope_a = sb("p_k_rope_a", [P, ROPE])
        k_rope_b = sb("p_k_rope_b", [P, ROPE])
        q_out = sb("p_q_out", [QK, HEADS, P])
        dq_out = sb("p_dq_out", [P, HEADS // 2, P])
        turn_x = ps("p_turn_x", [P, D])
        pair_b = ps("p_pair_b", [P, D])
        pair_c = ps("p_pair_c", [P, D])
        pair_d = ps("p_pair_d", [P, D])

        weight_loaded = [sem(f"p_weight_loaded{i}") for i in range(DT + 2)]
        small_loaded = sem("p_small_loaded")
        weight_gained = sem("p_weight_gained")
        eps_set = sem("p_eps_set")
        x_loaded = sem("p_x_loaded")
        x_squared, x_rooted, x_inverted = sem("p_x_squared"), sem("p_x_rooted"), sem("p_x_inverted")
        x_normed, x_turned, x_t_ready = sem("p_x_normed"), sem("p_x_turned"), sem("p_x_t_ready")
        c_projected, d_projected, v_projected = sem("p_c_projected"), sem("p_d_projected"), sem("p_v_projected")
        c_squared, c_rooted, c_inverted = sem("p_c_squared"), sem("p_c_rooted"), sem("p_c_inverted")
        c_normed, c_turned, c_t_ready = sem("p_c_normed"), sem("p_c_turned"), sem("p_c_t_ready")
        dqk_ready, d_turned, dq_t_ready, dk_t_ready = (sem("p_dqk_ready"), sem("p_d_turned"), sem("p_dq_t_ready"),
                                                       sem("p_dk_t_ready"))
        q_projected, kv_projected = sem("p_q_projected"), sem("p_kv_projected")
        q_rows_ready, k_nope_ready = sem("p_q_rows_ready"), sem("p_k_nope_ready")
        q_rope_parts, q_rope_ready = sem("p_q_rope_parts"), sem("p_q_rope_ready")
        k_rope_parts, k_rope_ready = sem("p_k_rope_parts"), sem("p_k_rope_ready")
        q_turned, q_t_ready, k_turned, k_t_ready = (sem("p_q_turned"), sem("p_q_t_ready"), sem("p_k_turned"),
                                                    sem("p_k_t_ready"))
        v_ready, dv_ready = sem("p_v_ready"), sem("p_dv_ready")
        q_stored, dq_stored = sem("p_q_stored"), sem("p_dq_stored")
        block = ctx.enter_context(nc.Block())

        @block.sync
        def _(sp):
            sp.dma_start(x_rows[:, :], io["x"][0:P, :]).then_inc(x_loaded, 16)
            sp.dma_start(ident[:, :], io["identity"]).then_inc(small_loaded, 16)
            sp.dma_start(gain_x[:, :], io["norm_mix"]).then_inc(small_loaded, 16)
            sp.dma_start(gain_c[:, 0:Q_TILES], io["mla_q_norm"]).then_inc(small_loaded, 16)
            sp.dma_start(gain_c[:, Q_TILES:C_TILES], io["mla_kv_norm"]).then_inc(small_loaded, 16)
            sp.dma_start(cos2[:, :, :], io["cos2"]).then_inc(small_loaded, 16)
            sp.dma_start(sin2[:, :, :], io["sin2"]).then_inc(small_loaded, 16)
            for t in range(DT):
                sp.dma_start(w_in[:, t, :], io["w_in"][P * t:P * (t + 1), :]).then_inc(weight_loaded[t], 16)
            sp.dma_start(w_uq[:, :, :], io["mla_w_uq"].rearrange("(t p) n -> p t n", p=P)).then_inc(weight_loaded[DT], 16)
            sp.dma_start(w_ukv[:, :, :], io["mla_w_ukv"].rearrange("(t p) n -> p t n", p=P)).then_inc(weight_loaded[DT + 1], 16)

            def store_queries(t):
                sp.wait_ge(dq_t_ready, t + 1)
                sp.dma_start(io["dil_q_t"][bass.ds(t, 1)].rearrange("a p h q -> (a p) h q"), dq_out[:, :, :]).then_inc(dq_stored, 16)
                sp.wait_ge(q_t_ready, t + 1)
                sp.dma_start(io["mla_q_t"][bass.ds(t, 1)].rearrange("a p h q -> (a p) h q"), q_out[:, :, :]).then_inc(q_stored, 16)

            with sp.Fori(0, CHUNKS - 1) as t:
                sp.wait_ge(x_normed, t + 1)
                sp.dma_start(x_rows[:, :], io["x"][bass.ds((t + 1) * P, P), :]).then_inc(x_loaded, 16)
                store_queries(t)
            store_queries(CHUNKS - 1)
            sp.wait_ge(dq_stored, 16 * CHUNKS)
            sp.wait_ge(q_stored, 16 * CHUNKS)

        @block.scalar
        def _(act):
            def square_x(t):
                act.wait_ge(x_loaded, 16 * (t + 1))
                act.activation(x_scaled[:, :], x_rows[:, :], ACT.Square, accum_out=x_stat[:, 0:1]).then_inc(x_squared, 1)
                act.wait_ge(x_squared, t + 1)
                act.activation(x_stat[:, 1:2], x_stat[:, 0:1], ACT.Sqrt, scale=1.0 / D, bias=eps[:, :]).then_inc(x_rooted, 1)

            def keep_x_t(t):
                act.wait_ge(x_turned, t + 1)
                act.activation(x_t[:, :], turn_x[:, :], ACT.Copy).then_inc(x_t_ready, 1)

            def chunk(t, more):
                act.wait_ge(c_projected, t + 1)
                act.activation(c_scaled[:, 0:Q_RANK], pair_b[:, 0:Q_RANK], ACT.Square,
                               accum_out=c_stat[:, 0:1]).then_inc(c_squared, 1)
                act.activation(c_scaled[:, Q_RANK:C_COLS], pair_b[:, BANK:BANK + KV_RANK], ACT.Square,
                               accum_out=c_stat[:, 1:2]).then_inc(c_squared, 1)
                act.wait_ge(c_squared, 2 * t + 2)
                act.activation(c_stat[:, 2:3], c_stat[:, 0:1], ACT.Sqrt, scale=1.0 / Q_RANK, bias=eps[:, :]).then_inc(c_rooted, 1)
                act.activation(c_stat[:, 3:4], c_stat[:, 1:2], ACT.Sqrt, scale=1.0 / KV_RANK, bias=eps[:, :]).then_inc(c_rooted, 1)
                act.wait_ge(d_projected, t + 1)
                act.activation(dqk[:, :], pair_c[:, :], ACT.Copy).then_inc(dqk_ready, 1)
                if more:
                    square_x(t + 1)
                    keep_x_t(t + 1)
                act.wait_ge(d_turned, t + 1)
                act.activation(dq_out[:, :, :].rearrange("p h q -> p (h q)"), pair_d[:, 0:BANK], ACT.Copy).then_inc(dq_t_ready, 1)
                act.wait_ge(q_projected, t + 1)
                act.activation(q_rows[:, :, :].rearrange("p (b h) c -> p b (h c)", b=2),
                               pair_c[:, :].rearrange("p (b w) -> p b w", b=2)[:, :, 0:QH], ACT.Copy).then_inc(q_rows_ready, 1)
                act.wait_ge(kv_projected, t + 1)
                act.activation(k_rows[:, :, 0:NOPE], pair_b[:, :].rearrange("p (h c) -> p h c", h=HEADS)[:, :, 0:NOPE],
                               ACT.Copy).then_inc(k_nope_ready, 1)
                act.wait_ge(q_turned, t + 1)
                act.activation(q_out[:, :, :].rearrange("p h q -> p (h q)"), pair_d[0:QK, :], ACT.Copy).then_inc(q_t_ready, 1)
                act.wait_ge(dq_stored, 16 * (t + 1))
                act.wait_ge(q_stored, 16 * (t + 1))

            act.wait_ge(eps_set, 1)
            square_x(0)
            keep_x_t(0)
            with act.Fori(0, CHUNKS - 1) as t:
                chunk(t, True)
            chunk(CHUNKS - 1, False)

        @block.vector
        def _(dve):
            dve.memset(eps[:, :], EPS).then_inc(eps_set, 1)

            def norm_x(t):
                dve.wait_ge(x_rooted, t + 1)
                dve.reciprocal(x_stat[:, 2:3], x_stat[:, 1:2]).then_inc(x_inverted, 1)
                dve.wait_ge(x_inverted, t + 1)
                dve.tensor_scalar(x_scaled[:, :], x_rows[:, :], x_stat[:, 2:3], None, ALU.mult).then_inc(x_normed, 1)

            def chunk(t, more):
                cos = cos2[:, bass.ds(t, 1), :]
                sin = sin2[:, bass.ds(t, 1), :]
                dve.wait_ge(c_rooted, 2 * t + 2)
                dve.reciprocal(c_stat[:, 4:6], c_stat[:, 2:4]).then_inc(c_inverted, 1)
                dve.wait_ge(c_inverted, t + 1)
                dve.tensor_scalar(c_scaled[:, 0:Q_RANK], pair_b[:, 0:Q_RANK], c_stat[:, 4:5], None, ALU.mult).then_inc(c_normed, 1)
                dve.tensor_scalar(c_scaled[:, Q_RANK:C_COLS], pair_b[:, BANK:BANK + KV_RANK], c_stat[:, 5:6], None,
                                  ALU.mult).then_inc(c_normed, 1)
                at = BANK + KV_RANK
                dve.tensor_tensor(k_rope_a[:, :].unsqueeze(1), pair_b[:, at:at + ROPE].unsqueeze(1), cos, ALU.mult).then_inc(k_rope_parts, 1)
                dve.tensor_tensor(k_rope_b[:, 0:HALF_ROPE].unsqueeze(1), pair_b[:, at + HALF_ROPE:at + ROPE].unsqueeze(1),
                                  sin[:, :, 0:HALF_ROPE], ALU.mult).then_inc(k_rope_parts, 1)
                dve.tensor_tensor(k_rope_b[:, HALF_ROPE:ROPE].unsqueeze(1), pair_b[:, at:at + HALF_ROPE].unsqueeze(1),
                                  sin[:, :, HALF_ROPE:ROPE], ALU.mult).then_inc(k_rope_parts, 1)
                dve.wait_ge(k_rope_parts, 3 * t + 3)
                dve.tensor_tensor(k_rows[:, :, NOPE:QK], k_rope_a[:, :].unsqueeze(1).to_broadcast([P, HEADS, ROPE]),
                                  k_rope_b[:, :].unsqueeze(1).to_broadcast([P, HEADS, ROPE]), ALU.add).then_inc(k_rope_ready, 1)
                dve.wait_ge(v_projected, t + 1)
                dve.tensor_copy(keep["values"][:, bass.ds(t, 1), WIDTH:2 * WIDTH], pair_d[:, 0:BANK].unsqueeze(1)).then_inc(dv_ready, 1)
                if more:
                    norm_x(t + 1)
                dve.wait_ge(c_turned, t + 1)
                dve.tensor_copy(c_t[:, :], pair_b[:, 0:C_COLS]).then_inc(c_t_ready, 1)
                dve.wait_ge(d_turned, t + 1)
                dve.tensor_copy(keep["dil_k_t"][:, :, bass.ds(t * P, P)],
                                pair_d[:, BANK:2 * BANK].rearrange("p (h q) -> p h q", q=P)).then_inc(dk_t_ready, 1)
                dve.wait_ge(q_rows_ready, t + 1)
                over_heads = lambda a, n: a.to_broadcast([P, HEADS, n])
                dve.tensor_tensor(q_rope_a[:, :, :], q_rows[:, :, NOPE:QK], over_heads(cos, ROPE), ALU.mult).then_inc(q_rope_parts, 1)
                dve.tensor_tensor(q_rope_b[:, :, 0:HALF_ROPE], q_rows[:, :, NOPE + HALF_ROPE:QK],
                                  over_heads(sin[:, :, 0:HALF_ROPE], HALF_ROPE), ALU.mult).then_inc(q_rope_parts, 1)
                dve.tensor_tensor(q_rope_b[:, :, HALF_ROPE:ROPE], q_rows[:, :, NOPE:NOPE + HALF_ROPE],
                                  over_heads(sin[:, :, HALF_ROPE:ROPE], HALF_ROPE), ALU.mult).then_inc(q_rope_parts, 1)
                dve.wait_ge(q_rope_parts, 3 * t + 3)
                dve.tensor_tensor(q_rows[:, :, NOPE:QK], q_rope_a[:, :, :], q_rope_b[:, :, :], ALU.add).then_inc(q_rope_ready, 1)
                dve.wait_ge(k_nope_ready, t + 1)
                dve.tensor_copy(keep["values"][:, bass.ds(t, 1), 0:WIDTH].rearrange("p a (h c) -> p (a h) c", h=HEADS),
                                pair_b[:, :].rearrange("p (h c) -> p h c", h=HEADS)[:, :, NOPE:NOPE + HEAD]).then_inc(v_ready, 1)
                dve.wait_ge(k_turned, t + 1)
                dve.tensor_copy(keep["mla_k_t"][0:QK, :, bass.ds(t * P, P)],
                                pair_c[0:QK, :].rearrange("p (h q) -> p h q", q=P)).then_inc(k_t_ready, 1)

            dve.wait_ge(small_loaded, 96)
            norm_x(0)
            for t in range(DT):
                dve.wait_ge(weight_loaded[t], 16)
                dve.tensor_scalar(w_in[:, t, :], w_in[:, t, :], gain_x[:, t:t + 1], None, ALU.mult).then_inc(weight_gained, 1)
            dve.wait_ge(weight_loaded[DT], 16)
            for t in range(Q_TILES):
                dve.tensor_scalar(w_uq[:, t, :], w_uq[:, t, :], gain_c[:, t:t + 1], None, ALU.mult).then_inc(weight_gained, 1)
            dve.wait_ge(weight_loaded[DT + 1], 16)
            for t in range(KV_TILES):
                dve.tensor_scalar(w_ukv[:, t, :], w_ukv[:, t, :], gain_c[:, Q_TILES + t:Q_TILES + t + 1], None,
                                  ALU.mult).then_inc(weight_gained, 1)
            with dve.Fori(0, CHUNKS - 1) as t:
                chunk(t, True)
            chunk(CHUNKS - 1, False)

        @block.tensor
        def _(pe):
            def turn_x_rows(t):
                pe.wait_ge(x_normed, t + 1)
                for k in range(DT):
                    last = pe.transpose(turn_x[:, P * k:P * (k + 1)], x_scaled[:, P * k:P * (k + 1)], ident[:, :])
                last.then_inc(x_turned, 1)

            def project(to, at, width):
                for k in range(DT):
                    last = pe.matmul(to, x_t[:, P * k:P * (k + 1)], w_in[:, k, at:at + width], start=(k == 0), stop=(k == DT - 1))
                return last

            def chunk(t, more):
                pe.wait_ge(x_t_ready, t + 1)
                project(pair_b[:, 0:Q_RANK], 0, Q_RANK)
                project(pair_b[:, BANK:BANK + KV_RANK + ROPE], Q_RANK, KV_RANK + ROPE).then_inc(c_projected, 1)
                at = C_COLS + ROPE
                project(pair_c[:, 0:BANK], at, WIDTH)
                project(pair_c[:, BANK:2 * BANK], at + WIDTH, WIDTH).then_inc(d_projected, 1)
                project(pair_d[:, 0:BANK], at + 2 * WIDTH, WIDTH).then_inc(v_projected, 1)
                if more:
                    turn_x_rows(t + 1)
                pe.wait_ge(dqk_ready, t + 1)
                pe.wait_ge(dv_ready, t + 1)
                for k in range(DT):
                    last = pe.transpose(pair_d[:, P * k:P * (k + 1)], dqk[:, P * k:P * (k + 1)], ident[:, :])
                last.then_inc(d_turned, 1)
                pe.wait_ge(c_normed, 2 * t + 2)
                pe.wait_ge(k_rope_parts, 3 * t + 3)
                for k in range(C_TILES):
                    last = pe.transpose(pair_b[:, P * k:P * (k + 1)], c_scaled[:, P * k:P * (k + 1)], ident[:, :])
                last.then_inc(c_turned, 1)
                pe.wait_ge(c_t_ready, t + 1)
                for b in range(2):
                    for k in range(Q_TILES):
                        last = pe.matmul(pair_c[:, BANK * b:BANK * b + QH], c_t[:, P * k:P * (k + 1)],
                                         w_uq[:, k, QH * b:QH * (b + 1)], start=(k == 0), stop=(k == Q_TILES - 1))
                last.then_inc(q_projected, 1)
                for b in range(2):
                    for k in range(KV_TILES):
                        at = P * (Q_TILES + k)
                        last = pe.matmul(pair_b[:, BANK * b:BANK * (b + 1)], c_t[:, at:at + P],
                                         w_ukv[:, k, BANK * b:BANK * (b + 1)], start=(k == 0), stop=(k == KV_TILES - 1))
                last.then_inc(kv_projected, 1)
                pe.wait_ge(dq_t_ready, t + 1)
                pe.wait_ge(dk_t_ready, t + 1)
                pe.wait_ge(q_rope_ready, t + 1)
                for h in range(HEADS):
                    last = pe.transpose(pair_d[0:QK, P * h:P * (h + 1)], q_rows[:, h, :], ident[:, :])
                last.then_inc(q_turned, 1)
                pe.wait_ge(k_nope_ready, t + 1)
                pe.wait_ge(k_rope_ready, t + 1)
                for h in range(HEADS):
                    last = pe.transpose(pair_c[0:QK, P * h:P * (h + 1)], k_rows[:, h, :], ident[:, :])
                last.then_inc(k_turned, 1)
                pe.wait_ge(v_ready, t + 1)
                pe.wait_ge(q_t_ready, t + 1)
                pe.wait_ge(k_t_ready, t + 1)

            turn_x_rows(0)
            pe.wait_ge(weight_gained, DT + C_TILES)
            with pe.Fori(0, CHUNKS - 1) as t:
                chunk(t, True)
            chunk(CHUNKS - 1, False)


def attend(nc, io, keep, first, end, live=None):
    with ExitStack() as ctx:
        sb, ps, sem = allocators(nc, ctx, f"_{first}")
        UNITS = 2 * HEADS
        SLOTS = 4
        ROW_SLOTS = 7
        BATCH = 2 * TOPK
        PROJECT_BLOCKS = 44
        FINISH_AT, ROOT_AT, NORM_AT, TURN_AT, PROJECT_AT = 0, 1, 2, 3, 5
        COUNT = end - first
        ALL_UNITS = [(i, u, first + i + 1) for i in range(COUNT) for u in range(UNITS)]

        ident = sb("a_ident", [P, P])
        w_out = sb("a_w_out", [P, DT, D])
        gain_mix = sb("a_gain_mix", [P, DT])
        eps = sb("a_eps", [P, 1])
        q_mla = sb("a_q_mla", [P, HEADS, P])
        q_dil = sb("a_q_dil", [P, HEADS // 2, P])
        causal = sb("a_causal", [P, SEQ])
        bias = sb("a_bias", [P, SLOTS, SEQ])
        probs = sb("a_probs", [P, 2, SEQ])
        probs_t = sb("a_probs_t", [P, 2, SEQ])
        neg_max = sb("a_neg_max", [P, UNITS])
        sums = sb("a_sums", [P, UNITS])
        inv_sums = sb("a_inv_sums", [P, UNITS])
        mixed = sb("a_mixed", [P, D])
        mixed_t = sb("a_mixed_t", [P, D])
        mix_stat = sb("a_mix_stat", [P, 6])
        residual = sb("a_residual", [P, D])
        scores = [ps(f"a_scores{i}", [P, SEQ]) for i in range(2)]
        turned = ps("a_turned", [P, SEQ])
        heads_out = ps("a_heads_out", [P, D])

        if live is not None:
            ROWS = [("u", k) for k in range(BATCH)]
            for b in range(1, PICKS // BATCH):
                for j in range(BATCH):
                    ROWS += [("u", BATCH * b + j), ("v", BATCH * (b - 1) + j)]
            ROWS += [("v", k) for k in range(PICKS - BATCH, PICKS)]
            weights = np.array([nb + 3 + (PROJECT_BLOCKS if i > 0 and u == PROJECT_AT else 0) for i, u, nb in ALL_UNITS])
            ROWS_AFTER = [0] + [int(c) for c in np.floor(len(ROWS) * np.cumsum(weights) / weights.sum())]
            rows = sb("a_rows", [P, ROW_SLOTS, D])
            dots = sb("a_dots", [P, PICKS])
            active = dots
            coeff = sb("a_coeff", [P, PICKS])
            end_stat = sb("a_end_stat", [P, 3])
            row_loaded = [sem(f"a_row_loaded{i}") for i in range(ROW_SLOTS)]
            u_used, v_used = sem("a_u_used"), sem("a_v_used")
            activated, coeff_ready = sem("a_activated"), sem("a_coeff_ready")
            gain_loaded = sem("a_gain_loaded")
            end_squared, end_rooted = sem("a_end_squared"), sem("a_end_rooted")
            end_inverted, out_ready, out_stored = sem("a_end_inverted"), sem("a_out_ready"), sem("a_out_stored")
            gain_final = live.x

            def wait_row_used(eng, p):
                kind, k = ROWS[p]
                eng.wait_ge(u_used if kind == "u" else v_used, k + 1)

        w_loaded = sem("a_w_loaded")
        small_loaded = sem("a_small_loaded")
        w_gained = sem("a_w_gained")
        eps_set = sem("a_eps_set")
        q_mla_loaded, q_dil_loaded = sem("a_q_mla_loaded"), sem("a_q_dil_loaded")
        causal_loaded = sem("a_causal_loaded")
        bias_loaded = [sem(f"a_bias_loaded{i}") for i in range(SLOTS)]
        x_loaded = sem("a_x_loaded")
        scored, shifted, exped = sem("a_scored"), sem("a_shifted"), sem("a_exped")
        p_turned, p_t_ready, weighed = sem("a_p_turned"), sem("a_p_t_ready"), sem("a_weighed")
        inverted, mixed_ready = sem("a_inverted"), sem("a_mixed_ready")
        squared, rooted, mix_inverted, normed = sem("a_squared"), sem("a_rooted"), sem("a_mix_inverted"), sem("a_normed")
        mix_turned, act_mix_t, dve_mix_t = sem("a_mix_turned"), sem("a_act_mix_t"), sem("a_dve_mix_t")
        projected, h1_ready, h1_stored = sem("a_projected"), sem("a_h1_ready"), sem("a_h1_stored")
        block = ctx.enter_context(nc.Block())

        @block.sync
        def _(sp):
            def load_mla_q(t):
                sp.dma_start(q_mla[0:QK, :, :], io["mla_q_t"][first + t]).then_inc(q_mla_loaded, 16)

            def load_dil_q(t):
                sp.dma_start(q_dil[:, :, :], io["dil_q_t"][first + t]).then_inc(q_dil_loaded, 16)

            def window(table, t):
                at = SEQ - P - P * (first + t)
                return io["score_bias"][table, :, at:SEQ]

            def load_causal(t):
                sp.dma_start(causal[:, 0:P * (first + t + 1)], window(0, t)).then_inc(causal_loaded, 16)

            def load_bias(h, t):
                sp.dma_start(bias[:, h % SLOTS, 0:P * (first + t + 1)], window(1 + h, t)).then_inc(bias_loaded[h % SLOTS], 16)

            def load_residual(t):
                sp.dma_start(residual[:, :], io["x"][P * (first + t):P * (first + t + 1), :]).then_inc(x_loaded, 16)

            def store_h1(t):
                sp.wait_ge(h1_ready, t + 1)
                sp.dma_start(io["h1"][first + t], residual[:, :]).then_inc(h1_stored, 16)
                sp.wait_ge(h1_stored, 16 * (t + 1))

            load_mla_q(0)
            load_causal(0)
            sp.dma_start(ident[:, :], io["identity"]).then_inc(small_loaded, 16)
            sp.dma_start(gain_mix[:, :], io["grp_norm"]).then_inc(small_loaded, 16)
            load_dil_q(0)
            for h in range(SLOTS):
                load_bias(h, 0)
            sp.dma_start(w_out[:, :, :], io["w_out"].rearrange("(t p) n -> p t n", p=P)).then_inc(w_loaded, 16)
            load_residual(0)
            for t in range(COUNT):
                more = t + 1 < COUNT
                if more:
                    sp.wait_ge(scored, UNITS * t + HEADS)
                    load_mla_q(t + 1)
                    sp.wait_ge(shifted, UNITS * t + HEADS)
                    load_causal(t + 1)
                for h in range(SLOTS, HEADS):
                    sp.wait_ge(shifted, UNITS * t + HEADS + h - SLOTS + 1)
                    load_bias(h, t)
                    if t > 0 and h == SLOTS:
                        store_h1(t - 1)
                        load_residual(t)
                if more:
                    for h in range(SLOTS):
                        sp.wait_ge(shifted, UNITS * (t + 1) - SLOTS + h + 1)
                        load_bias(h, t + 1)
                    sp.wait_ge(scored, UNITS * (t + 1))
                    load_dil_q(t + 1)
            store_h1(COUNT - 1)
            if live is not None:
                sp.wait_ge(u_used, PICKS)
                sp.dma_start(gain_final[:, :], io["norm_final_row"].partition_broadcast(P)).then_inc(gain_loaded, 16)
                sp.wait_ge(out_ready, 1)
                sp.dma_start(io["out"][0], live.h[:, :]).then_inc(out_stored, 16)
                sp.wait_ge(out_stored, 16)

        @block.scalar
        def _(act):
            def softmax(n):
                t, u, nb = ALL_UNITS[n]
                act.wait_ge(shifted, n + 1)
                nk = P * nb
                act.activation(probs[:, u % 2, 0:nk], probs[:, u % 2, 0:nk], ACT.Exp, scale=-1.0,
                               bias=neg_max[:, u:u + 1], accum_out=sums[:, u:u + 1]).then_inc(exped, 1)

            def square_mixed(t, g):
                act.wait_ge(mixed_ready, 2 * t + g + 1)
                act.activation(mixed_t[:, WIDTH * g:WIDTH * (g + 1)], mixed[:, WIDTH * g:WIDTH * (g + 1)],
                               ACT.Square, accum_out=mix_stat[:, g:g + 1]).then_inc(squared, 1)

            def root_mixed(t):
                square_mixed(t, 1)
                act.wait_ge(squared, 2 * t + 2)
                act.activation(mix_stat[:, 2:4], mix_stat[:, 0:2], ACT.Sqrt, scale=1.0 / WIDTH, bias=eps[:, :]).then_inc(rooted, 1)

            def keep_mixed_t(t):
                act.wait_ge(mix_turned, t + 1)
                act.activation(mixed_t[:, 0:BANK], turned[:, 0:BANK], ACT.Copy).then_inc(act_mix_t, 1)

            def activate(n):
                for p in range(ROWS_AFTER[n], ROWS_AFTER[n + 1]):
                    kind, k = ROWS[p]
                    if kind == "u" and k % BATCH == BATCH - 1:
                        at = slice(k + 1 - BATCH, k + 1)
                        act.wait_ge(u_used, k + 1)
                        act.activation(active[:, at], dots[:, at], ACT.Gelu).then_inc(activated, 1)

            act.wait_ge(eps_set, 1)
            softmax(0)
            for n, (t, u, nb) in enumerate(ALL_UNITS):
                act.wait_ge(p_turned, n + 1)
                act.activation(probs_t[:, u % 2, 0:P * nb], turned[:, 0:P * nb], ACT.Copy).then_inc(p_t_ready, 1)
                if n + 1 < len(ALL_UNITS):
                    softmax(n + 1)
                if u == HEADS + 1:
                    square_mixed(t, 0)
                if t > 0 and u == ROOT_AT:
                    root_mixed(t - 1)
                if t > 0 and u == TURN_AT:
                    keep_mixed_t(t - 1)
                if live is not None:
                    activate(n)
            root_mixed(COUNT - 1)
            keep_mixed_t(COUNT - 1)
            if live is not None:
                act.wait_ge(v_used, PICKS)
                act.activation(mixed[:, :], live.h[:, :], ACT.Square, accum_out=end_stat[:, 0:1]).then_inc(end_squared, 1)
                act.wait_ge(end_squared, 1)
                act.activation(end_stat[:, 1:2], end_stat[:, 0:1], ACT.Sqrt, scale=1.0 / D, bias=eps[:, :]).then_inc(end_rooted, 1)

        @block.vector
        def _(dve):
            def shift(n):
                t, u, nb = ALL_UNITS[n]
                dve.wait_ge(scored, n + 1)
                nk = P * nb
                if u < HEADS:
                    if u == 0:
                        dve.wait_ge(causal_loaded, 16 * (t + 1))
                    table, scale = causal[:, 0:nk], QK ** -0.5
                else:
                    h = u - HEADS
                    dve.wait_ge(bias_loaded[h % SLOTS], 16 * (HEADS // SLOTS * t + h // SLOTS + 1))
                    table, scale = bias[:, h % SLOTS, 0:nk], HEAD ** -0.5
                dve.tensor_tensor_reduce(probs[:, u % 2, 0:nk], scores[u % 2][:, 0:nk], table, -scale, 3e38,
                                         ALU.add, ALU.min, neg_max[:, u:u + 1]).then_inc(shifted, 1)

            def finish_group(t, g):
                heads = slice(HEADS * g, HEADS * (g + 1))
                cols = slice(WIDTH * g, WIDTH * (g + 1))
                by_head = lambda a: a[:, cols].rearrange("p (h c) -> p h c", h=HEADS)
                dve.wait_ge(weighed, 2 * t + g + 1)
                dve.reciprocal(inv_sums[:, heads], sums[:, heads]).then_inc(inverted, 1)
                dve.wait_ge(inverted, 2 * t + g + 1)
                dve.tensor_tensor(by_head(mixed), by_head(heads_out),
                                  inv_sums[:, heads].unsqueeze(2).to_broadcast([P, HEADS, HEAD]), ALU.mult).then_inc(mixed_ready, 1)

            def norm_mixed(t):
                dve.wait_ge(rooted, t + 1)
                dve.reciprocal(mix_stat[:, 4:6], mix_stat[:, 2:4]).then_inc(mix_inverted, 1)
                dve.wait_ge(mix_inverted, t + 1)
                for g in range(2):
                    dve.tensor_scalar(mixed[:, WIDTH * g:WIDTH * (g + 1)], mixed[:, WIDTH * g:WIDTH * (g + 1)],
                                      mix_stat[:, 4 + g:5 + g], None, ALU.mult).then_inc(normed, 1)

            def keep_mixed_t(t):
                dve.wait_ge(mix_turned, t + 1)
                dve.tensor_copy(mixed_t[:, BANK:D], turned[:, BANK:D]).then_inc(dve_mix_t, 1)

            def add_residual(t):
                dve.wait_ge(projected, t + 1)
                dve.wait_ge(x_loaded, 16 * (t + 1))
                dve.tensor_tensor(residual[:, :], turned[:, :], residual[:, :], ALU.add).then_inc(h1_ready, 1)

            def use_rows(n):
                for p in range(ROWS_AFTER[n], ROWS_AFTER[n + 1]):
                    kind, k = ROWS[p]
                    row = rows[:, p % ROW_SLOTS, :]
                    if kind == "v" and k % BATCH == 0:
                        at = slice(k, k + BATCH)
                        heads = slice(k // TOPK, (k + BATCH) // TOPK)
                        dve.wait_ge(activated, k // BATCH + 1)
                        dve.tensor_tensor(coeff[:, at], active[:, at], live.gate[:, heads, :].rearrange("p h k -> p (h k)"),
                                          ALU.mult).then_inc(coeff_ready, 1)
                    dve.wait_ge(row_loaded[p % ROW_SLOTS], 16 * (p // ROW_SLOTS + 1))
                    if kind == "u":
                        dve.tensor_tensor_reduce(row, row, live.x[:, :], 1.0, 0.0, ALU.mult, ALU.add,
                                                 dots[:, k:k + 1]).then_inc(u_used, 1)
                    else:
                        dve.wait_ge(coeff_ready, k // BATCH + 1)
                        if k > 0:
                            dve.wait_ge(v_used, k)
                        dve.scalar_tensor_tensor(live.h[:, :], row, coeff[:, k:k + 1], live.h[:, :], ALU.mult,
                                                 ALU.add).then_inc(v_used, 1)

            dve.memset(eps[:, :], EPS).then_inc(eps_set, 1)
            shift(0)
            for n, (t, u, nb) in enumerate(ALL_UNITS):
                if n + 1 < len(ALL_UNITS):
                    shift(n + 1)
                if u == HEADS:
                    finish_group(t, 0)
                if t > 0:
                    if u == FINISH_AT:
                        finish_group(t - 1, 1)
                    if u == NORM_AT:
                        norm_mixed(t - 1)
                    if u == TURN_AT:
                        keep_mixed_t(t - 1)
                if live is not None:
                    use_rows(n)
                if t > 0 and u == PROJECT_AT:
                    add_residual(t - 1)
            finish_group(COUNT - 1, 1)
            norm_mixed(COUNT - 1)
            keep_mixed_t(COUNT - 1)
            add_residual(COUNT - 1)
            if live is not None:
                dve.wait_ge(end_rooted, 1)
                dve.reciprocal(end_stat[:, 2:3], end_stat[:, 1:2]).then_inc(end_inverted, 1)
                dve.wait_ge(end_inverted, 1)
                dve.wait_ge(gain_loaded, 16)
                dve.scalar_tensor_tensor(live.h[:, :], live.h[:, :], end_stat[:, 2:3], gain_final[:, :], ALU.mult,
                                         ALU.mult).then_inc(out_ready, 1)

        @block.gpsimd
        def _(pool):
            pool.wait_ge(small_loaded, 32)
            pool.wait_ge(w_loaded, 16)
            for k in range(DT):
                pool.tensor_scalar(w_out[:, k, :], w_out[:, k, :], gain_mix[:, k:k + 1], 1.0, ALU.mult,
                                   ALU.mult).then_inc(w_gained, 1)
            if live is None:
                return

            def gather(p):
                if p >= ROW_SLOTS:
                    wait_row_used(pool, p - ROW_SLOTS)
                kind, k = ROWS[p]
                pool.indirect_dma_start(out=rows[:, p % ROW_SLOTS, :], out_offset=None,
                                        in_=io["peer_u"] if kind == "u" else io["peer_v"],
                                        in_offset=bass.IndirectOffsetOnAxis(ap=live.expert[:, k:k + 1], axis=0)
                                        ).then_inc(row_loaded[p % ROW_SLOTS], 16)

            for p in range(len(ROWS)):
                gather(p)

        @block.tensor
        def _(pe):
            def score(n):
                t, u, nb = ALL_UNITS[n]
                if u == 0:
                    pe.wait_ge(q_mla_loaded, 16 * (t + 1))
                if u == HEADS:
                    pe.wait_ge(q_dil_loaded, 16 * (t + 1))
                if n >= 2:
                    pe.wait_ge(shifted, n - 1)
                for at in range(0, P * nb, BANK):
                    width = min(BANK, P * nb - at)
                    to = scores[u % 2][:, at:at + width]
                    if u < HEADS:
                        last = pe.matmul(to, q_mla[0:QK, u, :], keep["mla_k_t"][0:QK, u, at:at + width], start=True, stop=True)
                    else:
                        h = u - HEADS
                        rows = slice(HEAD * (h % 2), HEAD * (h % 2) + HEAD)
                        last = pe.matmul(to, q_dil[rows, h // 2, :], keep["dil_k_t"][rows, h // 2, at:at + width],
                                         start=True, stop=True)
                last.then_inc(scored, 1)

            def weigh(n):
                t, u, nb = ALL_UNITS[n]
                pe.wait_ge(p_t_ready, n + 1)
                if t > 0 and u in (0, HEADS):
                    pe.wait_ge(mixed_ready, 2 * (t - 1) + u // HEADS + 1)
                for k in range(nb):
                    last = pe.matmul(heads_out[:, HEAD * u:HEAD * (u + 1)], probs_t[:, u % 2, P * k:P * (k + 1)],
                                     keep["values"][:, k, HEAD * u:HEAD * (u + 1)], start=(k == 0), stop=(k == nb - 1))
                if u in (HEADS - 1, UNITS - 1):
                    last.then_inc(weighed, 1)

            def turn_mixed(t):
                pe.wait_ge(normed, 2 * t + 2)
                for k in range(DT):
                    last = pe.transpose(turned[:, P * k:P * (k + 1)], mixed[:, P * k:P * (k + 1)], ident[:, :])
                last.then_inc(mix_turned, 1)

            def project(t):
                pe.wait_ge(w_gained, DT)
                for c in range(2):
                    for k in range(DT):
                        last = pe.matmul(turned[:, BANK * c:BANK * (c + 1)], mixed_t[:, P * k:P * (k + 1)],
                                         w_out[:, k, BANK * c:BANK * (c + 1)], start=(k == 0), stop=(k == DT - 1))
                last.then_inc(projected, 1)

            def wait_mixed_t(t):
                pe.wait_ge(act_mix_t, t + 1)
                pe.wait_ge(dve_mix_t, t + 1)

            pe.wait_ge(small_loaded, 32)
            score(0)
            score(1)
            for n, (t, u, nb) in enumerate(ALL_UNITS):
                if t > 0 and u == TURN_AT + 1:
                    wait_mixed_t(t - 1)
                if t > 0 and u == PROJECT_AT + 1:
                    pe.wait_ge(h1_ready, t)
                pe.wait_ge(exped, n + 1)
                for k in range(nb):
                    last = pe.transpose(turned[:, P * k:P * (k + 1)], probs[:, u % 2, P * k:P * (k + 1)], ident[:, :])
                last.then_inc(p_turned, 1)
                if t > 0 and u == TURN_AT:
                    weigh(n)
                    turn_mixed(t - 1)
                elif t > 0 and u == PROJECT_AT:
                    weigh(n)
                    project(t - 1)
                if n + 2 < len(ALL_UNITS):
                    score(n + 2)
                if not (t > 0 and u in (TURN_AT, PROJECT_AT)):
                    weigh(n)
            turn_mixed(COUNT - 1)
            wait_mixed_t(COUNT - 1)
            project(COUNT - 1)


def pick_buffers(sb, ps, sem, ident):
    b = PickBuffers()
    b.ident = ident
    b.gain_ffn = sb("e_gain_ffn", [P, D])
    b.slots = sb("e_slots", [P, TOPK])
    b.eps = sb("e_eps", [P, 1])
    b.rows = sb("e_rows", [P, D])
    b.rows_t = sb("e_rows_t", [P, D])
    b.work = sb("e_work", [P, 2 * D])
    b.stat = sb("e_stat", [P, 3])
    b.mem_stat = sb("e_mem_stat", [P, 4, MEM_HEADS])
    b.top = sb("e_top", [P, PEER_TABLES, TOPK])
    b.top_at = sb("e_top_at", [P, PEER_TABLES, TOPK], U32)
    b.top_at_f = b.top
    b.best = sb("e_best", [P, PEER_HEADS, TOPK])
    b.best_at = sb("e_best_at", [P, PICKS], U32)
    b.place = sb("e_place", [P, 2, PICKS], U32)
    b.place_f = sb("e_place_f", [P, 2, PICKS])
    b.key_at = b.place_f
    b.gate_next = sb("e_gate_next", [P, PEER_HEADS, TOPK])
    b.gate_sum = sb("e_gate_sum", [P, 2, PEER_HEADS])
    b.turned = ps("e_turned", [P, D])
    b.product = [ps(f"e_product{i}", [P, D]) for i in range(2)]
    b.h1_loaded = sem("e_h1_loaded")
    b.squared, b.rooted, b.inverted, b.normed = sem("e_squared"), sem("e_rooted"), sem("e_inverted"), sem("e_normed")
    b.rows_turned, b.rows_t_ready = sem("e_rows_turned"), sem("e_rows_t_ready")
    b.mem_scored, b.mem_maxed, b.mem_negated = sem("e_mem_scored"), sem("e_mem_maxed"), sem("e_mem_negated")
    b.mem_exped, b.mem_inverted, b.mem_normed = sem("e_mem_exped"), sem("e_mem_inverted"), sem("e_mem_normed")
    b.mem_out, b.h2_ready = sem("e_mem_out"), sem("e_h2_ready")
    b.squared2, b.rooted2, b.inverted2, b.normed2 = sem("e_squared2"), sem("e_rooted2"), sem("e_inverted2"), sem("e_normed2")
    b.peer_scored, b.scores_kept = sem("e_peer_scored"), sem("e_scores_kept")
    b.step = sem("e_step")
    b.gate_shifted, b.gate_exped = sem("e_gate_shifted"), sem("e_gate_exped")
    b.expert_u_ready, b.passed_dve = sem("e_expert_u_ready"), sem("e_passed_dve")
    b.eps_set = sem("e_eps_set")
    return b


def need(eng, semaphore, value):
    if not (isinstance(value, int) and value <= 0):
        eng.wait_ge(semaphore, value)


def pick_steps(nc, b, half_table, wait_work, target):
    def front_scalar(f, names):
        for name in names:
            if name == "square":
                nc.scalar.wait_ge(b.h1_loaded, 16 * (f + 1))
                nc.scalar.activation(b.rows[:, :], target(f).h_next[:, :], ACT.Square, accum_out=b.stat[:, 0:1]).then_inc(b.squared, 1)
                nc.scalar.wait_ge(b.squared, f + 1)
                nc.scalar.activation(b.stat[:, 1:2], b.stat[:, 0:1], ACT.Sqrt, scale=1.0 / D, bias=b.eps[:, :]).then_inc(b.rooted, 1)
            elif name in ("turn", "mem_turn", "turn2"):
                n = 3 * f + 1 + ("turn", "mem_turn", "turn2").index(name)
                nc.scalar.wait_ge(b.rows_turned, n)
                nc.scalar.activation(b.rows_t[:, :], b.turned[:, :], ACT.Copy).then_inc(b.rows_t_ready, 1)
            elif name == "mem_exp":
                nc.scalar.wait_ge(b.mem_negated, f + 1)
                for h in range(MEM_HEADS):
                    at = slice(MEM_LEN * h, MEM_LEN * (h + 1))
                    nc.scalar.activation(b.rows[:, at], b.product[0][:, at], ACT.Exp, bias=b.mem_stat[:, 1, h:h + 1],
                                   accum_out=b.mem_stat[:, 2, h:h + 1]).then_inc(b.mem_exped, 1)
            elif name == "square2":
                nc.scalar.wait_ge(b.h2_ready, f + 1)
                nc.scalar.activation(b.rows[:, :], target(f).h_next[:, :], ACT.Square, accum_out=target(f).stat2[:, 0:1]).then_inc(b.squared2, 1)
                nc.scalar.wait_ge(b.squared2, f + 1)
                nc.scalar.activation(target(f).stat2[:, 1:2], target(f).stat2[:, 0:1], ACT.Sqrt, scale=1.0 / D, bias=b.eps[:, :]).then_inc(b.rooted2, 1)
            elif name.startswith("keep_"):
                g = int(name[-1])
                nc.scalar.wait_ge(b.peer_scored, 4 * f + g + 1)
                if g == 0:
                    wait_work(nc.scalar, f)
                nc.scalar.activation(b.work[:, BANK * g:BANK * (g + 1)],
                               b.product[g // 2][:, BANK * (g % 2):BANK * (g % 2 + 1)], ACT.Copy).then_inc(b.scores_kept, 1)
            elif name == "gate_exp":
                nc.scalar.wait_ge(b.gate_shifted, f + 1)
                nc.scalar.activation(b.gate_next[:, :, :], b.gate_next[:, :, :], ACT.Exp).then_inc(b.gate_exped, 1)

    made = [0]

    def stepped(instruction):
        made[0] += 1
        instruction.then_inc(b.step, 1)

    def after_steps(f):
        nc.vector.wait_ge(b.step, PICK_STEPS * f + made[0])
        nc.vector.sem_inc(b.passed_dve, 1)

    def top_16(part, values, tops, places):
        for i in range(len(values)):
            if part == 0:
                stepped(nc.vector.max(tops[i][:, 0:8], values[i]))
            elif part == 1:
                stepped(nc.vector.max_index(places[i][:, 0:8], tops[i][:, 0:8], values[i]))
            elif part == 2:
                stepped(nc.vector.match_replace(values[i], tops[i][:, 0:8], values[i], -3e38))
            elif part == 3:
                stepped(nc.vector.max(tops[i][:, 8:16], values[i]))
            else:
                stepped(nc.vector.max_index(places[i][:, 8:16], tops[i][:, 8:16], values[i]))

    def front_vector(f, names):
        for name in names:
            if name == "norm":
                nc.vector.wait_ge(b.rooted, f + 1)
                nc.vector.reciprocal(b.stat[:, 2:3], b.stat[:, 1:2]).then_inc(b.inverted, 1)
                nc.vector.wait_ge(b.inverted, f + 1)
                nc.vector.tensor_scalar(b.rows[:, :], target(f).h_next[:, :], b.stat[:, 2:3], None, ALU.mult).then_inc(b.normed, 1)
            elif name == "mem_max":
                nc.vector.wait_ge(b.mem_scored, 2 * f + 2)
                nc.vector.tensor_reduce(b.mem_stat[:, 0, :], b.product[0][:, :].rearrange("p (h m) -> p h m", h=MEM_HEADS),
                                  AX_X, ALU.max).then_inc(b.mem_maxed, 1)
                nc.vector.wait_ge(b.mem_maxed, f + 1)
                nc.vector.tensor_scalar(b.mem_stat[:, 1, :], b.mem_stat[:, 0, :], -1.0, None, ALU.mult).then_inc(b.mem_negated, 1)
            elif name == "mem_norm":
                nc.vector.wait_ge(b.mem_exped, MEM_HEADS * (f + 1))
                nc.vector.reciprocal(b.mem_stat[:, 3, :], b.mem_stat[:, 2, :]).then_inc(b.mem_inverted, 1)
                nc.vector.wait_ge(b.mem_inverted, f + 1)
                heads = b.rows[:, :].rearrange("p (h m) -> p h m", h=MEM_HEADS)
                nc.vector.tensor_tensor(heads, heads, b.mem_stat[:, 3, :].unsqueeze(2).to_broadcast([P, MEM_HEADS, MEM_LEN]),
                                  ALU.mult).then_inc(b.mem_normed, 1)
            elif name == "h2":
                nc.vector.wait_ge(b.mem_out, 2 * f + 2)
                nc.vector.tensor_tensor(target(f).h_next[:, :], b.product[1][:, :], target(f).h_next[:, :], ALU.add).then_inc(b.h2_ready, 1)
            elif name == "norm2":
                nc.vector.wait_ge(b.rooted2, f + 1)
                nc.vector.reciprocal(target(f).stat2[:, 2:3], target(f).stat2[:, 1:2]).then_inc(b.inverted2, 1)
                nc.vector.wait_ge(b.inverted2, f + 1)
                nc.vector.tensor_scalar(b.rows[:, :], target(f).h_next[:, :], target(f).stat2[:, 2:3], None, ALU.mult).then_inc(b.normed2, 1)
            elif name.startswith("top_"):
                g, part = int(name[4]), int(name[6])
                if part > 0:
                    after_steps(f)
                else:
                    if g == 0:
                        made[0] = 0
                    nc.vector.wait_ge(b.scores_kept, 4 * f + g + 1)
                    nc.vector.sem_inc(b.passed_dve, 1)
                four = range(4 * g, 4 * g + 4)
                top_16(part, [b.work[:, PEER_KEYS * i:PEER_KEYS * (i + 1)] for i in four], [b.top[:, i, :] for i in four],
                       [b.top_at[:, i, :] for i in four])
            elif name == "pairs":
                after_steps(f)
                halves = b.top[:, :, :].rearrange("p (h two) k -> p h two k", two=2)
                stepped(nc.vector.tensor_tensor(
                    b.work[:, :].rearrange("p (h i j) -> p h i j", h=PEER_HEADS, i=TOPK),
                    halves[:, :, 0, :].unsqueeze(3).to_broadcast([P, PEER_HEADS, TOPK, TOPK]),
                    halves[:, :, 1, :].unsqueeze(2).to_broadcast([P, PEER_HEADS, TOPK, TOPK]), ALU.add))
            elif name == "floats":
                after_steps(f)
                stepped(nc.vector.tensor_copy(b.top_at_f[:, :, :], b.top_at[:, :, :]))
            elif name.startswith("best_"):
                g, part = int(name[5]), int(name[7])
                after_steps(f)
                two = range(2 * g, 2 * g + 2)
                pairs = TOPK * TOPK
                top_16(part, [b.work[:, pairs * h:pairs * (h + 1)] for h in two], [b.best[:, h, :] for h in two],
                       [b.best_at[:, TOPK * h:TOPK * (h + 1)] for h in two])
            elif name == "places":
                after_steps(f)
                nc.vector.tensor_tensor(b.gate_next[:, :, :], b.best[:, :, :],
                                        b.best[:, :, 0:1].to_broadcast([P, PEER_HEADS, TOPK]), ALU.subtract).then_inc(b.gate_shifted, 1)
                stepped(nc.vector.tensor_scalar(b.place[:, 0, :], b.best_at[:, :], 4, None, ALU.logical_shift_right))
                stepped(nc.vector.tensor_scalar(b.place[:, 1, :], b.best_at[:, :], TOPK - 1, None, ALU.bitwise_and))
                after_steps(f)
                stepped(nc.vector.tensor_copy(b.place_f[:, :, :], b.place[:, :, :]))
            elif name.startswith("pick_"):
                half, part = int(name[5]), int(name[7])
                after_steps(f)
                one_hot = b.work[:, :].rearrange("p (k s) -> p k s", s=TOPK)
                if part == 0:
                    stepped(nc.vector.tensor_tensor(one_hot, b.place_f[:, half, :].unsqueeze(2).to_broadcast([P, PICKS, TOPK]),
                                                    b.slots[:, :].unsqueeze(1).to_broadcast([P, PICKS, TOPK]), ALU.is_equal))
                elif part == 1:
                    keys = b.top_at_f[:, :, :].rearrange("p (h two) s -> p h two s", two=2)[:, :, half, :]
                    four_d = b.work[:, :].rearrange("p (h k s) -> p h k s", h=PEER_HEADS, k=TOPK)
                    stepped(nc.vector.tensor_tensor(four_d, four_d, keys.unsqueeze(2).to_broadcast([P, PEER_HEADS, TOPK, TOPK]),
                                                    ALU.mult))
                else:
                    stepped(nc.vector.tensor_reduce(b.key_at[:, half, :], one_hot, AX_X, ALU.add))
            elif name == "live":
                after_steps(f)
                nc.vector.scalar_tensor_tensor(target(f).expert[:, :], b.key_at[:, 0, :], float(PEER_KEYS), b.key_at[:, 1, :],
                                         ALU.mult, ALU.add).then_inc(b.expert_u_ready, 1)
                nc.vector.scalar_tensor_tensor(target(f).x[:, :], target(f).h_next[:, :], target(f).stat2[:, 2:3], b.gain_ffn[:, :], ALU.mult,
                                         ALU.mult).then_inc(b.step, 1)
                made[0] += 1
                nc.vector.wait_ge(b.gate_exped, f + 1)
                stepped(nc.vector.tensor_reduce(b.gate_sum[:, 0, :], b.gate_next[:, :, :], AX_X, ALU.add))
                after_steps(f)
                stepped(nc.vector.reciprocal(b.gate_sum[:, 1, :], b.gate_sum[:, 0, :]))
                after_steps(f)
                stepped(nc.vector.tensor_tensor(target(f).gate[:, :, :], b.gate_next[:, :, :],
                                          b.gate_sum[:, 1, :].unsqueeze(2).to_broadcast([P, PEER_HEADS, TOPK]), ALU.mult))
                after_steps(f)
                assert made[0] == PICK_STEPS

    PRODUCTS = {"mem_a": (b.product[0][:, 0:BANK], b.mem_scored), "mem_b": (b.product[0][:, BANK:D], b.mem_scored),
                "out_a": (b.product[1][:, 0:BANK], b.mem_out), "out_b": (b.product[1][:, BANK:D], b.mem_out)}
    PRODUCTS.update({f"peer_{g}": (b.product[g // 2][:, BANK * (g % 2):BANK * (g % 2 + 1)], b.peer_scored) for g in range(4)})

    def front_tensor(f, names):
        for name in names:
            if name in ("turn", "mem_turn", "turn2"):
                n = ("turn", "mem_turn", "turn2").index(name)
                nc.tensor.wait_ge((b.normed, b.mem_normed, b.normed2)[n], f + 1)
                need(nc.tensor, b.rows_t_ready, 3 * f + n)
                for k in range(DT):
                    last = nc.tensor.transpose(b.turned[:, P * k:P * (k + 1)], b.rows[:, P * k:P * (k + 1)], b.ident[:, :])
                last.then_inc(b.rows_turned, 1)
            elif name[:-2] in PRODUCTS:
                product, k = name[:-2], int(name[-1])
                if name == "mem_a_0":
                    nc.tensor.wait_ge(b.rows_t_ready, 3 * f + 1)
                    need(nc.tensor, b.scores_kept, 4 * f)
                elif name == "out_a_0":
                    nc.tensor.wait_ge(b.rows_t_ready, 3 * f + 2)
                elif name == "peer_0_0":
                    nc.tensor.wait_ge(b.rows_t_ready, 3 * f + 3)
                table = half_table(f, list(PRODUCTS).index(product), k == 0)
                bank, done = PRODUCTS[product]
                last = nc.tensor.matmul(bank, b.rows_t[:, P * k:P * (k + 1)], table[:, k, :], start=(k == 0), stop=(k == DT - 1))
                if k == DT - 1:
                    last.then_inc(done, 1)

    return front_scalar, front_vector, front_tensor


def make_first_picks(nc, io, live):
    with ExitStack() as ctx:
        sb, ps, sem = allocators(nc, ctx, "_first")
        HALVES = ([("mem_scores", BANK * i) for i in range(2)] + [("mem_values", BANK * i) for i in range(2)] +
                  [("peer_scores", BANK * i) for i in range(4)])
        HALF_SLOTS = 5
        halves = sb("e_halves", [P, HALF_SLOTS, DT, BANK])
        ident = sb("e_ident", [P, P])
        b = pick_buffers(sb, ps, sem, ident)
        live.h_next, live.stat2 = live.h, sb("e_stat2_0", [P, 3])
        following = Picks(h_next=sb("e_h_1", [P, D]), stat2=sb("e_stat2_1", [P, 3]), x=sb("e_x_1", [P, D]), expert=sb("e_expert_1", [P, PICKS], U32),
                                    gate=sb("e_gate_1", [P, PEER_HEADS, TOPK]))
        half_loaded = [sem(f"e_half_loaded{i}") for i in range(HALF_SLOTS)]
        small_loaded = sem("e_small_loaded")
        next_stored = sem("e_next_stored")

        def half_table(f, number, first):
            n = len(HALVES) * f + number
            if first:
                nc.tensor.wait_ge(half_loaded[n % HALF_SLOTS], 16 * (n // HALF_SLOTS + 1))
            return halves[:, n % HALF_SLOTS]

        def wait_work(eng, f):
            if f > 0:
                eng.wait_ge(b.step, PICK_STEPS * f)

        LATE = FRONT_STEPS.index("top_0_0")
        WORK_FROM = FRONT_STEPS.index("peer_0_0")
        BESIDE = {"top_2_4": ["norm"], "best_0_4": ["mem_max"], "best_1_4": ["mem_norm"], "best_3_4": ["h2"],
                  "pick_0_0": ["norm2"]}
        front_scalar, front_vector, front_tensor = pick_steps(nc, b, half_table, wait_work,
                                                              lambda f: (live, following)[f])
        block = ctx.enter_context(nc.Block())

        @block.sync
        def _(sp):
            def wait_half_used(n):
                f, number = divmod(n, len(HALVES))
                if number < 2:
                    sp.wait_ge(b.mem_scored, 2 * f + number + 1)
                elif number < 4:
                    sp.wait_ge(b.mem_out, 2 * f + number - 1)
                else:
                    sp.wait_ge(b.peer_scored, 4 * f + number - 3)

            def load_half(n):
                if n >= HALF_SLOTS:
                    wait_half_used(n - HALF_SLOTS)
                name, at = HALVES[n % len(HALVES)]
                sp.dma_start(halves[:, n % HALF_SLOTS, :, :], io[name][:, :, at:at + BANK]).then_inc(half_loaded[n % HALF_SLOTS], 16)

            sp.dma_start(live.h[:, :], io["h1"][0]).then_inc(b.h1_loaded, 16)
            sp.dma_start(ident[:, :], io["identity"]).then_inc(small_loaded, 16)
            sp.dma_start(b.slots[:, :], io["slots"]).then_inc(small_loaded, 16)
            sp.dma_start(b.gain_ffn[:, :], io["norm_ffn_row"].partition_broadcast(P)).then_inc(small_loaded, 16)
            for n in range(HALF_SLOTS):
                load_half(n)
            sp.wait_ge(b.squared, 1)
            sp.dma_start(following.h_next[:, :], io["h1"][1]).then_inc(b.h1_loaded, 16)
            for n in range(HALF_SLOTS, 2 * len(HALVES)):
                load_half(n)
            sp.wait_ge(b.step, 2 * PICK_STEPS)
            sp.wait_ge(b.expert_u_ready, 2)
            sp.dma_start(io["next_h"], following.h_next[:, :]).then_inc(next_stored, 16)
            sp.dma_start(io["next_x"], following.x[:, :]).then_inc(next_stored, 16)
            sp.dma_start(io["next_expert"], following.expert[:, :]).then_inc(next_stored, 16)
            sp.dma_start(io["next_gate"], following.gate[:, :, :]).then_inc(next_stored, 16)
            sp.wait_ge(next_stored, 64)

        @block.scalar
        def _(act):
            act.wait_ge(b.eps_set, 1)
            front_scalar(0, [step for step in FRONT_STEPS if step != "gate_exp"])
            front_scalar(1, FRONT_STEPS[:WORK_FROM])
            front_scalar(0, ["gate_exp"])
            front_scalar(1, FRONT_STEPS[WORK_FROM:])

        @block.vector
        def _(dve):
            dve.memset(b.eps[:, :], EPS).then_inc(b.eps_set, 1)
            dve.wait_ge(small_loaded, 48)
            front_vector(0, FRONT_STEPS[:LATE])
            for step in FRONT_STEPS[LATE:]:
                front_vector(0, [step])
                front_vector(1, BESIDE.get(step, []))
            front_vector(1, FRONT_STEPS[LATE:])

        @block.tensor
        def _(pe):
            pe.wait_ge(small_loaded, 48)
            for f in range(2):
                front_tensor(f, FRONT_STEPS)


def attend_memory_and_experts(nc, io):
    ORDER = [("u", k) for k in range(TOPK)]
    for h in range(1, PEER_HEADS):
        for i in range(TOPK):
            ORDER += [("u", TOPK * h + i), ("v", TOPK * (h - 1) + i)]
    ORDER += [("v", k) for k in range(PICKS - TOPK, PICKS)]
    GATHERS = len(ORDER)
    TURNS = GATHERS // RING
    U_END = {h: max(p for p, (kind, k) in enumerate(ORDER) if kind == "u" and k // TOPK == h) for h in range(PEER_HEADS)}
    DIAGONALS = 4
    STEP_AT = {"end_sum": 7, "end_root": 15, "end_out": 23, "square": 27, "norm": 30, "turn": 33,
               "mem_max": 54, "mem_exp": 56, "mem_norm": 60, "mem_turn": 63, "h2": 84, "square2": 86, "norm2": 90,
               "turn2": 93, "gate_exp": 223, "live": 246}
    for product, first in (("mem_a", 37), ("mem_b", 45), ("out_a", 67), ("out_b", 75)):
        STEP_AT.update({f"{product}_{k}": first + k for k in range(DT)})
    STEP_AT.update({f"peer_{g}_{k}": 97 + DT * g + k for g in range(4) for k in range(DT)})
    STEP_AT.update({f"keep_{g}": 105 + DT * g for g in range(4)})
    spread = [name for name in FRONT_STEPS if name not in STEP_AT]
    STEP_AT.update({name: 108 + i * (244 - 108) // len(spread) for i, name in enumerate(spread)})
    steps_at = {p: [name for name in ["end_sum", "end_root", "end_out"] + FRONT_STEPS if STEP_AT[name] == p]
                for p in range(GATHERS)}
    LAST = CHUNKS - 2

    with ExitStack() as ctx:
        sb, ps, sem = allocators(nc, ctx)
        ident = sb("e_ident", [P, P])
        mem_scores = sb("e_mem_scores", [P, DT, D])
        mem_values = sb("e_mem_values", [P, DT, D])
        peer_scores = sb("e_peer_scores", [P, DT, 2 * D])
        gain_final = sb("e_gain_final", [P, D])
        ring = sb("e_ring", [P, RING, D])
        diagonal = sb("e_diagonal", [P, DIAGONALS, P])
        b = pick_buffers(sb, ps, sem, ident)
        live = Picks(h_next=sb("e_h_next", [P, D]), stat2=sb("e_stat2", [P, 3]), x=sb("e_x", [P, D]), expert=sb("e_expert_u", [P, PICKS], U32),
                               gate=sb("e_gate", [P, PEER_HEADS, TOPK]))
        h_live = sb("e_h_live", [P, D])
        expert_v = sb("e_expert_v", [P, PICKS], U32)
        dots = sb("e_dots", [P, PICKS])
        active = dots
        coeff = sb("e_coeff", [P, PICKS])
        end_stat = sb("e_end_stat", [P, 3])
        acc = ps("e_acc", [P, D])

        small_loaded = sem("e_small_loaded")
        tables_loaded = [sem(f"e_tables_loaded{i}") for i in range(3)]
        state_loaded = sem("e_state_loaded")
        expert_v_ready = sem("e_expert_v_ready")
        gathered = [sem(f"e_gathered{i}") for i in range(RING)]
        u_used, v_used = sem("e_u_used"), sem("e_v_used")
        activated, coeff_ready, diagonal_ready = sem("e_activated"), sem("e_coeff_ready"), sem("e_diagonal_ready")
        h3_ready, h2_kept = sem("e_h3_ready"), sem("e_h2_kept")
        end_squared, end_rooted, end_inverted = sem("e_end_squared"), sem("e_end_rooted"), sem("e_end_inverted")
        out_ready, out_stored = sem("e_out_ready"), sem("e_out_stored")
        passed_pool = sem("e_passed_pool")
        block = ctx.enter_context(nc.Block())

        def half_table(f, number, first):
            i, table, at = ((0, mem_scores, number), (1, mem_values, number - 2),
                            (2, peer_scores, number - 4))[min(number // 2, 2)]
            if first and number in (0, 2, 4):
                nc.tensor.wait_ge(tables_loaded[i], 16)
            return table[:, :, BANK * at:BANK * (at + 1)]

        def wait_work(eng, f):
            need(eng, out_stored, 16 * f)

        front_scalar, front_vector, front_tensor = pick_steps(nc, b, half_table, wait_work, lambda f: live)

        def for_chunks(eng, body, end):
            body(0, True)
            with eng.Fori(1, LAST) as t:
                body(t, True)
            body(LAST, False)
            end(LAST, ["end_sum", "end_root", "end_out"])

        def steps(t, more, position, front, end):
            names = steps_at[position]
            if not (isinstance(t, int) and t == 0):
                end(t - 1, [n for n in names if n.startswith("end")])
            if more:
                front(t, [n for n in names if not n.startswith("end")])

        @block.sync
        def _(sp):
            def load_h1(f):
                sp.dma_start(live.h_next[:, :], io["h1"][bass.ds(f + 2, 1)].rearrange("a p d -> (a p) d")).then_inc(b.h1_loaded, 16)

            def store_out(t):
                sp.wait_ge(out_ready, t + 1)
                sp.dma_start(io["out"][bass.ds(t + 1, 1)].rearrange("a p d -> (a p) d"), b.work[:, 0:D]).then_inc(out_stored, 16)

            sp.dma_start(live.expert[:, :], io["next_expert"]).then_inc(state_loaded, 16)
            sp.dma_start(live.gate[:, :, :], io["next_gate"]).then_inc(state_loaded, 16)
            sp.dma_start(live.x[:, :], io["next_x"]).then_inc(state_loaded, 16)
            sp.dma_start(live.h_next[:, :], io["next_h"]).then_inc(state_loaded, 16)
            sp.dma_start(ident[:, :], io["identity"]).then_inc(small_loaded, 16)
            sp.dma_start(b.slots[:, :], io["slots"]).then_inc(small_loaded, 16)
            sp.dma_start(b.gain_ffn[:, :], io["norm_ffn_row"].partition_broadcast(P)).then_inc(small_loaded, 16)
            sp.dma_start(gain_final[:, :], io["norm_final_row"].partition_broadcast(P)).then_inc(small_loaded, 16)
            for i, (table, name) in enumerate(((mem_scores, "mem_scores"), (mem_values, "mem_values"),
                                               (peer_scores, "peer_scores"))):
                sp.dma_start(table[:, :, :], io[name]).then_inc(tables_loaded[i], 16)
            sp.wait_ge(h2_kept, 1)
            load_h1(0)
            with sp.Fori(1, LAST) as t:
                sp.wait_ge(h2_kept, t + 1)
                load_h1(t)
                store_out(t - 1)
            store_out(LAST - 1)
            store_out(LAST)
            sp.wait_ge(out_stored, 16 * (LAST + 1))

        @block.gpsimd
        def _(pool):
            def body(t, more):
                for p, (kind, k) in enumerate(ORDER):
                    before_kind, before = ORDER[(p - RING) % GATHERS]
                    chunk = t if p >= RING else t - 1
                    need(pool, u_used if before_kind == "u" else v_used, PICKS * chunk + before + 1)
                    if p == 0:
                        need(pool, b.expert_u_ready, t)
                    if (kind, k) == ("v", 0):
                        pool.wait_ge(expert_v_ready, t + 1)
                    pool.sem_inc(passed_pool, 1)
                    expert, table = (live.expert, io["peer_u"]) if kind == "u" else (expert_v, io["peer_v"])
                    pool.indirect_dma_start(out=ring[:, p % RING, :], out_offset=None, in_=table,
                                            in_offset=bass.IndirectOffsetOnAxis(ap=expert[:, k:k + 1], axis=0)
                                            ).then_inc(gathered[p % RING], 16)

            pool.wait_ge(state_loaded, 64)
            for_chunks(pool, body, lambda t, names: None)

        @block.scalar
        def _(act):
            def end(t, names):
                if "end_root" in names:
                    act.wait_ge(h3_ready, t + 1)
                    act.activation(b.work[:, D:2 * D], b.work[:, 0:D], ACT.Square, accum_out=end_stat[:, 0:1]).then_inc(end_squared, 1)
                    act.wait_ge(end_squared, t + 1)
                    act.activation(end_stat[:, 1:2], end_stat[:, 0:1], ACT.Sqrt, scale=1.0 / D, bias=b.eps[:, :]).then_inc(end_rooted, 1)

            def body(t, more):
                for p, (kind, k) in enumerate(ORDER):
                    if kind == "v":
                        if k % TOPK == 0:
                            h = k // TOPK
                            act.wait_ge(u_used, PICKS * t + TOPK * (h + 1))
                            at = slice(TOPK * h, TOPK * (h + 1))
                            act.activation(active[:, at], dots[:, at], ACT.Gelu).then_inc(activated, 1)
                            act.wait_ge(coeff_ready, PEER_HEADS * t + h + 1)
                        need(act, v_used, PICKS * t + k - DIAGONALS + 1)
                        act.activation(diagonal[:, k % DIAGONALS, :], ident[:, :], ACT.Copy,
                                       scale=coeff[:, k:k + 1]).then_inc(diagonal_ready, 1)
                    steps(t, more, p, front_scalar, end)

            act.wait_ge(b.eps_set, 1)
            act.wait_ge(small_loaded, 64)
            for_chunks(act, body, end)

        @block.vector
        def _(dve):
            def end(t, names):
                if "end_sum" in names:
                    dve.wait_ge(v_used, PICKS * (t + 1))
                    need(dve, out_stored, 16 * t)
                    dve.tensor_tensor(b.work[:, 0:D], acc[:, :], h_live[:, :], ALU.add).then_inc(h3_ready, 1)
                    dve.wait_ge(h3_ready, t + 1)
                if "end_out" in names:
                    dve.wait_ge(end_rooted, t + 1)
                    dve.reciprocal(end_stat[:, 2:3], end_stat[:, 1:2]).then_inc(end_inverted, 1)
                    dve.wait_ge(end_inverted, t + 1)
                    dve.scalar_tensor_tensor(b.work[:, 0:D], b.work[:, 0:D], end_stat[:, 2:3], gain_final[:, :], ALU.mult,
                                             ALU.mult).then_inc(out_ready, 1)

            def body(t, more):
                for p, (kind, k) in enumerate(ORDER):
                    for h, at in U_END.items():
                        if p == at + 4:
                            dve.wait_ge(activated, PEER_HEADS * t + h + 1)
                            dve.tensor_tensor(coeff[:, TOPK * h:TOPK * (h + 1)], active[:, TOPK * h:TOPK * (h + 1)],
                                              live.gate[:, h, :], ALU.mult).then_inc(coeff_ready, 1)
                    if kind == "u":
                        dve.wait_ge(gathered[p % RING], 16 * (TURNS * t + p // RING + 1))
                        row = ring[:, p % RING, :]
                        dve.tensor_tensor_reduce(row, row, live.x[:, :], 1.0, 0.0, ALU.mult, ALU.add,
                                                 dots[:, k:k + 1]).then_inc(u_used, 1)
                    steps(t, more, p, front_vector, end)
                    if p == RING - 1:
                        need(dve, v_used, PICKS * t)
                        dve.tensor_copy(expert_v[:, :], live.expert[:, :]).then_inc(expert_v_ready, 1)
                        dve.tensor_copy(h_live[:, :], live.h_next[:, :]).then_inc(h2_kept, 1)

            dve.memset(b.eps[:, :], EPS).then_inc(b.eps_set, 1)
            dve.wait_ge(b.eps_set, 1)
            dve.wait_ge(state_loaded, 64)
            dve.wait_ge(small_loaded, 64)
            for_chunks(dve, body, end)

        @block.tensor
        def _(pe):
            def body(t, more):
                for p, (kind, k) in enumerate(ORDER):
                    if kind == "v":
                        if k == 0:
                            need(pe, h3_ready, t)
                        pe.wait_ge(diagonal_ready, PICKS * t + k + 1)
                        pe.wait_ge(gathered[p % RING], 16 * (TURNS * t + p // RING + 1))
                        for c in range(2):
                            last = pe.matmul(acc[:, BANK * c:BANK * (c + 1)], diagonal[:, k % DIAGONALS, :],
                                             ring[:, p % RING, BANK * c:BANK * (c + 1)], start=(k == 0), stop=(k == PICKS - 1))
                        last.then_inc(v_used, 1)
                    steps(t, more, p, front_tensor, lambda t, names: None)

            pe.wait_ge(small_loaded, 64)
            for_chunks(pe, body, lambda t, names: None)


def hybrid_layer(nc, io):
    fold_weights(nc, io)
    with ExitStack() as ctx:
        sb, _, _ = allocators(nc, ctx)
        keep = {
            "mla_k_t": sb("mla_k_t", [P, HEADS, SEQ]),
            "dil_k_t": sb("dil_k_t", [P, HEADS // 2, SEQ]),
            "values": sb("values", [P, CHUNKS, 2 * WIDTH]),
        }
        project_tokens(nc, io, keep)
        attend(nc, io, keep, 0, 2)
        live = Picks(x=sb("live_x", [P, D]), h=sb("live_h", [P, D]), expert=sb("live_expert", [P, PICKS], U32),
                               gate=sb("live_gate", [P, PEER_HEADS, TOPK]))
        make_first_picks(nc, io, live)
        attend(nc, io, keep, 2, CHUNKS, live)
    attend_memory_and_experts(nc, io)


def kernel(x, mem, norm_mix, w_in, mla_q_norm, mla_kv_norm, mla_w_uq, mla_w_ukv, grp_norm_mla, grp_norm_dil, w_out,
           norm_mem_q, norm_mem_kv, w_mem_q, w_mem_kv, w_mem_o, norm_ffn, peer_w_q, peer_sub_keys, peer_u, peer_v,
           norm_final):
    import concourse.bacc as bacc
    from concourse.bass_utils import run_bass_kernel_spmd

    def columns(*gains):
        return np.ascontiguousarray(np.concatenate([np.asarray(g)[0].reshape(-1, P).T for g in gains], axis=1))

    arrays = {
        "x": np.asarray(x)[0],
        "mem": np.asarray(mem),
        "norm_mix": columns(norm_mix),
        "w_in": np.asarray(w_in)[0],
        "mla_q_norm": columns(mla_q_norm),
        "mla_kv_norm": columns(mla_kv_norm),
        "mla_w_uq": np.asarray(mla_w_uq)[0],
        "mla_w_ukv": np.asarray(mla_w_ukv)[0],
        "grp_norm": columns(grp_norm_mla, grp_norm_dil),
        "w_out": np.asarray(w_out)[0],
        "norm_mem_q": columns(norm_mem_q),
        "norm_mem_kv": columns(norm_mem_kv),
        "w_mem_q": np.asarray(w_mem_q)[0],
        "w_mem_kv": np.asarray(w_mem_kv)[0],
        "w_mem_o": np.asarray(w_mem_o)[0],
        "norm_ffn": columns(norm_ffn),
        "norm_ffn_row": np.asarray(norm_ffn)[0],
        "peer_w_q": np.asarray(peer_w_q)[0],
        "peer_sub_keys": np.asarray(peer_sub_keys)[0].reshape(PEER_TABLES, PEER_KEYS, P),
        "peer_u": np.asarray(peer_u)[0],
        "peer_v": np.asarray(peer_v)[0],
        "norm_final_row": np.asarray(norm_final),
    }
    arrays.update(shape_constants())
    arrays = {name: np.ascontiguousarray(a) for name, a in arrays.items()}

    nc = bacc.Bacc("TRN2", target_bir_lowering=False, num_devices=1)
    io = {name: nc.dram_tensor(name, a.shape, mybir.dt.from_np(a.dtype), kind="ExternalInput").ap()
          for name, a in arrays.items()}
    scratch = {
        "mem_scores": (P, DT, D),
        "mem_values": (P, DT, D),
        "peer_scores": (P, DT, 2 * D),
        "mla_q_t": (CHUNKS, QK, HEADS, P),
        "dil_q_t": (CHUNKS, P, HEADS // 2, P),
        "h1": (CHUNKS, P, D),
        "next_h": (P, D),
        "next_x": (P, D),
        "next_expert": (P, PICKS),
        "next_gate": (P, PEER_HEADS, TOPK),
    }
    for name, shape in scratch.items():
        io[name] = nc.dram_tensor(name, shape, U32 if name == "next_expert" else F32, kind="Internal").ap()
    io["out"] = nc.dram_tensor("out", (CHUNKS, P, D), F32, kind="ExternalOutput").ap()
    hybrid_layer(nc, io)
    result = run_bass_kernel_spmd(nc, [arrays], core_ids=[0])
    return result.results[0]["out"].reshape(1, SEQ, D)
```
